# Optimizing a Trainium2 kernel written in Bass

```python
import math
import jax
import jax.numpy as jnp
from jax import lax
import numpy as np
import jax, jax.numpy as jnp

D_MODEL = 1024
BATCH = 1
SEQ = 512
DEPTH = 2

GRID_W = 64
CTX_LEN = 256
HEAD_DIM = 64
MIX_W = D_MODEL
Q_BLOCK = 128
ROPE_THETA = 10000.0
DIFF_HEADS = MIX_W // 2 // (2 * HEAD_DIM)
DIFF_QK = DIFF_HEADS * 2 * HEAD_DIM
DIFF_V = DIFF_HEADS * 2 * HEAD_DIM
GQA_HEADS = MIX_W // 2 // HEAD_DIM
GQA_KV_HEADS = max(1, GQA_HEADS // 4)
GQA_GROUP = GQA_HEADS // GQA_KV_HEADS
GQA_Q = GQA_HEADS * HEAD_DIM
GQA_KV_W = GQA_KV_HEADS * HEAD_DIM
AB_Q = DIFF_QK + GQA_Q
AB_KV = DIFF_QK + DIFF_V + 2 * GQA_KV_W
AB_OUT = DIFF_V + GQA_Q
WINDOW = 128
WIN_HEADS = MIX_W // 2 // HEAD_DIM
WIN_KV_HEADS = max(1, WIN_HEADS // 4)
WIN_GROUP = WIN_HEADS // WIN_KV_HEADS
WIN_Q = WIN_HEADS * HEAD_DIM
WIN_KV_W = WIN_KV_HEADS * HEAD_DIM
NA_HEADS = MIX_W // 2 // HEAD_DIM
NA_W = NA_HEADS * HEAD_DIM
NA_ROWS_MAX = 8
NA_COLS = 16
CD_Q = WIN_Q + NA_W
CD_KV = 2 * WIN_KV_W + 2 * NA_W
CD_OUT = WIN_Q + NA_W
N_GROUPS = 4
EXPERTS_PER_GROUP = 8
N_EXPERTS = N_GROUPS * EXPERTS_PER_GROUP
TOP_K_IN_GROUP = 2
D_EXPERT = D_MODEL // 2
MOE_BLOCK = 128
N_EVEN = (DEPTH + 1) // 2
N_ODD = DEPTH // 2
ALPHA = (2.0 * DEPTH) ** 0.25
BETA = (8.0 * DEPTH) ** -0.25
LN_EPS = 1e-5
RMS_EPS = 1e-6
ATTN_SCALE = HEAD_DIM ** -0.5
NEG_INF = -1e30


def layer_norm(x, g, b):
    xf = x.astype(jnp.float32)
    mu = jnp.mean(xf, -1, keepdims=True)
    var = jnp.mean(jnp.square(xf - mu), -1, keepdims=True)
    y = (xf - mu) * lax.rsqrt(var + LN_EPS) * g.astype(jnp.float32) + b.astype(jnp.float32)
    return y.astype(x.dtype)

def rms_norm(x, g):
    xf = x.astype(jnp.float32)
    y = xf * lax.rsqrt(jnp.mean(jnp.square(xf), -1, keepdims=True) + RMS_EPS) * g.astype(jnp.float32)
    return y.astype(x.dtype)

def modulate(x, shift, scale):
    return x * (1.0 + scale) + shift

def lambda_init(layer_idx):
    return 0.8 - 0.6 * math.exp(-0.3 * layer_idx)

def axial_rope_tables(n_tokens):
    t = jnp.arange(n_tokens, dtype=jnp.int32)
    row = (t // GRID_W).astype(jnp.float32)
    col = (t % GRID_W).astype(jnp.float32)
    n_freq = HEAD_DIM // 4
    inv = ROPE_THETA ** (-jnp.arange(n_freq, dtype=jnp.float32) / n_freq)
    ang = jnp.concatenate([row[:, None] * inv, col[:, None] * inv], -1)
    return jnp.cos(ang), jnp.sin(ang)

def apply_rope(x, cos, sin):
    shp = (1, cos.shape[0]) + (1,) * (x.ndim - 3) + (cos.shape[1],)
    cos = cos.reshape(shp)
    sin = sin.reshape(shp)
    xf = x.astype(jnp.float32)
    x1, x2 = jnp.split(xf, 2, -1)
    return jnp.concatenate([x1 * cos - x2 * sin, x2 * cos + x1 * sin], -1).astype(x.dtype)

def sweep_query_blocks(fn, q):
    b, s = q.shape[:2]
    nb = s // Q_BLOCK
    qb = jnp.moveaxis(q.reshape((b, nb, Q_BLOCK) + q.shape[2:]), 1, 0)
    out = lax.map(lambda a: fn(a[0], a[1]), (jnp.arange(nb, dtype=jnp.int32), qb))
    out = jnp.moveaxis(out, 0, 1)
    return out.reshape((b, s) + out.shape[3:])

def diff_attend(qb, k, v, lam):
    s = jnp.einsum('bqhcd,bkhcd->bhcqk', qb, k).astype(jnp.float32) * ATTN_SCALE
    p = jax.nn.softmax(s, -1)
    a = p[:, :, 0] - lam * p[:, :, 1]
    return jnp.einsum('bhqk,bkhe->bqhe', a.astype(v.dtype), v)

def gqa_attend(qb, k, v):
    s = jnp.einsum('bqhgd,bkhd->bhgqk', qb, k).astype(jnp.float32) * ATTN_SCALE
    p = jax.nn.softmax(s, -1)
    return jnp.einsum('bhgqk,bkhd->bqhgd', p.astype(v.dtype), v)

def sink_attend(qb, k, v, sink, valid=None):
    s = jnp.einsum('bqhgd,bkhd->bhgqk', qb, k).astype(jnp.float32) * ATTN_SCALE
    if valid is not None:
        s = jnp.where(valid, s, NEG_INF)
    sk = jnp.broadcast_to(sink.astype(jnp.float32)[None, :, :, None, None], s.shape[:-1] + (1,))
    p = jax.nn.softmax(jnp.concatenate([s, sk], -1), -1)[..., :-1]
    return jnp.einsum('bhgqk,bkhd->bqhgd', p.astype(v.dtype), v)

def window_attention(q, k, v, kc, vc, sink):
    s = q.shape[1]
    n_ctx = kc.shape[1]
    span = Q_BLOCK + 2 * WINDOW
    pad = ((0, 0), (WINDOW, WINDOW), (0, 0), (0, 0))
    kp = jnp.pad(k, pad)
    vp = jnp.pad(v, pad)
    ctx_valid = jnp.ones((Q_BLOCK, n_ctx), dtype=bool)

    def block(bi, qb):
        start = bi * Q_BLOCK
        kb = lax.dynamic_slice_in_dim(kp, start, span, axis=1)
        vb = lax.dynamic_slice_in_dim(vp, start, span, axis=1)
        qpos = start + jnp.arange(Q_BLOCK)
        kpos = start - WINDOW + jnp.arange(span)
        local = (jnp.abs(qpos[:, None] - kpos[None, :]) <= WINDOW) & (kpos >= 0)[None, :] & (kpos < s)[None, :]
        valid = jnp.concatenate([local, ctx_valid], 1)
        return sink_attend(qb, jnp.concatenate([kb, kc], 1), jnp.concatenate([vb, vc], 1), sink, valid)

    return sweep_query_blocks(block, q)

def neighbourhood_attention(q, k, v, kc, vc, rpb):
    b, s, h, d = q.shape
    rows = s // GRID_W
    kr = min(NA_ROWS_MAX, rows)
    n_nb = kr * NA_COLS
    qg = jnp.moveaxis(q.reshape(b, rows, GRID_W, h, d), 1, 0)
    kg = k.reshape(b, rows, GRID_W, h, d)
    vg = v.reshape(b, rows, GRID_W, h, d)
    col = jnp.arange(GRID_W)
    col_start = jnp.clip(col - NA_COLS // 2, 0, GRID_W - NA_COLS)
    cols = col_start[:, None] + jnp.arange(NA_COLS)
    col_off = cols - col[:, None] + (NA_COLS - 1)

    def row_block(a):
        r, qr = a
        r0 = jnp.clip(r - kr // 2, 0, rows - kr)
        slab_k = lax.dynamic_slice_in_dim(kg, r0, kr, axis=1)
        slab_v = lax.dynamic_slice_in_dim(vg, r0, kr, axis=1)
        k_nb = jnp.moveaxis(slab_k[:, :, cols], 1, 2).reshape(b, GRID_W, n_nb, h, d)
        v_nb = jnp.moveaxis(slab_v[:, :, cols], 1, 2).reshape(b, GRID_W, n_nb, h, d)
        row_off = r0 + jnp.arange(kr) - r + (NA_ROWS_MAX - 1)
        bias = rpb[:, row_off[None, :, None], col_off[:, None, :]].reshape(h, GRID_W, n_nb)
        s_nb = jnp.einsum('bqhd,bqkhd->bhqk', qr, k_nb).astype(jnp.float32) * ATTN_SCALE + bias.astype(jnp.float32)[None]
        s_cx = jnp.einsum('bqhd,bkhd->bhqk', qr, kc).astype(jnp.float32) * ATTN_SCALE
        p = jax.nn.softmax(jnp.concatenate([s_nb, s_cx], -1), -1).astype(v.dtype)
        return (jnp.einsum('bhqk,bqkhd->bqhd', p[..., :n_nb], v_nb)
                + jnp.einsum('bhqk,bkhd->bqhd', p[..., n_nb:], vc))

    out = lax.map(row_block, (jnp.arange(rows, dtype=jnp.int32), qg))
    return jnp.moveaxis(out, 0, 1).reshape(b, s, h, d)

def mixer_ab(a_lat, a_ctx, ctx_kv_only, w_in, w_out, lam_vecs, subln_g, qk_g, lam_init, cos, sin):
    b = a_lat.shape[0]

    def split_q(p):
        n = p.shape[1]
        q_d = p[..., :DIFF_QK].reshape(b, n, DIFF_HEADS, 2, HEAD_DIM)
        q_g = rms_norm(p[..., DIFF_QK:AB_Q].reshape(b, n, GQA_KV_HEADS, GQA_GROUP, HEAD_DIM), qk_g[0])
        return q_d, q_g

    def split_kv(p):
        n = p.shape[1]
        o1 = DIFF_QK
        o2 = o1 + DIFF_V
        o3 = o2 + GQA_KV_W
        k_d = p[..., :o1].reshape(b, n, DIFF_HEADS, 2, HEAD_DIM)
        v_d = p[..., o1:o2].reshape(b, n, DIFF_HEADS, 2 * HEAD_DIM)
        k_g = rms_norm(p[..., o2:o3].reshape(b, n, GQA_KV_HEADS, HEAD_DIM), qk_g[1])
        v_g = p[..., o3:].reshape(b, n, GQA_KV_HEADS, HEAD_DIM)
        return k_d, v_d, k_g, v_g

    lv = lam_vecs.astype(jnp.float32)
    lam = jnp.exp(jnp.sum(lv[0] * lv[1])) - jnp.exp(jnp.sum(lv[2] * lv[3])) + lam_init

    p_lat = a_lat @ w_in
    q_d, q_g = split_q(p_lat[..., :AB_Q])
    k_d, v_d, k_g, v_g = split_kv(p_lat[..., AB_Q:])
    q_d, k_d, q_g, k_g = (apply_rope(t, cos, sin) for t in (q_d, k_d, q_g, k_g))
    if ctx_kv_only:
        ck_d, cv_d, ck_g, cv_g = split_kv(a_ctx @ w_in[:, AB_Q:])
    else:
        p_ctx = a_ctx @ w_in
        cq_d, cq_g = split_q(p_ctx[..., :AB_Q])
        ck_d, cv_d, ck_g, cv_g = split_kv(p_ctx[..., AB_Q:])

    kd_all = jnp.concatenate([k_d, ck_d], 1)
    vd_all = jnp.concatenate([v_d, cv_d], 1)
    kg_all = jnp.concatenate([k_g, ck_g], 1)
    vg_all = jnp.concatenate([v_g, cv_g], 1)
    o_d = sweep_query_blocks(lambda _, qb: diff_attend(qb, kd_all, vd_all, lam), q_d)
    o_g = sweep_query_blocks(lambda _, qb: gqa_attend(qb, kg_all, vg_all), q_g)

    def merge(od, og):
        n = od.shape[1]
        od = rms_norm(od, subln_g) * (1.0 - lam_init)
        return jnp.concatenate([od.reshape(b, n, DIFF_V), og.reshape(b, n, GQA_Q)], -1) @ w_out

    out_lat = merge(o_d, o_g)
    if ctx_kv_only:
        return out_lat, None
    out_ctx = merge(diff_attend(cq_d, ck_d, cv_d, lam), gqa_attend(cq_g, ck_g, cv_g))
    return out_lat, out_ctx

def mixer_cd(a_lat, a_ctx, ctx_kv_only, w_in, w_out, sink, rpb, cos, sin):
    b = a_lat.shape[0]
    sink_hg = sink.reshape(WIN_KV_HEADS, WIN_GROUP)

    def split_q(p):
        n = p.shape[1]
        q_w = p[..., :WIN_Q].reshape(b, n, WIN_KV_HEADS, WIN_GROUP, HEAD_DIM)
        q_n = p[..., WIN_Q:CD_Q].reshape(b, n, NA_HEADS, HEAD_DIM)
        return q_w, q_n

    def split_kv(p):
        n = p.shape[1]
        o1 = WIN_KV_W
        o2 = o1 + WIN_KV_W
        o3 = o2 + NA_W
        k_w = p[..., :o1].reshape(b, n, WIN_KV_HEADS, HEAD_DIM)
        v_w = p[..., o1:o2].reshape(b, n, WIN_KV_HEADS, HEAD_DIM)
        k_n = p[..., o2:o3].reshape(b, n, NA_HEADS, HEAD_DIM)
        v_n = p[..., o3:].reshape(b, n, NA_HEADS, HEAD_DIM)
        return k_w, v_w, k_n, v_n

    p_lat = a_lat @ w_in
    q_w, q_n = split_q(p_lat[..., :CD_Q])
    k_w, v_w, k_n, v_n = split_kv(p_lat[..., CD_Q:])
    q_w = apply_rope(q_w, cos, sin)
    k_w = apply_rope(k_w, cos, sin)
    if ctx_kv_only:
        ck_w, cv_w, ck_n, cv_n = split_kv(a_ctx @ w_in[:, CD_Q:])
    else:
        p_ctx = a_ctx @ w_in
        cq_w, cq_n = split_q(p_ctx[..., :CD_Q])
        ck_w, cv_w, ck_n, cv_n = split_kv(p_ctx[..., CD_Q:])

    o_w = window_attention(q_w, k_w, v_w, ck_w, cv_w, sink_hg)
    o_n = neighbourhood_attention(q_n, k_n, v_n, ck_n, cv_n, rpb)

    def merge(ow, on):
        n = ow.shape[1]
        return jnp.concatenate([ow.reshape(b, n, WIN_Q), on.reshape(b, n, NA_W)], -1) @ w_out

    out_lat = merge(o_w, o_n)
    if ctx_kv_only:
        return out_lat, None
    n_ctx = a_ctx.shape[1]
    co_w = sink_attend(cq_w, ck_w, cv_w, sink_hg)
    co_n = gqa_attend(cq_n.reshape(b, n_ctx, NA_HEADS, 1, HEAD_DIM), ck_n, cv_n)
    return out_lat, merge(co_w, co_n)

def hier_moe(h, w_group, b_group, w_router, b_router, w1, w3, w2):
    t, d = h.shape
    g_logits = (h @ w_group).astype(jnp.float32) + b_group.astype(jnp.float32)
    _, g_idx = lax.top_k(g_logits, 1)
    g_w = jnp.take_along_axis(jax.nn.softmax(g_logits, -1), g_idx, -1)
    e_logits = ((h @ w_router).astype(jnp.float32) + b_router.astype(jnp.float32)).reshape(t, N_GROUPS, EXPERTS_PER_GROUP)
    e_in = jnp.take_along_axis(e_logits, g_idx[:, :, None], 1)[:, 0]
    top_v, top_i = lax.top_k(e_in, TOP_K_IN_GROUP)
    weights = g_w * jax.nn.softmax(top_v, -1)
    experts = g_idx * EXPERTS_PER_GROUP + top_i

    n_assign = t * TOP_K_IN_GROUP
    e_flat = experts.reshape(n_assign)
    tok = jnp.repeat(jnp.arange(t, dtype=jnp.int32), TOP_K_IN_GROUP)
    w_flat = weights.reshape(n_assign)
    order = jnp.argsort(e_flat)
    e_s = e_flat[order]
    tok_s = tok[order]
    w_s = w_flat[order]
    counts = jnp.bincount(e_flat, length=N_EXPERTS)
    starts = jnp.cumsum(counts) - counts
    padded = (counts + MOE_BLOCK - 1) // MOE_BLOCK * MOE_BLOCK
    p_ends = jnp.cumsum(padded)
    p_starts = p_ends - padded
    dest = p_starts[e_s] + (jnp.arange(n_assign, dtype=jnp.int32) - starts[e_s])
    n_blocks = (n_assign + MOE_BLOCK - 1) // MOE_BLOCK + N_EXPERTS
    buf = jnp.zeros((n_blocks * MOE_BLOCK, d), h.dtype).at[dest].set(h[tok_s])
    blk_e = jnp.minimum(jnp.searchsorted(p_ends, jnp.arange(n_blocks) * MOE_BLOCK, side='right'), N_EXPERTS - 1)

    def expert_block(a):
        xb, e = a
        return (jax.nn.silu(xb @ w1[e]) * (xb @ w3[e])) @ w2[e]

    yb = lax.map(expert_block, (buf.reshape(n_blocks, MOE_BLOCK, d), blk_e)).reshape(n_blocks * MOE_BLOCK, d)
    return jnp.zeros((t, d), h.dtype).at[tok_s].add(w_s[:, None].astype(h.dtype) * yb[dest])

def first_inputs(seed: int = 0) -> dict:
    key = jax.random.key(seed)
    ks = jax.random.split(key, 32)
    D = D_MODEL

    def nrm(k, shape, s):
        return jax.random.normal(k, shape, jnp.float32) * s

    ab_kv_scale = jnp.concatenate([jnp.ones((DIFF_QK,)), jnp.full((DIFF_V,), BETA), jnp.ones((GQA_KV_W,)), jnp.full((GQA_KV_W,), BETA)]).astype(jnp.float32)
    cd_kv_scale = jnp.concatenate([jnp.ones((WIN_KV_W,)), jnp.full((WIN_KV_W,), BETA), jnp.ones((NA_W,)), jnp.full((NA_W,), BETA)]).astype(jnp.float32)
    return {
        'x': nrm(ks[0], (BATCH, SEQ, D), 1.0),
        'c': nrm(ks[1], (BATCH, D), 1.0),
        'ctx': nrm(ks[2], (BATCH, CTX_LEN, D), 1.0),
        'c_ctx': nrm(ks[3], (D,), 1.0),
        'mod_w': nrm(ks[4], (DEPTH, D, 6 * D), 0.5 * D ** -0.5),
        'mod_b': nrm(ks[5], (DEPTH, 6 * D), 0.02),
        'ln_g': 1.0 + nrm(ks[6], (DEPTH, 2, D), 0.02),
        'ln_b': nrm(ks[7], (DEPTH, 2, D), 0.02),
        'ab_w_in': jnp.concatenate([nrm(ks[8], (N_EVEN, D, AB_Q), D ** -0.5), nrm(ks[9], (N_EVEN, D, AB_KV), D ** -0.5) * ab_kv_scale], -1),
        'ab_w_out': nrm(ks[10], (N_EVEN, AB_OUT, D), AB_OUT ** -0.5 * BETA),
        'diff_lambda': nrm(ks[11], (N_EVEN, 4, HEAD_DIM), 0.1),
        'diff_subln_g': 1.0 + nrm(ks[12], (N_EVEN, 2 * HEAD_DIM), 0.02),
        'gqa_qk_g': 1.0 + nrm(ks[13], (N_EVEN, 2, HEAD_DIM), 0.02),
        'cd_w_in': jnp.concatenate([nrm(ks[14], (N_ODD, D, CD_Q), D ** -0.5), nrm(ks[15], (N_ODD, D, CD_KV), D ** -0.5) * cd_kv_scale], -1),
        'cd_w_out': nrm(ks[16], (N_ODD, CD_OUT, D), CD_OUT ** -0.5 * BETA),
        'win_sink': nrm(ks[17], (N_ODD, WIN_HEADS), 0.5),
        'na_rpb': nrm(ks[18], (N_ODD, NA_HEADS, 2 * NA_ROWS_MAX - 1, 2 * NA_COLS - 1), 0.1),
        'moe_w_group': nrm(ks[19], (DEPTH, D, N_GROUPS), D ** -0.5),
        'moe_b_group': nrm(ks[20], (DEPTH, N_GROUPS), 0.01),
        'moe_w_router': nrm(ks[21], (DEPTH, D, N_EXPERTS), D ** -0.5),
        'moe_b_router': nrm(ks[22], (DEPTH, N_EXPERTS), 0.01),
        'moe_w1': nrm(ks[23], (DEPTH, N_EXPERTS, D, D_EXPERT), D ** -0.5),
        'moe_w3': nrm(ks[24], (DEPTH, N_EXPERTS, D, D_EXPERT), D ** -0.5),
        'moe_w2': nrm(ks[25], (DEPTH, N_EXPERTS, D_EXPERT, D), D_EXPERT ** -0.5 * BETA),
    }

def first_block(x, c, ctx, c_ctx, mod_w, mod_b, ln_g, ln_b, ab_w_in, ab_w_out, diff_lambda, diff_subln_g, gqa_qk_g, cd_w_in, cd_w_out, win_sink, na_rpb, moe_w_group, moe_b_group, moe_w_router, moe_b_router, moe_w1, moe_w3, moe_w2):
    b, s, d = x.shape
    n_ctx = ctx.shape[1]
    cos, sin = axial_rope_tables(s)
    silu_c = jax.nn.silu(c)
    silu_cc = jax.nn.silu(c_ctx)
    h_lat, h_ctx = x, ctx
    for i in range(DEPTH):
        last = i == DEPTH - 1
        j = i // 2
        mods = (silu_c @ mod_w[i] + mod_b[i]).reshape(b, 1, 6, d)
        n_cm = 2 if last else 6
        cmods = (silu_cc @ mod_w[i][:, :n_cm * d] + mod_b[i][:n_cm * d]).reshape(1, 1, n_cm, d)

        a_lat = modulate(h_lat, mods[:, :, 0], mods[:, :, 1])
        a_ctx = modulate(h_ctx, cmods[:, :, 0], cmods[:, :, 1])
        if i % 2 == 0:
            o_lat, o_ctx = mixer_ab(a_lat, a_ctx, last, ab_w_in[j], ab_w_out[j], diff_lambda[j], diff_subln_g[j], gqa_qk_g[j], lambda_init(i), cos, sin)
        else:
            o_lat, o_ctx = mixer_cd(a_lat, a_ctx, last, cd_w_in[j], cd_w_out[j], win_sink[j], na_rpb[j], cos, sin)
        h_lat = layer_norm(ALPHA * h_lat + mods[:, :, 2] * o_lat, ln_g[i, 0], ln_b[i, 0])

        def moe(tokens):
            return hier_moe(tokens, moe_w_group[i], moe_b_group[i], moe_w_router[i], moe_b_router[i], moe_w1[i], moe_w3[i], moe_w2[i])

        f_lat = modulate(h_lat, mods[:, :, 3], mods[:, :, 4]).reshape(b * s, d)
        if last:
            y_lat = moe(f_lat)
        else:
            h_ctx = layer_norm(ALPHA * h_ctx + cmods[:, :, 2] * o_ctx, ln_g[i, 0], ln_b[i, 0])
            f_ctx = modulate(h_ctx, cmods[:, :, 3], cmods[:, :, 4]).reshape(b * n_ctx, d)
            y = moe(jnp.concatenate([f_lat, f_ctx], 0))
            y_lat = y[:b * s]
            h_ctx = layer_norm(ALPHA * h_ctx + cmods[:, :, 5] * y[b * s:].reshape(b, n_ctx, d), ln_g[i, 1], ln_b[i, 1])
        h_lat = layer_norm(ALPHA * h_lat + mods[:, :, 5] * y_lat.reshape(b, s, d), ln_g[i, 1], ln_b[i, 1])
    return h_lat


DEPTH_2 = 1

EPS = 1e-6
N_BRANCH = 3
BRANCH_WIDTH = D_MODEL // 2
GLA_HEADS = 4
GLA_DV = BRANCH_WIDTH // GLA_HEADS
GLA_DK = GLA_DV // 2
GLA_RANK = 16
GLA_TAU = 16.0
GLA_CHUNK = 16
GLA_QK = GLA_HEADS * GLA_DK
GLA_V = GLA_HEADS * GLA_DV
SC_WIDTH = BRANCH_WIDTH
CONV_K = 3
DIL_PATTERNS = ((128, 1), (512, 4), (2048, 16))
DIL_GROUPS = len(DIL_PATTERNS)
DIL_HEADS = 4
DIL_HD = BRANCH_WIDTH // DIL_HEADS
DIL_W = DIL_GROUPS * DIL_HEADS * DIL_HD
DIL_BLOCK = 128
D_FF = 2816

IN_SIZES = (GLA_QK, GLA_QK, GLA_V, GLA_V, GLA_RANK,
            SC_WIDTH, SC_WIDTH, SC_WIDTH,
            DIL_W, DIL_W, DIL_W)
IN_COLS = sum(IN_SIZES)


def rmsnorm(x, g):
    xf = x.astype(jnp.float32)
    r = lax.rsqrt(jnp.mean(xf * xf, axis=-1, keepdims=True) + EPS)
    return (xf * r).astype(x.dtype) * g

def causal_dwconv(u, w):
    K = w.shape[0]
    S = u.shape[1]
    up = jnp.pad(u, ((0, 0), (K - 1, 0), (0, 0)))
    y = w[0] * up[:, 0:S]
    for k in range(1, K):
        y = y + w[k] * up[:, k:k + S]
    return y

def rope(x, pos):
    hd = x.shape[-1]
    inv = ROPE_THETA ** (-jnp.arange(0, hd, 2, dtype=jnp.float32) / hd)
    ang = pos.astype(jnp.float32)[..., None] * inv
    cos = jnp.cos(ang)[:, :, None, None, :]
    sin = jnp.sin(ang)[:, :, None, None, :]
    xf = x.astype(jnp.float32)
    x1, x2 = xf[..., :hd // 2], xf[..., hd // 2:]
    return jnp.concatenate([x1 * cos - x2 * sin, x2 * cos + x1 * sin], axis=-1).astype(x.dtype)

def gla_branch(q, k, v, g, a_low, w_a_up, b_a, norm_g):
    B, S, _ = q.shape
    H, C = GLA_HEADS, GLA_CHUNK
    N = S // C
    f32 = jnp.float32
    loga = jax.nn.log_sigmoid((a_low.astype(f32) @ w_a_up.astype(f32)) + b_a.astype(f32)) / GLA_TAU

    def chunks(t, d):
        return t.astype(f32).reshape(B, N, C, H, d).transpose(0, 3, 1, 2, 4)

    qc = chunks(q, GLA_DK) * (GLA_DK ** -0.5)
    kc = chunks(k, GLA_DK)
    vc = chunks(v, GLA_DV)
    lc = jnp.cumsum(chunks(loga, GLA_DK), axis=3)

    causal = jnp.tril(jnp.ones((C, C), dtype=bool))
    rel = lc[..., :, None, :] - lc[..., None, :, :]
    decay = jnp.exp(jnp.where(causal[:, :, None], rel, -jnp.inf))
    scores = jnp.einsum('bhnid,bhnjd,bhnijd->bhnij', qc, kc, decay)
    o_intra = jnp.einsum('bhnij,bhnje->bhnie', scores, vc)

    lend = lc[..., -1:, :]
    q_in = qc * jnp.exp(lc)
    k_in = kc * jnp.exp(lend - lc)
    dec_chunk = jnp.exp(lend[..., 0, :])

    def step(state, xs):
        qn, kn, vn, dn = xs
        o = jnp.einsum('bhid,bhde->bhie', qn, state)
        state = state * dn[..., None] + jnp.einsum('bhjd,bhje->bhde', kn, vn)
        return state, o

    xs = (jnp.moveaxis(q_in, 2, 0), jnp.moveaxis(k_in, 2, 0),
          jnp.moveaxis(vc, 2, 0), jnp.moveaxis(dec_chunk, 2, 0))
    s0 = jnp.zeros((B, H, GLA_DK, GLA_DV), f32)
    _, o_inter = lax.scan(step, s0, xs)
    o = o_intra + jnp.moveaxis(o_inter, 0, 2)
    o = o.transpose(0, 2, 3, 1, 4).reshape(B, S, H, GLA_DV).astype(v.dtype)
    o = rmsnorm(o, norm_g).reshape(B, S, GLA_V)
    return o * jax.nn.silu(g)

def strided_window_attn(q, k, v, span, dil):
    B, S, H, D = q.shape
    L = S // dil
    BLK = DIL_BLOCK
    nb = -(-L // BLK)
    Lp = nb * BLK

    def to_sub(t):
        return t.reshape(B, L, dil, H, D).transpose(0, 2, 3, 1, 4)

    qs, ks, vs = to_sub(q), to_sub(k), to_sub(v)
    qb = jnp.pad(qs, ((0, 0), (0, 0), (0, 0), (0, Lp - L), (0, 0))).reshape(B, dil, H, nb, BLK, D)

    def kv_blocks(t):
        tp = jnp.pad(t, ((0, 0), (0, 0), (0, 0), (BLK, Lp - L), (0, 0)))
        prev = tp[:, :, :, :Lp].reshape(B, dil, H, nb, BLK, D)
        cur = tp[:, :, :, BLK:].reshape(B, dil, H, nb, BLK, D)
        return jnp.concatenate([prev, cur], axis=4)

    kb, vb = kv_blocks(ks), kv_blocks(vs)
    i = jnp.arange(BLK)[:, None]
    m = jnp.arange(2 * BLK)[None, :]
    blk = jnp.arange(nb)[:, None, None]
    dist = i + BLK - m
    key_idx = (blk - 1) * BLK + m
    valid = (dist >= 0) & (dist <= span) & (key_idx >= 0)

    s = jnp.einsum('brhnid,brhnmd->brhnim', qb, kb).astype(jnp.float32) * (D ** -0.5)
    s = jnp.where(valid, s, -jnp.inf)
    mx = jnp.max(s, axis=-1, keepdims=True)
    p = jnp.exp(s - mx)
    den = jnp.sum(p, axis=-1, keepdims=True)
    o = jnp.einsum('brhnim,brhnmd->brhnid', p, vb.astype(jnp.float32)) / den
    lse = (mx + jnp.log(den))[..., 0]

    o = o.reshape(B, dil, H, Lp, D)[:, :, :, :L].transpose(0, 3, 1, 2, 4).reshape(B, S, H, D)
    lse = lse.reshape(B, dil, H, Lp)[:, :, :, :L].transpose(0, 3, 1, 2).reshape(B, S, H)
    return o, lse

def dilated_branch(dq, dk, dv, pos):
    B, S, _ = dq.shape
    shp = (B, S, DIL_GROUPS, DIL_HEADS, DIL_HD)
    q = rope(dq.reshape(shp), pos)
    k = rope(dk.reshape(shp), pos)
    v = dv.reshape(shp)
    outs, lses = [], []
    for gi, (win, dil) in enumerate(DIL_PATTERNS):
        o, lse = strided_window_attn(q[:, :, gi], k[:, :, gi], v[:, :, gi], win // dil, dil)
        outs.append(o)
        lses.append(lse)
    w = jax.nn.softmax(jnp.stack(lses, axis=0), axis=0)
    o = jnp.sum(w[..., None] * jnp.stack(outs, axis=0), axis=0)
    return o.reshape(B, S, DIL_HEADS * DIL_HD).astype(dq.dtype)

def second_inputs(seed: int = 0) -> dict:
    key = jax.random.key(seed)
    ks = jax.random.split(key, 24)
    f32 = jnp.float32

    def nrm(k, shape, scale):
        return jax.random.normal(k, shape, f32) * scale

    def gain(k, shape):
        return 1.0 + 0.02 * jax.random.normal(k, shape, f32)

    x = jax.random.normal(ks[0], (BATCH, SEQ, D_MODEL), f32)
    offset = jax.random.randint(ks[1], (BATCH, 1), 0, 4096, dtype=jnp.int32)
    positions = (offset + jnp.arange(SEQ, dtype=jnp.int32)[None, :]).astype(jnp.int32)
    return {
        "x": x,
        "positions": positions,
        "w_in": nrm(ks[2], (DEPTH_2, D_MODEL, IN_COLS), D_MODEL ** -0.5),
        "w_alpha_up": nrm(ks[3], (DEPTH_2, GLA_RANK, GLA_QK), GLA_RANK ** -0.5),
        "b_alpha": nrm(ks[4], (DEPTH_2, GLA_QK), 0.1),
        "gla_norm_g": gain(ks[5], (DEPTH_2, GLA_DV)),
        "sc_conv_w": nrm(ks[6], (DEPTH_2, CONV_K, SC_WIDTH), CONV_K ** -0.5),
        "w_gate": nrm(ks[7], (DEPTH_2, D_MODEL, N_BRANCH * D_MODEL), D_MODEL ** -0.5),
        "b_gate": nrm(ks[8], (DEPTH_2, N_BRANCH * D_MODEL), 0.02),
        "w_branch": nrm(ks[9], (DEPTH_2, N_BRANCH, BRANCH_WIDTH, D_MODEL), BRANCH_WIDTH ** -0.5),
        "w_mix_out": nrm(ks[10], (DEPTH_2, D_MODEL, D_MODEL), D_MODEL ** -0.5),
        "pre_mix_g": gain(ks[11], (DEPTH_2, D_MODEL)),
        "post_mix_g": gain(ks[12], (DEPTH_2, D_MODEL)),
        "pre_ffn_g": gain(ks[13], (DEPTH_2, D_MODEL)),
        "post_ffn_g": gain(ks[14], (DEPTH_2, D_MODEL)),
        "w_ff_gate": nrm(ks[15], (DEPTH_2, D_MODEL, D_FF), D_MODEL ** -0.5),
        "w_ff_up": nrm(ks[16], (DEPTH_2, D_MODEL, D_FF), D_MODEL ** -0.5),
        "ff_conv_w": nrm(ks[17], (DEPTH_2, CONV_K, D_FF), CONV_K ** -0.5),
        "ff_conv_b": nrm(ks[18], (DEPTH_2, D_FF), 0.02),
        "w_ff_down": nrm(ks[19], (DEPTH_2, D_FF, D_MODEL), D_FF ** -0.5),
    }

def second_block(x, positions, w_in, w_alpha_up, b_alpha, gla_norm_g, sc_conv_w, w_gate, b_gate,
              w_branch, w_mix_out, pre_mix_g, post_mix_g, pre_ffn_g, post_ffn_g,
              w_ff_gate, w_ff_up, ff_conv_w, ff_conv_b, w_ff_down):
    B, S, _ = x.shape
    split_points = np.cumsum(np.array(IN_SIZES))[:-1].tolist()
    for l in range(DEPTH_2):
        h = rmsnorm(x, pre_mix_g[l])
        z = h @ w_in[l]
        (g_q, g_k, g_v, g_o, a_low, sc_b, sc_c, sc_x,
         d_q, d_k, d_v) = jnp.split(z, split_points, axis=-1)

        y_gla = gla_branch(g_q, g_k, g_v, g_o, a_low, w_alpha_up[l], b_alpha[l], gla_norm_g[l])
        y_sc = sc_b * causal_dwconv(sc_c * sc_x, sc_conv_w[l])
        y_dil = dilated_branch(d_q, d_k, d_v, positions)

        br = jnp.stack([y_gla, y_sc, y_dil], axis=2)
        proj = jnp.einsum('bsgc,gcd->bsgd', br, w_branch[l])
        gates = jax.nn.sigmoid(h @ w_gate[l] + b_gate[l]).reshape(B, S, N_BRANCH, D_MODEL)
        merged = jnp.sum(gates * proj, axis=2)
        x = x + rmsnorm(merged @ w_mix_out[l], post_mix_g[l])

        h = rmsnorm(x, pre_ffn_g[l])
        gt = causal_dwconv(h @ w_ff_gate[l], ff_conv_w[l]) + ff_conv_b[l]
        y = (jax.nn.gelu(gt, approximate=True) * (h @ w_ff_up[l])) @ w_ff_down[l]
        x = x + rmsnorm(y, post_ffn_g[l])
    return x


def setup_inputs(seed=0):
    out = dict(first_inputs(seed))
    for name, value in second_inputs(seed + 1).items():
        if name != "x":
            out[name + "_2"] = value
    return out


def reference(
    x, c, ctx, c_ctx, mod_w, mod_b, ln_g, ln_b, ab_w_in, ab_w_out, diff_lambda, diff_subln_g,
    gqa_qk_g, cd_w_in, cd_w_out, win_sink, na_rpb, moe_w_group, moe_b_group, moe_w_router,
    moe_b_router, moe_w1, moe_w3, moe_w2, positions_2, w_in_2, w_alpha_up_2, b_alpha_2,
    gla_norm_g_2, sc_conv_w_2, w_gate_2, b_gate_2, w_branch_2, w_mix_out_2, pre_mix_g_2,
    post_mix_g_2, pre_ffn_g_2, post_ffn_g_2, w_ff_gate_2, w_ff_up_2, ff_conv_w_2, ff_conv_b_2,
    w_ff_down_2,
):
    x = first_block(
        x, c, ctx, c_ctx, mod_w, mod_b, ln_g, ln_b, ab_w_in, ab_w_out, diff_lambda,
        diff_subln_g, gqa_qk_g, cd_w_in, cd_w_out, win_sink, na_rpb, moe_w_group, moe_b_group,
        moe_w_router, moe_b_router, moe_w1, moe_w3, moe_w2,
    )
    return second_block(
        x, positions_2, w_in_2, w_alpha_up_2, b_alpha_2, gla_norm_g_2, sc_conv_w_2, w_gate_2,
        b_gate_2, w_branch_2, w_mix_out_2, pre_mix_g_2, post_mix_g_2, pre_ffn_g_2, post_ffn_g_2,
        w_ff_gate_2, w_ff_up_2, ff_conv_w_2, ff_conv_b_2, w_ff_down_2,
    )


_drawn_inputs = setup_inputs


def setup_inputs(seed=0):
    import zlib

    import numpy as np

    out = dict(_drawn_inputs(seed))
    spreads = {}
    factors = {'mod_b': 3.254,
     'diff_lambda': 5.607,
     'diff_subln_g': 8.0,
     'gqa_qk_g': 24.886,
     'win_sink': 59.336,
     'na_rpb': 64.0,
     'moe_b_group': 28.322,
     'moe_b_router': 21.578,
     'b_alpha_2': 2.874,
     'gla_norm_g_2': 6.053,
     'b_gate_2': 8.0,
     'post_mix_g_2': 3.43,
     'pre_ffn_g_2': 3.343,
     'post_ffn_g_2': 50.572,
     'ff_conv_b_2': 4.932}
    for name, (base, spread) in spreads.items():
        noise = np.random.default_rng([zlib.crc32(name.encode()), seed]).standard_normal(out[name].shape)
        drawn = base * np.exp(spread * noise) if base else spread * noise
        out[name] = jnp.asarray(drawn.astype(out[name].dtype))
    for name, factor in factors.items():
        out[name] = (out[name] * factor).astype(out[name].dtype)
    return out
```

```python
from contextlib import ExitStack
import math

import numpy as np

import concourse.bass as bass
from concourse import mybir

F32 = mybir.dt.float32
I32 = mybir.dt.int32
ALU = mybir.AluOpType
ACT = mybir.ActivationFunctionType
AX = mybir.AxisListType
ds = bass.ds

P = 128
D = 1024
C = D // P
LAT, CTX = 512, 256
TOK = LAT + CTX
NLAT, NCTX = LAT // P, CTX // P
NTILE = NLAT + NCTX
DEPTH = 2
HD = 64
GRID_W = 64
ROWS = LAT // GRID_W
NA_COLS = 16
WINDOW = 128
NG, EPG = 4, 8
NE = NG * EPG
DE = 512
ALPHA = (2.0 * DEPTH) ** 0.25
LN_EPS = 1e-5
RMS_EPS = 1e-6
SCALE = HD ** -0.5
NEG = -1e30
LAM_INIT = 0.8 - 0.6 * math.exp(0.0)


class Steps:

    def __init__(self, eng, sem):
        self.eng, self.sem, self.n = eng, sem, 0

    def __call__(self, ins):
        self.n += 1
        ins.then_inc(self.sem, 1)
        self.eng.wait_ge(self.sem, self.n)

    def restart(self):
        self.eng.sem_clear(self.sem)
        self.n = 0


class Phase:

    POOL = 52
    FIRST = 150
    count = 0

    def __init__(self, nc):
        self.nc, self.stack = nc, ExitStack()
        self.base = Phase.FIRST + Phase.POOL * (Phase.count % 2)
        self.other = Phase.FIRST + Phase.POOL * ((Phase.count + 1) % 2)
        self.first = Phase.count == 0
        self.used = 0
        Phase.count += 1

    def __enter__(self):
        return self

    def __exit__(self, *a):
        return self.stack.__exit__(*a)

    def sb(self, name, shape, dt=F32):
        return self.stack.enter_context(self.nc.sbuf_tensor(f"{name}_{Phase.count}", shape, dt))

    def ps(self, name, shape, dt=F32):
        return self.stack.enter_context(self.nc.psum_tensor(f"{name}_{Phase.count}", shape, dt))

    def sem(self, name):
        s = self.stack.enter_context(self.nc.semaphore(f"{name}_{Phase.count}", num=self.base + self.used))
        self.used += 1
        assert self.used <= Phase.POOL
        return s

    def sems(self, name, n=2):
        return [self.sem(f"{name}{i}") for i in range(n)]

    def block(self):
        return self.stack.enter_context(self.nc.Block())

    def clear_other_pool(self, sp):
        if not self.first:
            sp.sem_clear(range(self.other, self.other + Phase.POOL))


def modulation_phase(nc, g):
    W = 1024
    with Phase(nc) as ph:
        vec = ph.sb("vec", [P, 2, C])
        act_vec = ph.sb("act_vec", [P, C, 2])
        w = ph.sb("w", [P, 2, C, W])
        bias = ph.sb("bias", [2, 2, W])
        row = ph.sb("row", [2, 2, W])
        acc = [ph.ps(f"acc{b}", [P, W]) for b in range(2)]
        vec_in, silu_done = ph.sem("vec_in"), ph.sem("silu_done")
        w_in, product, added, stored = (ph.sems(n) for n in ("w_in", "product", "added", "stored"))
        block = ph.block()

        def chunks(eng):
            for l in range(DEPTH):
                with eng.Fori(0, 3) as m:
                    yield l, m, m + 3 * l

        @block.sync
        def _(sp):
            ph.clear_other_pool(sp)
            sp.dma_start(vec[:, 0, :], g["c"].rearrange("a (p k) -> (a p) k", p=P)).then_inc(vec_in, 16)
            sp.dma_start(vec[:, 1, :], g["c_ctx"].rearrange("(p k) -> p k", p=P)).then_inc(vec_in, 16)
            for l, m, n in chunks(sp):
                wv = g["mod_w"][l].rearrange("(p k) n -> p k n", p=P)
                bv = g["mod_b"][l:l + 1, :].broadcast_to([2, 6 * D])
                for b in range(2):
                    sp.wait_ge(product[b], n + 1)
                    sp.wait_ge(added[b], n + 1)
                    sp.dma_start(w[:, b], wv[:, :, ds(m * 2 * W + b * W, W)]).then_inc(w_in[b], 16)
                    sp.dma_start(bias[:, b], bv[:, ds(m * 2 * W + b * W, W)]).then_inc(w_in[b], 16)

        @block.scalar
        def _(act):
            act.wait_ge(vec_in, 32)
            act.activation(act_vec[:].rearrange("p k v -> p v k"), vec[:], ACT.Silu).then_inc(silu_done, 1)
            for b in range(2):
                act.sem_inc(stored[b], 16)
            for l, m, n in chunks(act):
                for b in range(2):
                    act.wait_ge(added[b], n + 2)
                    act.dma_start(g["mods"][l, :, ds(m * 2 * W + b * W, W)], row[:, b]).then_inc(stored[b], 16)
            for b in range(2):
                act.wait_ge(stored[b], 16 * (3 * DEPTH + 1))

        @block.vector
        def _(dve):
            for b in range(2):
                dve.sem_inc(added[b], 1)
            for l, m, n in chunks(dve):
                for b in range(2):
                    dve.wait_ge(w_in[b], 32 * (n + 1))
                    dve.wait_ge(product[b], n + 2)
                    dve.wait_ge(stored[b], 16 * (n + 1))
                    dve.tensor_tensor(row[:, b], acc[b][0:2, :], bias[:, b], ALU.add).then_inc(added[b], 1)

        @block.tensor
        def _(pe):
            for b in range(2):
                pe.sem_inc(product[b], 1)
            pe.wait_ge(silu_done, 1)
            for l, m, n in chunks(pe):
                for b in range(2):
                    pe.wait_ge(w_in[b], 32 * (n + 1))
                    pe.wait_ge(added[b], n + 1)
                    for h in range(W // 512):
                        for k in range(C):
                            last = pe.matmul(acc[b][0:2, h * 512:(h + 1) * 512], act_vec[:, k, :],
                                             w[:, b, k, h * 512:(h + 1) * 512], start=(k == 0), stop=(k == C - 1))
                    last.then_inc(product[b], 1)


GROUPS = [
    [(0, 4, False, None, True, "q", 0), (512, 4, False, 0, True, "q", 4),
     (1024, 4, False, None, True, "k", 0), (2048, 2, True, 1, True, "k", 4)],
    [(0, 4, False, None, True, "q", 0), (512, 4, False, None, False, "q", 4),
     (1024, 2, True, None, True, "k", 0), (1280, 4, False, None, False, "k", 2)],
]
V_COLS = [(1536, 2176), (1792, 1152)]


def projection_phase(nc, g, l, srcs, qT, kT, V):
    w_in_dram = g["ab_w_in" if l == 0 else "cd_w_in"][0].rearrange("(p k) n -> p k n", p=P)
    with Phase(nc) as ph:
        rows = ph.sb("rows", [P, 2, D])
        aT = ph.sb("aT", [P, C, TOK])
        mcol = ph.sb("mcol", [P, 2, 2, C])
        w = ph.sb("w", [P, 2, C, P])
        wv = ph.sb("wv", [P, C, 640])
        xs = ph.sb("xs", [P, 2, TOK])
        sq = ph.sb("sq", [P, 2, TOK])
        t1 = ph.sb("t1", [P, 2, LAT])
        t2 = ph.sb("t2", [P, 2, LAT])
        cos, sin = ph.sb("cos", [P, LAT]), ph.sb("sin", [P, LAT])
        rot, blk = ph.sb("rot", [P, P]), ph.sb("blk", [P, P])
        gain = ph.sb("gain", [P, 2])
        eps = ph.sb("eps", [P, 1])
        pa = [ph.ps(f"pa{b}", [P, 1024]) for b in range(2)]
        pn = ph.ps("pn", [P, 1024])
        pr = [ph.ps(f"pr{b}", [P, 512]) for b in range(2)]
        const_in, wv_in, plus_one, eps_set = (ph.sem(n) for n in ("const_in", "wv_in", "plus_one", "eps_set"))
        row_in, turned, moved = ph.sems("row_in"), ph.sems("turned"), ph.sems("moved")
        w_in, projected, x_ready, squared, meaned, rooted, rotated, written = (
            ph.sems(n) for n in ("w_in", "projected", "x_ready", "squared", "meaned", "rooted", "rotated", "written"))
        v_done, v_out = ph.sems("v_done"), ph.sems("v_out")
        order = ph.sem("order")
        block = ph.block()
        ident = g["ident"]

        def pairs(eng):
            with eng.Fori(0, NLAT // 2) as m:
                yield srcs[0], m, 0, m
            yield srcs[1], 0, 1, NLAT // 2

        def groups(eng):
            n0 = 0
            for col, n, dup, norm, rope, dst, at in GROUPS[l]:
                with eng.Fori(0, n // 2) as i:
                    yield (col, dup, norm, rope, qT if dst == "q" else kT, at), i, i + n0
                n0 += n // 2

        @block.sync
        def _(sp):
            ph.clear_other_pool(sp)
            for v in range(2):
                for s in range(2):
                    sp.dma_start(mcol[:, v, s, :], g["mods"][l, v, s * D:(s + 1) * D].rearrange("(p k) -> p k", p=P)).then_inc(const_in, 16)
            for dst, src in ((cos, "cos"), (sin, "sin"), (rot, "rot64"), (blk, "blk64")):
                sp.dma_start(dst[:], g[src]).then_inc(const_in, 16)
            for s in range(2):
                for half in range(2):
                    sp.dma_start(gain[half * HD:(half + 1) * HD, s:s + 1],
                                 g["gqa_qk_g"][0, s, :].rearrange("(p o) -> p o", o=1)).then_inc(const_in, 16)
            for (src, m, v, n) in pairs(sp):
                for b in range(2):
                    sp.wait_ge(turned[1], 2 * n + b + 1)
                    sp.dma_start(rows[:, b], src[ds(m * 2 * P + b * P, P), :]).then_inc(row_in[b], 16)
            c5, c1 = V_COLS[l]
            sp.dma_start(wv[:, :, 0:512], w_in_dram[:, :, c5:c5 + 512]).then_inc(wv_in, 16)
            sp.dma_start(wv[:, :, 512:640], w_in_dram[:, :, c1:c1 + 128]).then_inc(wv_in, 16)
            for (col, dup, norm, rope, dst, at), i, n in groups(sp):
                for b in range(2):
                    sp.wait_ge(projected[b], n + 1)
                    if dup:
                        src = w_in_dram[:, :, col + b * HD:col + (b + 1) * HD]
                        src = src.rearrange("p k (o n) -> p k o n", o=1).broadcast_to([P, C, 2, HD])
                        dstw = w[:, b].rearrange("p k (o n) -> p k o n", o=2)
                        for o in range(2):
                            sp.dma_start(dstw[:, :, o, :], src[:, :, o, :]).then_inc(w_in[b], 16)
                    else:
                        for o in range(2):
                            sp.dma_start(w[o * 64:(o + 1) * 64, b], w_in_dram[o * 64:(o + 1) * 64, :, ds(i * 2 * P + col + b * P, P)]).then_inc(w_in[b], 16)

        @block.tensor
        def _(pe):
            pe.sem_inc(turned[1], 2)
            for b in range(2):
                pe.sem_inc(projected[b], 1)
            for (src, m, v, n) in pairs(pe):
                for b in range(2):
                    pe.wait_ge(row_in[b], 16 * (n + 1))
                    for h in range(2):
                        pe.wait_ge(moved[h], 2 * n + b + 1)
                        for k in range(4):
                            last = pe.transpose(pr[h][:, k * P:(k + 1) * P], rows[:, b, h * 4 + k::C], ident[:])
                        last.then_inc(turned[h], 1)
            pe.wait_ge(const_in, 16 * 12)
            pe.wait_ge(moved[0], NTILE + 1)
            pe.wait_ge(moved[1], NTILE + 1)
            for (col, dup, norm, rope, dst, at), i, n in groups(pe):
                for b in range(2):
                    pe.wait_ge(w_in[b], 32 * (n + 1))
                    pe.wait_ge(x_ready[b], n + 1)
                    pe.wait_ge(written[b], n + 1)
                    for k in range(C):
                        pe.matmul(pa[b][:, 0:512], w[:, b, k, :], aT[:, k, 0:512], start=(k == 0), stop=(k == C - 1))
                        last = pe.matmul(pa[b][:, 512:768], w[:, b, k, :], aT[:, k, 512:768], start=(k == 0), stop=(k == C - 1))
                    last.then_inc(projected[b], 1)
                if norm is not None:
                    for b in range(2):
                        pe.wait_ge(squared[b], i + 1 + (norm * 2))
                        pe.wait_ge(rooted[1 - b], i + norm * 2 + 1)
                        pe.matmul(pn[:, 0:512], blk[:], sq[:, b, 0:512], start=True, stop=True)
                        pe.matmul(pn[:, 512:768], blk[:], sq[:, b, 512:768], start=True, stop=True).then_inc(meaned[b], 1)
                if rope:
                    for b in range(2):
                        pe.wait_ge(x_ready[b], n + 2)
                        pe.matmul(pr[b][:, :], rot[:], xs[:, b, 0:512], start=True, stop=True).then_inc(rotated[b], 1)
            pe.wait_ge(wv_in, 32)
            npairs = sum(x[1] for x in GROUPS[l]) // 2
            for b in range(2):
                pe.wait_ge(x_ready[b], npairs + 1)
                pe.wait_ge(written[b], npairs + 1)
            for t in range(NTILE):
                b = t % 2
                if t >= 2:
                    pe.wait_ge(v_out[b], t // 2)
                for k in range(C):
                    pe.matmul(pa[b][:, 0:512], aT[:, k, t * P:(t + 1) * P], wv[:, k, 0:512], start=(k == 0), stop=(k == C - 1))
                    last = pe.matmul(pa[b][:, 512:640], aT[:, k, t * P:(t + 1) * P], wv[:, k, 512:640], start=(k == 0), stop=(k == C - 1))
                last.then_inc(v_done[b], 1)

        @block.scalar
        def _(act):
            act.sem_inc(moved[0], 1)
            for b in range(2):
                act.sem_inc(x_ready[b], 1)
            act.sem_inc(rooted[1], 1)
            act.wait_ge(plus_one, 1)
            for (src, m, v, n) in pairs(act):
                for b in range(2):
                    act.wait_ge(turned[0], 2 * n + b + 1)
                    for k in range(4):
                        last = act.activation(aT[:, k, ds(n * 2 * P + b * P, P)], pr[0][:, k * P:(k + 1) * P], ACT.Identity,
                                              scale=mcol[:, v, 1, k:k + 1], bias=mcol[:, v, 0, k:k + 1])
                    last.then_inc(moved[0], 1)
            for (col, dup, norm, rope, dst, at), i, n in groups(act):
                for b in range(2):
                    act.wait_ge(projected[b], n + 2)
                    act.wait_ge(written[b], n + 1)
                    if norm is not None:
                        act.activation(sq[:, b, :], pa[b][:, 0:768], ACT.Square).then_inc(squared[b], 1)
                    else:
                        last = act.activation(dst[:, ds(i * 2 + at + b, 1), 512:768], pa[b][:, 512:768], ACT.Copy)
                        if rope:
                            last = act.activation(xs[:, b, 0:512], pa[b][:, 0:512], ACT.Copy)
                        last.then_inc(x_ready[b], 1)
                if norm is not None:
                    for b in range(2):
                        act.wait_ge(meaned[b], i + 1 + norm * 2)
                        act.activation(sq[:, b, :], pn[:, 0:768], ACT.Sqrt, bias=eps[:]).then_inc(rooted[b], 1)
            for t in range(NTILE):
                act.wait_ge(v_done[t % 2], t // 2 + 1)
                act.activation(V[:, t, :], pa[t % 2][:, 0:640], ACT.Copy).then_inc(v_out[t % 2], 1)

        @block.vector
        def _(dve):
            step = Steps(dve, order)
            dve.sem_inc(moved[1], 1)
            for b in range(2):
                dve.sem_inc(written[b], 1)
            dve.wait_ge(const_in, 16 * 12)
            step(dve.memset(eps[:], RMS_EPS))
            dve.tensor_scalar(mcol[:, :, 1, :], mcol[:, :, 1, :], 1.0, None, ALU.add).then_inc(plus_one, 1)
            dve.wait_ge(plus_one, 1)
            for (src, m, v, n) in pairs(dve):
                for b in range(2):
                    dve.wait_ge(turned[1], 2 * n + b + 3)
                    for k in range(4):
                        last = dve.tensor_scalar(aT[:, 4 + k, ds(n * 2 * P + b * P, P)], pr[1][:, k * P:(k + 1) * P],
                                                 mcol[:, v, 1, 4 + k:5 + k], mcol[:, v, 0, 4 + k:5 + k], ALU.mult, ALU.add)
                    last.then_inc(moved[1], 1)
            for (col, dup, norm, rope, dst, at), i, n in groups(dve):
                step.restart()
                for b in range(2):
                    o = dst[:, ds(i * 2 + at + b, 1), :].rearrange("p o n -> p (o n)")
                    if norm is not None:
                        dve.wait_ge(rooted[b], i + 1 + norm * 2 + b)
                        step(dve.reciprocal(sq[:, b, :], sq[:, b, :]))
                        dve.scalar_tensor_tensor(out=xs[:, b, :], in0=pa[b][:, 0:768], scalar=gain[:, norm:norm + 1],
                                                 in1=sq[:, b, :], op0=ALU.mult, op1=ALU.mult).then_inc(x_ready[b], 1)
                for b in range(2):
                    o = dst[:, ds(i * 2 + at + b, 1), :]
                    if rope:
                        dve.wait_ge(x_ready[b], n + 2)
                        dve.tensor_tensor(t1[:, b, :], xs[:, b, 0:512], cos[:], ALU.mult)
                        dve.wait_ge(rotated[b], n + 1 - _unrotated(l, col))
                        step(dve.tensor_tensor(t2[:, b, :], pr[b][:, :], sin[:], ALU.mult))
                        if norm is not None:
                            dve.tensor_copy(o[:, :, 512:768], xs[:, b:b + 1, 512:768])
                        dve.tensor_tensor(o[:, :, 0:512], t1[:, b:b + 1, :], t2[:, b:b + 1, :], ALU.add).then_inc(written[b], 1)
                    else:
                        dve.wait_ge(projected[b], n + 2)
                        dve.tensor_copy(o[:, :, 0:512], pa[b][:, 0:512].rearrange("p (o n) -> p o n", o=1)).then_inc(written[b], 1)


def _unrotated(l, col):
    n = 0
    for c, k, dup, norm, rope, dst, at in GROUPS[l]:
        if c == col:
            return n
        n += 0 if rope else k // 2


def neighbour_bias_phase(nc, g, bias):
    NH, NR, NC = 8, 15, 31
    PAD = (P - NC) // 2
    W = 14 * HD // 2
    with Phase(nc) as ph:
        pad = ph.sb("pad", [NH * NR, P])
        keep, mask, flip = ph.sb("keep", [P, HD]), ph.sb("mask", [P, HD]), ph.sb("flip", [P, P])
        back = ph.sb("back", [P, NH, 14, HD])
        pF = [ph.ps(f"pF{b}", [P, 512]) for b in range(2)]
        zeroed, table_in, padded, bias_in, const_in, flipped, kept, order = (
            ph.sem(n) for n in ("zeroed", "table_in", "padded", "bias_in", "const_in", "flipped", "kept", "order"))
        block = ph.block()

        @block.sync
        def _(sp):
            ph.clear_other_pool(sp)
            for dst, src in ((keep, "na_keep"), (mask, "na_mask"), (flip, "flip64")):
                sp.dma_start(dst[:], g[src]).then_inc(const_in, 16)
            sp.wait_ge(zeroed, 1)
            sp.dma_start(pad[:, PAD:PAD + NC], g["na_rpb"][0].rearrange("h r k -> (h r) k")).then_inc(table_in, 16)
            sp.wait_ge(table_in, 16)
            sp.dma_start(g["rpb_pad"], pad[:]).then_inc(padded, 16)
            sp.wait_ge(padded, 16)
            for h in range(NH):
                for r in range(2):
                    src = bass.AP(g["rpb_pad"].tensor, (h * NR + 1 - r) * P, [[1, 64], [P, 14], [1, 64]])
                    sp.dma_start(back[r * 64:(r + 1) * 64, h], src).then_inc(bias_in, 16)

        @block.tensor
        def _(pe):
            pe.wait_ge(const_in, 48)
            pe.wait_ge(bias_in, 16 * 2 * NH)
            for i in range(2 * NH):
                if i >= 2:
                    pe.wait_ge(kept, i - 1)
                pe.matmul(pF[i % 2][:, 0:W], flip[:], back[:, i // 2].rearrange("p a n -> p (a n)")[:, (i % 2) * W:(i % 2 + 1) * W],
                          start=True, stop=True).then_inc(flipped, 1)

        @block.vector
        def _(dve):
            step = Steps(dve, order)
            dve.memset(pad[:], 0.0).then_inc(zeroed, 1)
            dve.wait_ge(const_in, 48)
            for i in range(2 * NH):
                def wide(x):
                    return x[:].rearrange("p (o n) -> p o n", o=1).broadcast_to([P, 7, HD])
                to = bias[:, i // 2, (i % 2) * 7:(i % 2 + 1) * 7, :]
                dve.wait_ge(flipped, i + 1)
                dve.tensor_tensor(to, pF[i % 2][:, 0:W].rearrange("p (a n) -> p a n", n=HD), wide(keep), ALU.mult).then_inc(kept, 1)
                dve.wait_ge(kept, i + 1)
                step(dve.tensor_tensor(to, to, wide(mask), ALU.add))


def attention_phase(nc, g, l, srcs, qT, kT, V, logits, na_bias):
    diff = 4 if l == 0 else 0
    R = diff + 2 * (8 - diff)
    last_l = l == DEPTH - 1
    groups = [(0, NLAT, 0, 6)] + ([] if last_l else [(NLAT, NCTX, 1, 2)])
    with Phase(nc) as ph:
        q2 = ph.sb("q2", [P, 8, P])
        E = ph.sb("E", [P, 2, 2, TOK])
        a = ph.sb("a", [P, 2, TOK]) if diff else None
        PT = ph.sb("PT", [P, 6, P])
        o = ph.sb("o", [P, D])
        oT = ph.sb("oT", [P, C, P])
        wout = ph.sb("wout", [P, C, D])
        wr = ph.sb("wr", [P, C, 36])
        rb = ph.sb("rb", [P, 36])
        h = ph.sb("h", [P, D])
        r = ph.sb("r", [P, D])
        f = ph.sb("f", [P, D])
        nv = len(groups)
        mrow = ph.sb("mrow", [P, nv, 3, D])
        lrow = ph.sb("lrow", [P, 2, D])
        st = ph.sb("st", [P, 2, 2, 6])
        bn = ph.sb("bn", [P, 2, 6])
        mv = ph.sb("mv", [P, 4])
        eps = ph.sb("eps", [P, 2])
        lv = ph.sb("lv", [P, 4, HD]) if diff else None
        lam = ph.sb("lam", [P, 8]) if diff else None
        sub_g = ph.sb("sub_g", [P, P]) if diff else None
        ss = ph.sb("ss", [P, 4]) if diff else None
        wmask = None if diff else ph.sb("wmask", [P, NLAT, LAT])
        sink = None if diff else ph.sb("sink", [P, 8])
        pS = [ph.ps(f"pS{b}", [P, 1024]) for b in range(2)]
        pT = ph.ps("pT", [P, 1024])
        pO = ph.ps("pO", [P, 2, 2, P])
        pX = ph.ps("pX", [P, 512])
        const_in, const_set, lam_sum, lam_exp = (ph.sem(n) for n in ("const_in", "const_set", "lam_sum", "lam_exp"))
        q_ready, h_in = ph.sem("q_ready"), ph.sem("h_in")
        scored, s_free, shifted, e_ready, summed, r_ready = (
            ph.sems(n) for n in ("scored", "s_free", "shifted", "e_ready", "summed", "r_ready"))
        a_ready, turned, movedA, movedD, pv, o_out, merged, mixed = (
            ph.sem(n) for n in ("a_ready", "turned", "movedA", "movedD", "pv", "o_out", "merged", "mixed"))
        o_ready, var_ready, root_ready, h_ready, f_ready, ss_ready, ss_root = (
            ph.sem(n) for n in ("o_ready", "var_ready", "root_ready", "h_ready", "f_ready", "ss_ready", "ss_root"))
        bigT, bigA, bigD, f_free, routed, logit_out, h_stored, f_stored = (
            ph.sem(n) for n in ("bigT", "bigA", "bigD", "f_free", "routed", "logit_out", "h_stored", "f_stored"))
        order, order_a = ph.sem("order"), ph.sem("order_a")
        block = ph.block()
        ident = g["ident"]
        n_const = 1 + 2 + 2 + 3 * nv + 2 + (2 if diff else 2)

        def tiles(eng):
            for base, n, v, nk in groups:
                with eng.Fori(0, n) as t:
                    yield t + base, t, v, 6 - nk, nk

        def rounds(i):
            return [i] if i < diff else [diff + 2 * (i - diff) + b for b in range(2)]

        def k_chunk(i):
            if l == 0:
                return i if i < 4 else 4 + (i - 4) // 2
            return i // 2 if i < 4 else 2 + i - 4

        def v_cols(i, b):
            if i < diff:
                return i * P, P
            grouped = i >= 4 if l == 0 else i < 4
            if grouped:
                return 512 + HD * ((i % 4) // 2), HD
            return (i % 4) * P + b * HD, HD

        @block.sync
        def _(sp):
            ph.clear_other_pool(sp)
            w_out_dram = g["ab_w_out" if l == 0 else "cd_w_out"][0].rearrange("(p k) n -> p k n", p=P)
            sp.dma_start(wout[:], w_out_dram).then_inc(const_in, 16)
            sp.dma_start(wr[:, :, 0:NG], g["moe_w_group"][l].rearrange("(p k) n -> p k n", p=P)).then_inc(const_in, 16)
            sp.dma_start(wr[:, :, NG:36], g["moe_w_router"][l].rearrange("(p k) n -> p k n", p=P)).then_inc(const_in, 16)
            sp.dma_start(rb[:, 0:NG], g["moe_b_group"][l:l + 1, :].broadcast_to([P, NG])).then_inc(const_in, 16)
            sp.dma_start(rb[:, NG:36], g["moe_b_router"][l:l + 1, :].broadcast_to([P, NE])).then_inc(const_in, 16)
            for v in range(nv):
                for j, m in enumerate((2, 3, 4)):
                    sp.dma_start(mrow[:, v, j], g["mods"][l, v:v + 1, m * D:(m + 1) * D].broadcast_to([P, D])).then_inc(const_in, 16)
            sp.dma_start(lrow[:, 0], g["ln_g"][l, 0:1, :].broadcast_to([P, D])).then_inc(const_in, 16)
            sp.dma_start(lrow[:, 1], g["ln_b"][l, 0:1, :].broadcast_to([P, D])).then_inc(const_in, 16)
            if diff:
                sp.dma_start(lv[:].rearrange("p a b -> p (a b)"),
                             g["diff_lambda"].rearrange("o a b -> o (a b)").broadcast_to([P, 4 * HD])).then_inc(const_in, 16)
                sp.dma_start(sub_g[:], g["diff_subln_g"].broadcast_to([P, P])).then_inc(const_in, 16)
            else:
                sp.dma_start(wmask[:], g["win_mask"].rearrange("(t p) n -> p t n", p=P)).then_inc(const_in, 16)
                sp.dma_start(sink[:], g["win_sink"].broadcast_to([P, 8])).then_inc(const_in, 16)
            for n, t, v, k0, nk in tiles(sp):
                sp.wait_ge(merged, n + 1)
                sp.dma_start(h[:], srcs[v][ds(t * P, P), :]).then_inc(h_in, 16)
                sp.wait_ge(h_ready, n + 1)
                sp.dma_start(g["h_mid"][ds(n * P, P), :], r[:]).then_inc(h_stored, 16)
                sp.wait_ge(f_ready, n + 1)
                sp.dma_start(g["f"][ds(n * P, P), :], f[:]).then_inc(f_stored, 16)
            total = sum(x[1] for x in groups)
            sp.wait_ge(h_stored, 16 * (total + 1))
            sp.wait_ge(f_stored, 16 * (total + 1))

        @block.gpsimd
        def _(pool):
            for n, t, v, k0, nk in tiles(pool):
                pool.wait_ge(merged, n + 1)
                pool.tensor_copy(q2[:], qT[:, :, ds(n * P, P)]).then_inc(q_ready, 1)

        @block.tensor
        def _(pe):
            pe.wait_ge(const_in, 16 * n_const)
            for n, t, v, k0, nk in tiles(pe):
                def score(i, b):
                    pe.wait_ge(s_free[b], 8 * n + i + 1)
                    rows = slice(b * HD, (b + 1) * HD)
                    if nk == 6:
                        pe.matmul(pS[b][:, 0:512], q2[rows, i, :], kT[rows, k_chunk(i), 0:512], start=True, stop=True)
                    pe.matmul(pS[b][:, 512:768], q2[rows, i, :], kT[rows, k_chunk(i), 512:768],
                              start=True, stop=True).then_inc(scored[b], 1)

                def turn(i, j):
                    c = rounds(i)[j]
                    if i < diff:
                        pe.wait_ge(a_ready, diff * n + i + 1)
                        src = a[:, i % 2]
                    else:
                        pe.wait_ge(e_ready[j], 8 * n + i + 1)
                        src = E[:, i % 2, j]
                    pe.wait_ge(movedA, R * n + c + 1)
                    pe.wait_ge(movedD, R * n + c + 1)
                    for k in range(k0, 6):
                        last = pe.transpose(pT[:, k * P:(k + 1) * P], src[:, k * P:(k + 1) * P], ident[:])
                    last.then_inc(turned, 1)

                def weigh(i, j):
                    c = rounds(i)[j]
                    pe.wait_ge(movedA, R * n + c + 2)
                    pe.wait_ge(movedD, R * n + c + 2)
                    pe.wait_ge(o_out, R * n + c + 1)
                    c0, w = v_cols(i, j)
                    for k in range(k0, 6):
                        last = pe.matmul(pO[:, i % 2, j, 0:w], PT[:, k, :], V[:, k, c0:c0 + w], start=(k == k0), stop=(k == 5))
                    last.then_inc(pv, 1)

                def turn_rows(src, count):
                    for k in range(C):
                        last = pe.transpose(pT[:, k * P:(k + 1) * P], src[:, k::C], ident[:])
                    last.then_inc(bigT, 1)
                    pe.wait_ge(bigA, 2 * n + count)
                    pe.wait_ge(bigD, 2 * n + count)

                pe.wait_ge(q_ready, n + 1)
                pe.wait_ge(merged, n + 1)
                score(0, 0)
                score(0, 1)
                for i in range(8):
                    for j in range(len(rounds(i))):
                        turn(i, j)
                        if i < 7:
                            for b in ([0, 1] if i < diff else [j]):
                                score(i + 1, b)
                        weigh(i, j)
                pe.wait_ge(o_ready, n + 1)
                turn_rows(o, 1)
                for b in range(2):
                    for k in range(C):
                        last = pe.matmul(pS[0][:, b * 512:(b + 1) * 512], oT[:, k, :], wout[:, k, b * 512:(b + 1) * 512],
                                         start=(k == 0), stop=(k == C - 1))
                last.then_inc(mixed, 1)
                pe.wait_ge(f_ready, n + 1)
                turn_rows(f, 2)
                pe.wait_ge(logit_out, n + 1)
                for k in range(C):
                    last = pe.matmul(pX[:, 0:36], oT[:, k, :], wr[:, k, :], start=(k == 0), stop=(k == C - 1))
                last.then_inc(routed, 1)

        @block.scalar
        def _(act):
            step = Steps(act, order_a)
            for s in s_free + [movedA, o_out]:
                act.sem_inc(s, 1)
            if diff:
                act.wait_ge(lam_sum, 1)
                act.activation(lam[:, 2:4], lam[:, 0:2], ACT.Exp).then_inc(lam_exp, 1)
            act.wait_ge(const_set, 1)
            for n, t, v, k0, nk in tiles(act):
                step.restart()
                keys = slice(k0 * P, TOK)

                def exp(i, b):
                    s = st[:, i % 2, b]
                    act.wait_ge(shifted[b], 8 * n + i + 1)
                    src, scale = (pS[b][:, keys], SCALE) if l == 0 else (E[:, i % 2, b, keys], 1.0)
                    last = act.activation(E[:, i % 2, b, keys], src, ACT.Exp, bias=s[:, 1:2], scale=scale, accum_out=s[:, 2:3])
                    if l == 1 and i < 4:
                        last = act.activation(s[:, 3:4], sink[:, 2 * i + b:2 * i + b + 1], ACT.Exp, bias=s[:, 1:2])
                    last.then_inc(e_ready[b], 1)
                    if l == 0:
                        act.wait_ge(e_ready[b], 8 * n + i + 1)
                        act.sem_inc(s_free[b], 1)

                exp(0, 0)
                exp(0, 1)
                for i in range(8):
                    for j, c in enumerate(rounds(i)):
                        act.wait_ge(turned, R * n + c + 1)
                        if nk == 6:
                            act.activation(PT[:, 0:4, :].rearrange("p k n -> p (k n)"), pT[:, 0:512], ACT.Copy).then_inc(movedA, 1)
                        else:
                            act.sem_inc(movedA, 1)
                        if i < 7:
                            for b in ([0, 1] if i < diff else [j]):
                                exp(i + 1, b)
                        act.wait_ge(pv, R * n + c + 1)
                        if i < diff:
                            act.activation(o[:, i * P:(i + 1) * P], pO[:, i % 2, j, :], ACT.Copy).then_inc(o_out, 1)
                        else:
                            act.wait_ge(r_ready[j], (8 - diff) * n + i - diff + 1)
                            act.activation(o[:, i * P + j * HD:i * P + (j + 1) * HD], pO[:, i % 2, j, 0:HD], ACT.Copy,
                                           scale=st[:, i % 2, j, 4:5]).then_inc(o_out, 1)
                if diff:
                    act.wait_ge(ss_ready, n + 1)
                    act.activation(ss[:], ss[:], ACT.Sqrt, scale=1.0 / P, bias=eps[:, 1:2]).then_inc(ss_root, 1)
                for c in range(2):
                    act.wait_ge(bigT, 2 * n + c + 1)
                    act.activation(oT[:, 0:4, :].rearrange("p k n -> p (k n)"), pT[:, 0:512], ACT.Copy).then_inc(bigA, 1)
                    if c == 0:
                        act.wait_ge(var_ready, n + 1)
                        act.activation(mv[:, 2:3], mv[:, 1:2], ACT.Sqrt, bias=eps[:, 0:1]).then_inc(root_ready, 1)

        @block.vector
        def _(dve):
            step = Steps(dve, order)
            for s in (movedD, merged, logit_out):
                dve.sem_inc(s, 1)
            dve.sem_inc(h_stored, 16)
            dve.sem_inc(f_stored, 16)
            dve.wait_ge(const_in, 16 * n_const)
            dve.memset(eps[:, 0:1], LN_EPS)
            dve.memset(eps[:, 1:2], RMS_EPS)
            for v in range(nv):
                last = dve.tensor_scalar(mrow[:, v, 2], mrow[:, v, 2], 1.0, None, ALU.add)
            last.then_inc(const_set, 1)
            dve.wait_ge(const_set, 1)
            if diff:
                for j in range(2):
                    last = dve.tensor_tensor_reduce(lv[:, 2 * j], lv[:, 2 * j], lv[:, 2 * j + 1], 1.0, 0.0, ALU.mult, ALU.add, lam[:, j:j + 1])
                last.then_inc(lam_sum, 1)
                dve.wait_ge(lam_exp, 1)
                step(dve.tensor_tensor(lam[:, 4:5], lam[:, 3:4], lam[:, 2:3], ALU.subtract))
                step(dve.tensor_scalar(lam[:, 5:6], lam[:, 4:5], -LAM_INIT, None, ALU.add))
                step(dve.tensor_scalar(sub_g[:], sub_g[:], 1.0 - LAM_INIT, None, ALU.mult))
            for n, t, v, k0, nk in tiles(dve):
                step.restart()
                keys = slice(k0 * P, TOK)

                def shift(i, b):
                    s = st[:, i % 2, b]
                    dve.wait_ge(scored[b], 8 * n + i + 1)
                    if l == 0:
                        step(dve.tensor_reduce(s[:, 0:1], pS[b][:, keys], AX.X, ALU.max))
                        dve.tensor_scalar(s[:, 1:2], s[:, 0:1], -SCALE, None, ALU.mult).then_inc(shifted[b], 1)
                        return
                    e = E[:, i % 2, b]
                    if i < 4:
                        bias = wmask[:, ds(t, 1), :].rearrange("p o n -> p (o n)")
                    else:
                        bias = na_bias[:, 2 * (i - 4) + b, ds(6 - 2 * t, 8), :].rearrange("p a n -> p (a n)")
                    dve.scalar_tensor_tensor(out=e[:, 0:512], in0=pS[b][:, 0:512], scalar=SCALE, in1=bias, op0=ALU.mult, op1=ALU.add)
                    dve.tensor_scalar(e[:, 512:768], pS[b][:, 512:768], SCALE, None, ALU.mult).then_inc(s_free[b], 1)
                    dve.wait_ge(s_free[b], 8 * n + i + 2)
                    step(dve.tensor_reduce(s[:, 0:1], e[:, :], AX.X, ALU.max))
                    if i < 4:
                        step(dve.tensor_tensor(s[:, 0:1], s[:, 0:1], sink[:, 2 * i + b:2 * i + b + 1], ALU.max))
                    dve.tensor_scalar(s[:, 1:2], s[:, 0:1], -1.0, None, ALU.mult).then_inc(shifted[b], 1)

                shift(0, 0)
                shift(0, 1)
                for i in range(8):
                    s = st[:, i % 2]
                    for b in range(2):
                        dve.wait_ge(e_ready[b], 8 * n + i + 1)
                        if l == 1 and i < 4:
                            step(dve.tensor_tensor(s[:, b, 2:3], s[:, b, 2:3], s[:, b, 3:4], ALU.add))
                        if i < diff:
                            step(dve.reciprocal(s[:, b, 4:5], s[:, b, 2:3]))
                        else:
                            dve.reciprocal(s[:, b, 4:5], s[:, b, 2:3]).then_inc(r_ready[b], 1)
                    if i < diff:
                        step(dve.tensor_tensor(s[:, 1, 5:6], s[:, 1, 4:5], lam[:, 5:6], ALU.mult))
                        step(dve.tensor_scalar(a[:, i % 2, keys], E[:, i % 2, 0, keys], s[:, 0, 4:5], None, ALU.mult))
                        dve.scalar_tensor_tensor(out=a[:, i % 2, keys], in0=E[:, i % 2, 1, keys], scalar=s[:, 1, 5:6],
                                                 in1=a[:, i % 2, keys], op0=ALU.mult, op1=ALU.add).then_inc(a_ready, 1)
                    for j, c in enumerate(rounds(i)):
                        dve.wait_ge(turned, R * n + c + 1)
                        dve.tensor_copy(PT[:, 4:6, :].rearrange("p k n -> p (k n)"), pT[:, 512:768]).then_inc(movedD, 1)
                        if i < 7:
                            for b in ([0, 1] if i < diff else [j]):
                                shift(i + 1, b)
                dve.wait_ge(o_out, R * (n + 1) + 1)
                if diff:
                    dve.wait_ge(f_stored, 16 * (n + 1))
                    for hd in range(4):
                        oh = o[:, hd * P:(hd + 1) * P]
                        last = dve.tensor_tensor_reduce(f[:, hd * P:(hd + 1) * P], oh, oh, 1.0, 0.0, ALU.mult, ALU.add, ss[:, hd:hd + 1])
                    last.then_inc(ss_ready, 1)
                    dve.wait_ge(ss_root, n + 1)
                    step(dve.reciprocal(ss[:], ss[:]))
                    for hd in range(4):
                        oh = o[:, hd * P:(hd + 1) * P]
                        last = dve.scalar_tensor_tensor(out=oh, in0=oh, scalar=ss[:, hd:hd + 1], in1=sub_g[:], op0=ALU.mult, op1=ALU.mult)
                    last.then_inc(o_ready, 1)
                else:
                    dve.sem_inc(o_ready, 1)
                dve.wait_ge(bigT, 2 * n + 1)
                dve.tensor_copy(oT[:, 4:8, :].rearrange("p k n -> p (k n)"), pT[:, 512:1024]).then_inc(bigD, 1)
                dve.wait_ge(mixed, n + 1)
                dve.wait_ge(h_in, 16 * (n + 1))
                dve.wait_ge(h_stored, 16 * (n + 1))
                dve.wait_ge(f_stored, 16 * (n + 1))
                step(dve.tensor_tensor(r[:], pS[0][:, :], mrow[:, v, 0], ALU.mult))
                step(dve.scalar_tensor_tensor(out=r[:], in0=h[:], scalar=ALPHA, in1=r[:], op0=ALU.mult, op1=ALU.add))
                dve.sem_inc(merged, 1)
                layer_norm_rows(dve, step, r, f, bn, mv, lrow, var_ready, root_ready, n)
                dve.tensor_tensor(r[:], f[:], lrow[:, 1], ALU.add).then_inc(h_ready, 1)
                dve.wait_ge(h_ready, n + 1)
                step(dve.tensor_tensor(f[:], r[:], mrow[:, v, 2], ALU.mult))
                dve.tensor_tensor(f[:], f[:], mrow[:, v, 1], ALU.add).then_inc(f_ready, 1)
                dve.wait_ge(bigT, 2 * n + 2)
                dve.tensor_copy(oT[:, 4:8, :].rearrange("p k n -> p (k n)"), pT[:, 512:1024]).then_inc(bigD, 1)
                dve.wait_ge(routed, n + 1)
                dve.tensor_tensor(logits[:, ds(n, 1), :], pX[:, 0:36].rearrange("p (o n) -> p o n", o=1),
                                  rb[:].rearrange("p (o n) -> p o n", o=1), ALU.add).then_inc(logit_out, 1)


def layer_norm_rows(dve, step, r, f, bn, mv, lrow, var_ready, root_ready, n):
    dve.bn_stats(bn[:, 0, :], r[:, 0:512])
    step(dve.bn_stats(bn[:, 1, :], r[:, 512:1024]))
    dve.bn_aggr(mv[:, 0:2], bn[:]).then_inc(var_ready, 1)
    dve.wait_ge(root_ready, n + 1)
    step(dve.reciprocal(mv[:, 3:4], mv[:, 2:3]))
    step(dve.tensor_scalar(f[:], r[:], mv[:, 0:1], mv[:, 3:4], ALU.subtract, ALU.mult))
    step(dve.tensor_tensor(f[:], f[:], lrow[:, 0], ALU.mult))


BIG = 1 << 20


def items(nt):
    n = (2 * nt * P - NE) // P + NE
    return n + n % 2


def routing_phase(nc, g, nt, logits, share, gather_at, scatter_at, expert_of, pairs_of):
    T = nt * P
    NW = items(nt)
    with Phase(nc) as ph:
        x = ph.sb("x", [P, nt, NE])
        ohg = ph.sb("ohg", [P, nt, NG])
        oh = ph.sb("oh", [P, 2, nt, NE])
        both = ph.sb("both", [P, nt, NE])
        tmp = ph.sb("tmp", [P, nt, NE])
        vals = ph.sb("vals", [P, 2, nt, 3, NW])
        m = ph.sb("m", [P, nt, 12])
        rank = ph.sb("rank", [P, 2, nt])
        place = ph.sb("place", [P, 2, nt])
        item = ph.sb("item", [P, 2, nt])
        full = ph.sb("full", [P, 2, nt])
        slot = ph.sb("slot", [P, 2, P])
        count, token = ph.sb("count", [P, P]), ph.sb("token", [P, NTILE])
        down = ph.sb("down", [P, P])
        ones, earlier = ph.sb("ones", [P, P]), ph.sb("earlier", [P, P])
        cut = ph.sb("cut", [P, 3, NE])
        past = ph.sb("past", [P, NW, NE])
        ids = ph.sb("ids", [P, NW])
        number = ph.sb("number", [P, 1], I32)
        table = ph.sb("table", [P, 3, NW])
        pR = ph.ps("pR", [P, nt + 1, NE])
        pV = ph.ps("pV", [P, 3 * NW])
        const_in, exp_in, exp_out, used, ranked, slotted, slot_used = (
            ph.sem(n) for n in ("const_in", "exp_in", "exp_out", "used", "ranked", "slotted", "slot_used"))
        order = ph.sem("order")
        block = ph.block()

        @block.sync
        def _(sp):
            ph.clear_other_pool(sp)
            for dst, src in ((count, "count"), (token, "token"), (ones, "ones"), (earlier, "earlier")):
                sp.dma_start(dst[:], g[src]).then_inc(const_in, 16)

        @block.scalar
        def _(act):
            act.wait_ge(exp_in, 1)
            act.activation(m[:, :, 4:8], m[:, :, 4:8], ACT.Exp).then_inc(exp_out, 1)
            act.wait_ge(exp_in, 2)
            act.activation(m[:, :, 9:10], m[:, :, 9:10], ACT.Exp).then_inc(exp_out, 1)

        @block.tensor
        def _(pe):
            pe.wait_ge(const_in, 64)
            pe.wait_ge(used, 1)
            for t in range(nt + 1):
                for s in range(t):
                    last = pe.matmul(pR[:, t, :], ones[:], both[:, s, :], start=(s == 0), stop=(t == nt and s == nt - 1))
                if t < nt:
                    last = pe.matmul(pR[:, t, :], earlier[:], both[:, t, :], start=(t == 0), stop=True)
            last.then_inc(ranked, 1)
            for i in range(2 * nt):
                k, t = i % 2, i // 2
                pe.wait_ge(slotted, i + 1)
                pe.matmul(pV[:, :], slot[:, k, :], vals[:, k, t].rearrange("p a w -> p (a w)"),
                          start=(i == 0), stop=(i == 2 * nt - 1)).then_inc(slot_used, 1)

        @block.vector
        def _(dve):
            step = Steps(dve, order)
            dve.wait_ge(const_in, 64)
            gl = logits[:, 0:nt, 0:NG]
            el = logits[:, 0:nt, NG:36]

            def wide(ap, n):
                return ap.broadcast_to([P, nt, n])

            def row(ap, n):
                return ap.rearrange("p (o n) -> p o n", o=1).broadcast_to([P, nt, n])

            def first_max(src, n, m_at, out):
                step(dve.tensor_reduce(m[:, :, m_at:m_at + 1], src, AX.X, ALU.max))
                step(dve.tensor_tensor(tmp[:, :, 0:n], src, wide(m[:, :, m_at:m_at + 1], n), ALU.is_equal))
                step(dve.tensor_tensor(tmp[:, :, 0:n], tmp[:, :, 0:n], row(down[:, 0:n], n), ALU.mult))
                step(dve.tensor_reduce(m[:, :, 8:9], tmp[:, :, 0:n], AX.X, ALU.max))
                step(dve.tensor_tensor(out, tmp[:, :, 0:n], wide(m[:, :, 8:9], n), ALU.is_equal))

            step(dve.tensor_scalar(down[:], count[:], -1.0, float(P), ALU.mult, ALU.add))
            first_max(gl, NG, 0, ohg[:])
            dve.tensor_tensor(m[:, :, 4:8], gl, wide(m[:, :, 0:1], NG), ALU.subtract).then_inc(exp_in, 1)
            step(dve.tensor_scalar(ohg[:], ohg[:], -1.0, -NEG, ALU.add, ALU.mult))
            for e in range(NG):
                step(dve.tensor_tensor(x[:, :, e * EPG:(e + 1) * EPG], el[:, :, e * EPG:(e + 1) * EPG],
                                       wide(ohg[:, :, e:e + 1], EPG), ALU.add))
            first_max(x[:], NE, 1, oh[:, 0])
            step(dve.tensor_scalar(both[:], oh[:, 0], -1e38, None, ALU.mult))
            step(dve.tensor_tensor(x[:], x[:], both[:], ALU.add))
            first_max(x[:], NE, 2, oh[:, 1])
            dve.tensor_tensor(both[:], oh[:, 0], oh[:, 1], ALU.add).then_inc(used, 1)
            dve.tensor_tensor(m[:, :, 9:10], m[:, :, 2:3], m[:, :, 1:2], ALU.subtract).then_inc(exp_in, 1)
            dve.wait_ge(exp_out, 1)
            step(dve.tensor_reduce(m[:, :, 10:11], m[:, :, 4:8], AX.X, ALU.add))
            dve.wait_ge(exp_out, 2)
            step(dve.tensor_scalar(m[:, :, 11:12], m[:, :, 9:10], 1.0, None, ALU.add))
            step(dve.tensor_tensor(m[:, :, 10:11], m[:, :, 10:11], m[:, :, 11:12], ALU.mult))
            step(dve.reciprocal(share[:, 0:nt, 0:1], m[:, :, 10:11]))
            step(dve.tensor_tensor(share[:, 0:nt, 1:2], share[:, 0:nt, 0:1], m[:, :, 9:10], ALU.mult))
            dve.wait_ge(ranked, 1)
            step(dve.memset(cut[:, 0], 0.0))
            for j in range(nt):
                step(dve.scalar_tensor_tensor(out=cut[:, 0], in0=pR[:, nt, :], scalar=float(j * P), in1=cut[:, 0], op0=ALU.is_gt, op1=ALU.add))
            step(dve.tensor_tensor_scan(cut[:, 1], ones[:, 0:NE], cut[:, 0], 0.0, ALU.mult, ALU.add))
            step(dve.tensor_tensor(cut[:, 2], cut[:, 1], cut[:, 0], ALU.subtract))
            for k in range(2):
                step(dve.tensor_tensor(tmp[:], oh[:, k], pR[:, 0:nt, :], ALU.mult))
                step(dve.tensor_reduce(rank[:, k].rearrange("p (t o) -> p t o", o=1), tmp[:], AX.X, ALU.add))
                step(dve.tensor_tensor(tmp[:], oh[:, k], row(cut[:, 2], NE), ALU.mult))
                step(dve.tensor_reduce(item[:, k].rearrange("p (t o) -> p t o", o=1), tmp[:], AX.X, ALU.add))
            step(dve.tensor_copy(place[:], rank[:]))
            for j in range(1, nt):
                step(dve.tensor_scalar(full[:], rank[:], float(j * P), None, ALU.is_ge))
                step(dve.tensor_tensor(item[:], item[:], full[:], ALU.add))
                step(dve.scalar_tensor_tensor(out=place[:], in0=full[:], scalar=-float(P), in1=place[:], op0=ALU.mult, op1=ALU.add))
            for i in range(2 * nt):
                k, t = i % 2, i // 2
                v = vals[:, k, t]
                step(dve.tensor_scalar(v[:, 1, :], count[:, 0:NW], item[:, k, t:t + 1], None, ALU.is_equal))
                dve.tensor_scalar(v[:, 0, :], v[:, 1, :], token[:, t:t + 1], None, ALU.mult)
                dve.tensor_scalar(v[:, 2, :], v[:, 1, :], float(k * T), None, ALU.mult)
                if i >= 2:
                    dve.wait_ge(slot_used, i - 1)
                dve.tensor_scalar(slot[:, k, :], count[:], place[:, k, t:t + 1], None, ALU.is_equal).then_inc(slotted, 1)
            step(dve.tensor_tensor(past[:], count[:, 0:NW].rearrange("p (w o) -> p w o", o=1).broadcast_to([P, NW, NE]),
                                   cut[:, 1].rearrange("p (o e) -> p o e", o=1).broadcast_to([P, NW, NE]), ALU.is_ge))
            step(dve.tensor_reduce(ids[:].rearrange("p (w o) -> p w o", o=1), past[:], AX.X, ALU.add))
            step(dve.tensor_scalar(ids[:], ids[:], float(NE - 1), None, ALU.min))
            step(dve.tensor_copy(expert_of[:, 0:NW], ids[:]))
            step(dve.tensor_scalar(cut[:, 0, 0:1], cut[:, 1, NE - 1:NE], 1.0, None, ALU.add))
            step(dve.tensor_copy(number[:], cut[:, 0, 0:1]))
            step(dve.tensor_scalar(pairs_of[:], number[:], 1, None, ALU.arith_shift_right))
            step(dve.memset(gather_at[:, NW:NW + 2], 0))
            dve.wait_ge(slot_used, 2 * nt)
            step(dve.tensor_copy(table[:].rearrange("p a w -> p (a w)"), pV[:, :]))
            step(dve.tensor_copy(gather_at[:, 0:NW], table[:, 0]))
            step(dve.tensor_tensor(table[:, 0], table[:, 0], table[:, 2], ALU.add))
            step(dve.tensor_scalar(table[:, 1], table[:, 1], -float(BIG), float(BIG), ALU.mult, ALU.add))
            step(dve.tensor_tensor(table[:, 0], table[:, 0], table[:, 1], ALU.add))
            step(dve.tensor_copy(scatter_at[:, 0:NW], table[:, 0]))


def expert_phase(nc, g, l, nt, gather_at, scatter_at, expert_of, pairs_of):
    T = nt * P
    HC = DE // P
    NW = items(nt)
    with Phase(nc) as ph:
        w1, w3 = ph.sb("w1", [P, 2, C, DE]), ph.sb("w3", [P, 2, C, DE])
        w2 = ph.sb("w2", [P, 2, HC, D])
        at = ph.sb("at", [P, 2, 2], I32)
        x = ph.sb("x", [P, 2, D])
        xT = ph.sb("xT", [P, 2, C, P])
        hs = ph.sb("hs", [P, 2, DE])
        hh = ph.sb("hh", [P, 2, DE])
        hT = ph.sb("hT", [P, 2, HC, P])
        y = ph.sb("y", [P, 2, D])
        pT = [ph.ps(f"pT{i}", [P, 512]) for i in range(2)]
        pH = [[ph.ps(f"pH{b}{k}", [P, DE]) for k in range(2)] for b in range(2)]
        pY = ph.ps("pY", [P, 1024])
        w13_in, w2_in, y_free, hidden, gated, silu, multiplied = (
            ph.sems(n) for n in ("w13_in", "w2_in", "y_free", "hidden", "gated", "silu", "multiplied"))
        x_in, y_out = ([ph.stack.enter_context(nc.semaphore(f"{n}{b}_{l}", num=Phase.FIRST - 8 + 4 * l + 2 * i + b)) for b in range(2)]
                       for i, n in enumerate(("x_in", "y_out")))
        turned, moved = ph.sems("turned"), ph.sems("moved")
        yA, yD, order = (ph.sem(n) for n in ("yA", "yD", "order"))
        block = ph.block()
        ident = g["ident"]
        QUADS = [(0, "h", 0, 0), (1, "x", 0, 0), (0, "x", 0, 4), (1, "h", 1, 0), (0, "x", 1, 0), (1, "x", 1, 4)]
        HEAD = [(0, "x", 0, 0), (1, "x", 0, 4), (0, "x", 1, 0), (1, "x", 1, 4)]

        def pair_loop(eng):
            n = eng.value_load(pairs_of[0:1, 0:1], min_val=1, max_val=NW // 2)
            with eng.Fori(0, n) as p:
                yield p

        def empty(eng, bank, quads, at0):
            for r, (_, what, b, k0) in enumerate([q for q in quads if q[0] == bank]):
                yield at0 + r, what, b, (xT[:, b, k0:k0 + 4] if what == "x" else hT[:, b]).rearrange("p k n -> p (k n)")

        @block.sync
        def _(sp):
            ph.clear_other_pool(sp)
            for p in pair_loop(sp):
                for b in range(2):
                    e = sp.value_load(expert_of[0:1, ds(2 * p + b, 1)], min_val=0, max_val=NE - 1)
                    sp.wait_ge(hidden[b], p + 1)
                    for dst, src in ((w1, "moe_w1"), (w3, "moe_w3")):
                        sp.dma_start(dst[:, b], g[src][l, ds(e, 1)].rearrange("o (p k) n -> p (o k) n", p=P)).then_inc(w13_in[b], 16)
                    sp.wait_ge(multiplied[b], p + 1)
                    sp.dma_start(w2[:, b], g["moe_w2"][l, ds(e, 1)].rearrange("o (p k) n -> p (o k) n", p=P)).then_inc(w2_in[b], 16)

        @block.gpsimd
        def _(pool):
            last_row, last_out = pool.to_reg(T - 1), pool.to_reg(2 * T - 1)
            step = Steps(pool, order)

            def gather(p, b):
                step(pool.tensor_copy(at[:, b, 0:1], gather_at[:, ds(2 * p + b, 1)]))
                pool.indirect_dma_start(out=x[:, b], out_offset=None, in_=g["f"][0:T, :],
                                        in_offset=bass.IndirectOffsetOnAxis(ap=at[:, b, 0:1], axis=0),
                                        bounds_check=last_row, oob_is_err=False).then_inc(x_in[b], 16)

            for b in range(2):
                pool.sem_inc(y_free[b], 1)
                gather(0, b)
            for p in pair_loop(pool):
                step.restart()
                for b in range(2):
                    for bank in range(2):
                        pool.wait_ge(turned[bank], 3 * p + 1 + b)
                    gather(p + 1, b)
                for b in range(2):
                    pool.wait_ge(yA, 2 * p + b + 2)
                    pool.wait_ge(yD, 2 * p + b + 2)
                    step(pool.tensor_copy(at[:, b, 1:2], scatter_at[:, ds(2 * p + b, 1)]))
                    pool.indirect_dma_start(out=g["y"][0:2 * T, :], out_offset=bass.IndirectOffsetOnAxis(ap=at[:, b, 1:2], axis=0),
                                            in_=y[:, b], in_offset=None, bounds_check=last_out, oob_is_err=False).then_inc(y_out[b], 16)
                for b in range(2):
                    pool.wait_ge(y_out[b], 16 * (p + 1))
                    pool.sem_inc(y_free[b], 1)
                    pool.wait_ge(x_in[b], 16 * (p + 2))

        @block.tensor
        def _(pe):
            def turn(bank, what, b, k0, r):
                src = (lambda k: x[:, b, k::C]) if what == "x" else (lambda k: hh[:, b, k::HC])
                if r is not None:
                    pe.wait_ge(moved[bank], r)
                for k in range(4):
                    last = pe.transpose(pT[bank][:, k * P:(k + 1) * P], src(k0 + k), ident[:])
                last.then_inc(turned[bank], 1)

            for b in range(2):
                pe.sem_inc(hidden[b], 1)
                pe.sem_inc(multiplied[b], 1)
            for i, (bank, what, b, k0) in enumerate(HEAD):
                pe.wait_ge(x_in[b], 16)
                turn(bank, what, b, k0, i // 2 if i >= 2 else None)
            for p in pair_loop(pe):
                for b in range(2):
                    pe.wait_ge(w13_in[b], 32 * (p + 1))
                    pe.wait_ge(gated[b], p + 1)
                    pe.wait_ge(moved[0], 3 * p + 1 + b)
                    pe.wait_ge(moved[1], 3 * p + 1 + b)
                    for i, w in enumerate((w1, w3)):
                        for k in range(C):
                            last = pe.matmul(pH[b][i][:], xT[:, b, k, :], w[:, b, k, :], start=(k == 0), stop=(k == C - 1))
                    last.then_inc(hidden[b], 1)
                for b in range(2):
                    pe.wait_ge(gated[b], p + 2)
                    pe.wait_ge(x_in[b], 16 * (p + 2))
                    for j in range(3):
                        i = 3 * b + j
                        turn(*QUADS[i], 3 * p + 2 + i // 2)
                    pe.wait_ge(moved[b], 3 * p + 3 + b)
                    pe.wait_ge(w2_in[b], 16 * (p + 1))
                    pe.wait_ge(yA, 2 * p + b + 1)
                    pe.wait_ge(yD, 2 * p + b + 1)
                    for i in range(2):
                        for k in range(HC):
                            last = pe.matmul(pY[:, i * 512:(i + 1) * 512], hT[:, b, k, :], w2[:, b, k, i * 512:(i + 1) * 512],
                                             start=(k == 0), stop=(k == HC - 1))
                    last.then_inc(multiplied[b], 1)

        @block.scalar
        def _(act):
            act.sem_inc(yA, 1)
            for r, what, b, to in empty(act, 0, HEAD, 1):
                act.wait_ge(turned[0], r)
                act.activation(to, pT[0][:], ACT.Copy).then_inc(moved[0], 1)
            for p in pair_loop(act):
                for b in range(2):
                    act.wait_ge(hidden[b], p + 2)
                    act.activation(hs[:, b], pH[b][0][:], ACT.Silu).then_inc(silu[b], 1)
                quads = list(empty(act, 0, QUADS, 3))
                for b in range(2):
                    for r, what, _, to in (quads[:2] if b == 0 else quads[2:]):
                        act.wait_ge(turned[0], 3 * p + r)
                        act.activation(to, pT[0][:], ACT.Copy).then_inc(moved[0], 1)
                    act.wait_ge(multiplied[b], p + 2)
                    act.wait_ge(y_free[b], p + 1)
                    act.activation(y[:, b, 0:512], pY[:, 0:512], ACT.Copy).then_inc(yA, 1)

        @block.vector
        def _(dve):
            dve.sem_inc(yD, 1)
            for b in range(2):
                dve.sem_inc(gated[b], 1)
            for r, what, b, to in empty(dve, 1, HEAD, 1):
                dve.wait_ge(turned[1], r)
                dve.tensor_copy(to, pT[1][:]).then_inc(moved[1], 1)
            for p in pair_loop(dve):
                for b in range(2):
                    dve.wait_ge(silu[b], p + 1)
                    dve.tensor_tensor(hh[:, b], hs[:, b], pH[b][1][:], ALU.mult).then_inc(gated[b], 1)
                quads = list(empty(dve, 1, QUADS, 3))
                for b in range(2):
                    for r, what, _, to in (quads[:1] if b == 0 else quads[1:]):
                        dve.wait_ge(turned[1], 3 * p + r)
                        dve.tensor_copy(to, pT[1][:]).then_inc(moved[1], 1)
                    dve.wait_ge(multiplied[b], p + 2)
                    dve.wait_ge(y_free[b], p + 1)
                    dve.tensor_copy(y[:, b, 512:1024], pY[:, 512:1024]).then_inc(yD, 1)


def combine_phase(nc, g, l, share, out):
    last_l = l == DEPTH - 1
    groups = [(0, NLAT, 0)] + ([] if last_l else [(NLAT, NCTX, 1)])
    T = sum(x[1] for x in groups) * P
    with Phase(nc) as ph:
        yh = ph.sb("yh", [P, 2, 3, D])
        r = ph.sb("r", [P, D])
        f = ph.sb("f", [P, 2, D])
        gate = ph.sb("gate", [P, len(groups), D])
        lrow = ph.sb("lrow", [P, 2, D])
        bn = ph.sb("bn", [P, 2, 6])
        mv = ph.sb("mv", [P, 4])
        eps = ph.sb("eps", [P, 1])
        const_in, eps_set, var_ready, root_ready, order = (ph.sem(n) for n in ("const_in", "eps_set", "var_ready", "root_ready", "order"))
        rows_in, summed, normed, stored = (ph.sems(n) for n in ("rows_in", "summed", "normed", "stored"))
        block = ph.block()

        def pairs(eng):
            for base, n, v in groups:
                with eng.Fori(0, n // 2) as m:
                    yield m + base // 2, v

        @block.sync
        def _(sp):
            ph.clear_other_pool(sp)
            sp.dma_start(lrow[:, 0], g["ln_g"][l, 1:2, :].broadcast_to([P, D])).then_inc(const_in, 16)
            sp.dma_start(lrow[:, 1], g["ln_b"][l, 1:2, :].broadcast_to([P, D])).then_inc(const_in, 16)
            for _, _, v in groups:
                sp.dma_start(gate[:, v], g["mods"][l, v:v + 1, 5 * D:6 * D].broadcast_to([P, D])).then_inc(const_in, 16)
            for n, v in pairs(sp):
                for b in range(2):
                    sp.wait_ge(summed[b], n + 1)
                    rows = n * 2 * P + b * P
                    sp.dma_start(yh[:, b, 0], g["y"][ds(rows, P), :]).then_inc(rows_in[b], 16)
                    sp.dma_start(yh[:, b, 1], g["y"][ds(rows + T, P), :]).then_inc(rows_in[b], 16)
                    sp.dma_start(yh[:, b, 2], g["h_mid"][ds(rows, P), :]).then_inc(rows_in[b], 16)

        @block.scalar
        def _(act):
            for b in range(2):
                act.sem_inc(stored[b], 16)
            act.wait_ge(eps_set, 1)
            for n, v in pairs(act):
                for b in range(2):
                    act.wait_ge(var_ready, 2 * n + b + 1)
                    act.activation(mv[:, 2:3], mv[:, 1:2], ACT.Sqrt, bias=eps[:]).then_inc(root_ready, 1)
                    act.wait_ge(normed[b], n + 1)
                    act.dma_start(out[ds(n * 2 * P + b * P, P), :], f[:, b]).then_inc(stored[b], 16)
            for b in range(2):
                act.wait_ge(stored[b], 16 * (T // P // 2 + 1))

        @block.vector
        def _(dve):
            step = Steps(dve, order)
            for b in range(2):
                dve.sem_inc(summed[b], 1)
            dve.memset(eps[:], LN_EPS).then_inc(eps_set, 1)
            dve.wait_ge(const_in, 16 * (2 + len(groups)))
            for n, v in pairs(dve):
                step.restart()
                for b in range(2):
                    w = share[:, ds(2 * n + b, 1), :].rearrange("p o k -> p (o k)")
                    dve.wait_ge(rows_in[b], 48 * (n + 1))
                    step(dve.tensor_scalar(r[:], yh[:, b, 0], w[:, 0:1], None, ALU.mult))
                    step(dve.scalar_tensor_tensor(out=r[:], in0=yh[:, b, 1], scalar=w[:, 1:2], in1=r[:], op0=ALU.mult, op1=ALU.add))
                    step(dve.tensor_tensor(r[:], r[:], gate[:, v], ALU.mult))
                    dve.scalar_tensor_tensor(out=r[:], in0=yh[:, b, 2], scalar=ALPHA, in1=r[:], op0=ALU.mult, op1=ALU.add).then_inc(summed[b], 1)
                    dve.wait_ge(summed[b], n + 2)
                    dve.wait_ge(stored[b], 16 * (n + 1))
                    layer_norm_rows(dve, step, r, f[:, b], bn, mv, lrow, var_ready, root_ready, n * 2 + b)
                    dve.tensor_tensor(f[:, b], f[:, b], lrow[:, 1], ALU.add).then_inc(normed[b], 1)


EPS2 = 1e-6
GH, GCH = 4, 16
NCH = LAT // GCH
GLA_Q, GLA_V, GLA_A = 256, 512, 16
SC_AT = 2 * GLA_Q + 2 * GLA_V + GLA_A
DIL_AT = SC_AT + 3 * 512
DIL_W = 1536


def norm_turn_phase(nc, g, src, gain, hT):
    with Phase(nc) as ph:
        x = ph.sb("x", [P, 2, D])
        sq = ph.sb("sq", [P, D])
        gcol = ph.sb("gcol", [P, C])
        ss = ph.sb("ss", [P, 2, 2])
        eps = ph.sb("eps", [P, 1])
        pT = [ph.ps(f"pT{i}", [P, 512]) for i in range(2)]
        const_in, eps_set, order, squared = (ph.sem(n) for n in ("const_in", "eps_set", "order", "squared"))
        x_in, rooted, scaled, turned, moved = (ph.sems(n) for n in ("x_in", "rooted", "scaled", "turned", "moved"))
        block = ph.block()

        def pairs(eng):
            with eng.Fori(0, NLAT // 2) as m:
                yield m

        @block.sync
        def _(sp):
            ph.clear_other_pool(sp)
            sp.dma_start(gcol[:], gain[0].rearrange("(p k) -> p k", p=P)).then_inc(const_in, 16)
            for m in pairs(sp):
                for b in range(2):
                    sp.wait_ge(turned[1], 2 * m + b + 1)
                    sp.dma_start(x[:, b], src[ds(m * 2 * P + b * P, P), :]).then_inc(x_in[b], 16)

        @block.scalar
        def _(act):
            act.wait_ge(eps_set, 1)
            act.wait_ge(const_in, 16)
            act.sem_inc(moved[0], 1)
            for m in pairs(act):
                for b in range(2):
                    act.wait_ge(x_in[b], 16 * (m + 1))
                    act.activation(sq[:], x[:, b], ACT.Square, accum_out=ss[:, b, 0:1]).then_inc(squared, 1)
                    act.wait_ge(squared, 2 * m + b + 1)
                    act.activation(ss[:, b, 1:2], ss[:, b, 0:1], ACT.Sqrt, scale=1.0 / D, bias=eps[:]).then_inc(rooted[b], 1)
                    act.wait_ge(turned[0], 2 * m + b + 1)
                    for k in range(4):
                        last = act.activation(hT[:, k, ds(m * 2 * P + b * P, P)], pT[0][:, k * P:(k + 1) * P], ACT.Copy, scale=gcol[:, k:k + 1])
                    last.then_inc(moved[0], 1)

        @block.vector
        def _(dve):
            step = Steps(dve, order)
            dve.memset(eps[:], EPS2).then_inc(eps_set, 1)
            dve.wait_ge(const_in, 16)
            dve.sem_inc(moved[1], 1)
            for m in pairs(dve):
                step.restart()
                for b in range(2):
                    dve.wait_ge(rooted[b], m + 1)
                    step(dve.reciprocal(ss[:, b, 1:2], ss[:, b, 1:2]))
                    dve.tensor_scalar(x[:, b], x[:, b], ss[:, b, 1:2], None, ALU.mult).then_inc(scaled[b], 1)
                    dve.wait_ge(turned[1], 2 * m + b + 3)
                    for k in range(4):
                        last = dve.tensor_scalar(hT[:, 4 + k, ds(m * 2 * P + b * P, P)], pT[1][:, k * P:(k + 1) * P], gcol[:, 4 + k:5 + k], None, ALU.mult)
                    last.then_inc(moved[1], 1)

        @block.tensor
        def _(pe):
            pe.sem_inc(turned[1], 2)
            for m in pairs(pe):
                for b in range(2):
                    pe.wait_ge(scaled[b], m + 1)
                    for h in range(2):
                        pe.wait_ge(moved[h], 2 * m + b + 1)
                        for k in range(4):
                            last = pe.transpose(pT[h][:, k * P:(k + 1) * P], x[:, b, h * 4 + k::C], g["ident"][:])
                        last.then_inc(turned[h], 1)


def angle_tables(act, dve, step, pos, ang, cos, sin, inv, pos_in, angle, tables):
    TURN = 2 * math.pi
    C1 = 6.28125
    C2 = float(np.float32(1.93500518798828125e-3))
    C3 = TURN - C1 - C2
    MAGIC = 1.5 * 2 ** 23
    if dve is not None:
        dve.wait_ge(pos_in, 48)
        step(dve.tensor_copy(ang[:], pos[:]))
        step(dve.tensor_scalar(ang[:], ang[:], inv[:], None, ALU.mult))
        step(dve.tensor_scalar(cos[:], ang[:], 1.0 / TURN, None, ALU.mult))
        step(dve.tensor_scalar(cos[:], cos[:], MAGIC, None, ALU.add))
        step(dve.tensor_scalar(cos[:], cos[:], MAGIC, None, ALU.subtract))
        for c in (C1, C2, C3):
            step(dve.scalar_tensor_tensor(out=ang[:], in0=cos[:], scalar=-c, in1=ang[:], op0=ALU.mult, op1=ALU.add))
        step(dve.tensor_scalar(ang[:], ang[:], 3.1415925, -3.1415925, ALU.min, ALU.max))
        dve.scalar_tensor_tensor(out=cos[:], in0=ang[:], scalar=-1.0, in1=ang[:], op0=ALU.mult, op1=ALU.max).then_inc(angle, 1)
        dve.wait_ge(angle, 1)
        dve.tensor_scalar(cos[:], cos[:], -1.0, math.pi / 2, ALU.mult, ALU.add).then_inc(angle, 1)
    if act is not None:
        act.wait_ge(angle, 2)
        act.activation(sin[:], ang[:], ACT.Sin).then_inc(tables, 1)
        act.activation(cos[:], cos[:], ACT.Sin).then_inc(tables, 1)


def columns_phase(nc, g, hT, col, n, dst, turn=False):
    w_dram = g["w_in_2"][0].rearrange("(p k) n -> p k n", p=P)
    with Phase(nc) as ph:
        w = ph.sb("w", [P, 2, C, P])
        xs = ph.sb("xs", [P, 2, LAT]) if turn else None
        tmp = ph.sb("tmp", [P, 2, 2, LAT]) if turn else None
        rot = ph.sb("rot", [P, P]) if turn else None
        inv = ph.sb("inv", [P, 1]) if turn else None
        pos = ph.sb("pos", [P, LAT], I32) if turn else None
        ang, cos, sin = ([ph.sb(k, [P, LAT]) for k in ("ang", "cos", "sin")]) if turn else (None,) * 3
        pa = [ph.ps(f"pa{b}", [P, 512]) for b in range(2)]
        pr = [ph.ps(f"pr{b}", [P, 512]) for b in range(2)]
        w_in, product, moved, x_ready, rotated = (ph.sems(k) for k in ("w_in", "product", "moved", "x_ready", "rotated"))
        pos_in, angle, tables, order = (ph.sem(k) for k in ("pos_in", "angle", "tables", "order"))
        block = ph.block()

        @block.sync
        def _(sp):
            ph.clear_other_pool(sp)
            if turn:
                sp.dma_start(rot[:], g["rot128"]).then_inc(pos_in, 16)
                sp.dma_start(pos[:], g["positions_2"].broadcast_to([P, LAT])).then_inc(pos_in, 16)
                sp.dma_start(inv[:], g["inv_freq"]).then_inc(pos_in, 16)
                sp.wait_ge(pos_in, 48)
            with sp.Fori(0, n // 2) as i:
                for b in range(2):
                    sp.wait_ge(product[b], i + 1)
                    sp.dma_start(w[:, b], w_dram[:, :, ds(i * 2 * P + (col + b * P), P)]).then_inc(w_in[b], 16)

        @block.tensor
        def _(pe):
            for b in range(2):
                pe.sem_inc(product[b], 1)
            if turn:
                pe.wait_ge(pos_in, 48)
            with pe.Fori(0, n // 2) as i:
                for b in range(2):
                    pe.wait_ge(w_in[b], 16 * (i + 1))
                    pe.wait_ge(x_ready[b] if turn else moved[b], i + 1)
                    for k in range(C):
                        last = pe.matmul(pa[b][:], w[:, b, k, :], hT[:, k, :], start=(k == 0), stop=(k == C - 1))
                    last.then_inc(product[b], 1)
                if turn:
                    for b in range(2):
                        pe.wait_ge(x_ready[b], i + 2)
                        pe.wait_ge(moved[b], i + 1)
                        pe.matmul(pr[b][:], rot[:], xs[:, b], start=True, stop=True).then_inc(rotated[b], 1)

        @block.scalar
        def _(act):
            if turn:
                angle_tables(act, None, None, pos, ang, cos, sin, inv, pos_in, angle, tables)
                act.sem_inc(x_ready[0], 1)
                act.sem_inc(x_ready[1], 1)
            else:
                act.sem_inc(moved[0], 1)
            with act.Fori(0, n // 2) as i:
                for b in (0, 1) if turn else (0,):
                    act.wait_ge(product[b], i + 2)
                    if turn:
                        act.wait_ge(moved[b], i + 1)
                        act.activation(xs[:, b], pa[b][:], ACT.Copy).then_inc(x_ready[b], 1)
                    else:
                        act.activation(dst[:, ds(2 * i, 1), :], pa[0][:].rearrange("p (o n) -> p o n", o=1), ACT.Copy).then_inc(moved[0], 1)

        @block.vector
        def _(dve):
            step = Steps(dve, order)
            if turn:
                dve.wait_ge(pos_in, 48)
                angle_tables(None, dve, step, pos, ang, cos, sin, inv, pos_in, angle, tables)
                dve.wait_ge(tables, 2)
                dve.sem_inc(moved[0], 1)
            dve.sem_inc(moved[1], 1)
            with dve.Fori(0, n // 2) as i:
                step.restart()
                if turn:
                    for b in range(2):
                        dve.wait_ge(x_ready[b], i + 2)
                        dve.tensor_tensor(tmp[:, b, 0], xs[:, b], cos[:], ALU.mult)
                        dve.wait_ge(rotated[b], i + 1)
                        step(dve.tensor_tensor(tmp[:, b, 1], pr[b][:], sin[:], ALU.mult))
                        dve.tensor_tensor(dst[:, ds(2 * i + b, 1), :], tmp[:, b, 0:1], tmp[:, b, 1:2], ALU.add).then_inc(moved[b], 1)
                else:
                    dve.wait_ge(product[1], i + 2)
                    dve.tensor_copy(dst[:, ds(2 * i + 1, 1), :], pa[1][:].rearrange("p (o n) -> p o n", o=1)).then_inc(moved[1], 1)


def rows_phase(nc, g, hT, cols, dst):
    w_dram = g["w_in_2"][0].rearrange("(p k) n -> p k n", p=P)
    with Phase(nc) as ph:
        w = ph.sb("w", [P, 2, C, 512])
        pa = [ph.ps(f"pa{b}", [P, 512]) for b in range(2)]
        w_in, product, moved = (ph.sems(k) for k in ("w_in", "product", "moved"))
        block = ph.block()

        @block.sync
        def _(sp):
            ph.clear_other_pool(sp)
            for i, col in enumerate(cols):
                if i >= 2:
                    sp.wait_ge(product[1], 2 * (i - 1))
                sp.dma_start(w[:, i % 2], w_dram[:, :, col:col + 512]).then_inc(w_in[i % 2], 16)

        @block.tensor
        def _(pe):
            for i in range(len(cols)):
                pe.wait_ge(w_in[i % 2], 16 * (i // 2 + 1))
                for t in range(NLAT):
                    if 4 * i + t >= 2:
                        pe.wait_ge(moved[t % 2], (4 * i + t) // 2)
                    for k in range(C):
                        last = pe.matmul(pa[t % 2][:], hT[:, k, t * P:(t + 1) * P], w[:, i % 2, k, :], start=(k == 0), stop=(k == C - 1))
                    last.then_inc(product[t % 2], 1)

        @block.scalar
        def _(act):
            for n in range(2 * len(cols)):
                act.wait_ge(product[0], n + 1)
                act.activation(dst[:, 2 * n % 4, n // 2, :], pa[0][:], ACT.Copy).then_inc(moved[0], 1)

        @block.vector
        def _(dve):
            for n in range(2 * len(cols)):
                dve.wait_ge(product[1], n + 1)
                dve.tensor_copy(dst[:, (2 * n + 1) % 4, n // 2, :], pa[1][:]).then_inc(moved[1], 1)


def gla_phase(nc, g, hT, G, vrow, yT):
    BM = P // GCH
    with Phase(nc) as ph:
        wa = ph.sb("wa", [P, C, GLA_A])
        wu = ph.sb("wu", [GLA_A, 2, P])
        ba = ph.sb("ba", [P, 2])
        al = ph.sb("al", [GLA_A, LAT])
        keep, member = ph.sb("keep", [P, LAT]), ph.sb("member", [P, BM])
        ones = ph.sb("ones", [P, P])
        gn = ph.sb("gn", [P, 1])
        eps = ph.sb("eps", [P, 1])
        lc = ph.sb("lc", [P, 2, LAT])
        u = ph.sb("u", [P, 2, LAT])
        rel = ph.sb("rel", [P, 2, 2, LAT])
        m = ph.sb("m", [P, 2, 2, LAT])
        qi = ph.sb("qi", [P, 2, LAT])
        ki = ph.sb("ki", [P, 2, LAT])
        kr = ph.sb("kr", [P, NLAT, 2, P])
        dn = ph.sb("dn", [P, 2, NCH])
        vm = ph.sb("vm", [P, 2, BM, P])
        S = ph.sb("S", [P, 2, NCH, P])
        pv = ph.sb("pv", [P, 2, LAT])
        pA = ph.ps("pA", [P, 4, 512])
        pB = ph.ps("pB", [P, 4, 512])
        names = ("const_in", "a_low", "a_moved", "raised", "logs", "cum", "exped", "inputs", "k_turned", "k_moved", "vm_ready",
                 "kv", "kv_moved", "states", "inter", "inter_out", "rel_ready", "rel_exp", "m_ready", "s_done", "s_used",
                 "squares", "means", "roots", "silus", "order", "order_a")
        s = {k: ph.sem(k) for k in names}
        block = ph.block()
        qT, kT, vT, gT = G[:, 0:2], G[:, 2:4], G[:, 4:8], G[:, 8:12]
        o = yT[:, 0:4]

        def by_chunk(ap):
            return ap.rearrange("p (c i) -> p c i", i=GCH)

        @block.sync
        def _(sp):
            ph.clear_other_pool(sp)
            a0 = 2 * GLA_Q + 2 * GLA_V
            sp.dma_start(wa[:], g["w_in_2"][0].rearrange("(p k) n -> p k n", p=P)[:, :, a0:a0 + GLA_A]).then_inc(s["const_in"], 16)
            sp.dma_start(wu[:].rearrange("a c n -> a (c n)"), g["w_alpha_up_2"][0]).then_inc(s["const_in"], 16)
            for c in range(2):
                sp.dma_start(ba[:, c:c + 1], g["b_alpha_2"][0, c * P:(c + 1) * P].rearrange("(p o) -> p o", o=1)).then_inc(s["const_in"], 16)
            sp.dma_start(keep[:], g["chunk_keep"]).then_inc(s["const_in"], 16)
            sp.dma_start(member[:], g["member"]).then_inc(s["const_in"], 16)
            sp.dma_start(ones[:], g["ones"]).then_inc(s["const_in"], 16)
            sp.dma_start(gn[:], g["gla_norm_g_2"].rearrange("o p -> p o")).then_inc(s["const_in"], 16)
            sp.wait_ge(s["const_in"], 128)

        @block.gpsimd
        def _(pool):
            pool.wait_ge(s["const_in"], 128)
            for i in range(NLAT * GH):
                t, h = i // GH, i % GH
                if i >= 2:
                    pool.wait_ge(s["kv"], i - 1)
                pool.tensor_tensor(vm[:, i % 2], vrow[:, t, 0, h * P:(h + 1) * P].rearrange("p (o e) -> p o e", o=1).broadcast_to([P, BM, P]),
                                   member[:].rearrange("p (c o) -> p c o", o=1).broadcast_to([P, BM, P]), ALU.mult).then_inc(s["vm_ready"], 1)

        @block.tensor
        def _(pe):
            pe.wait_ge(s["const_in"], 128)
            for k in range(C):
                last = pe.matmul(pA[0:GLA_A, 0, :], wa[:, k, :], hT[:, k, :], start=(k == 0), stop=(k == C - 1))
            last.then_inc(s["a_low"], 1)
            pe.wait_ge(s["a_moved"], 1)
            for c in range(2):
                last = pe.matmul(pA[:, 1 + c, :], wu[:, c, :], al[:], start=True, stop=True)
            last.then_inc(s["raised"], 1)
            pe.wait_ge(s["inputs"], 1)
            for t in range(NLAT):
                if t:
                    pe.wait_ge(s["k_moved"], t)
                for c in range(2):
                    last = pe.transpose(pA[:, 0, c * P:(c + 1) * P], ki[:, c, t * P:(t + 1) * P], g["ident"][:])
                last.then_inc(s["k_turned"], 1)
            pe.wait_ge(s["k_moved"], NLAT)
            for i in range(NLAT * GH):
                t, h = i // GH, i % GH
                pe.wait_ge(s["vm_ready"], i + 1)
                if i >= 2:
                    pe.wait_ge(s["kv_moved"], i - 1)
                for half in range(2):
                    last = pe.matmul(pB[:, 2 * (i % 2) + half, :], kr[:, t, h // 2, :], vm[:, i % 2, half * 4:half * 4 + 4].rearrange("p c e -> p (c e)"),
                                     start=True, stop=True)
                last.then_inc(s["kv"], 1)
            pe.wait_ge(s["states"], NCH)
            for h in range(GH):
                rows = slice((h % 2) * 64, (h % 2) * 64 + 64)
                for n in range(1, NCH):
                    last = pe.matmul(pA[:, h, n * GCH:(n + 1) * GCH], S[rows, h // 2, n - 1, :], qi[rows, h // 2, n * GCH:(n + 1) * GCH],
                                     start=True, stop=True)
            last.then_inc(s["inter"], 1)
            pe.wait_ge(s["inter_out"], 1)
            for d in range(GCH):
                w = NCH * (GCH - d)
                pe.wait_ge(s["m_ready"], d + 1)
                for h in range(GH):
                    if d:
                        pe.wait_ge(s["s_used"], 4 * (d - 1) + h + 1)
                    rows = slice((h % 2) * 64, (h % 2) * 64 + 64)
                    pe.matmul(pB[:, h, 0:w], ones[rows, :], m[rows, d % 2, h // 2, 0:w], start=True, stop=True).then_inc(s["s_done"], 1)
            pe.wait_ge(s["squares"], 1)
            for h in range(GH):
                last = pe.matmul(pA[:, h, :], ones[:], S[:, 0].rearrange("p n e -> p (n e)")[:, h * 512:(h + 1) * 512], start=True, stop=True)
            last.then_inc(s["means"], 1)

        @block.scalar
        def _(act):
            step = Steps(act, s["order_a"])
            act.wait_ge(s["a_low"], 1)
            act.activation(al[:], pA[0:GLA_A, 0, :], ACT.Copy).then_inc(s["a_moved"], 1)
            act.wait_ge(s["logs"], 1)
            step(act.activation(u[:], u[:], ACT.Exp, scale=-1.0))
            act.activation(u[:], u[:], ACT.Ln, bias=1.0).then_inc(s["logs"], 1)
            act.wait_ge(s["cum"], 1)
            act.activation(qi[:], lc[:], ACT.Exp)
            act.activation(ki[:], u[:], ACT.Exp)
            act.activation(dn[:], lc[:].rearrange("p a (c i) -> p a c i", i=GCH)[:, :, :, GCH - 1], ACT.Exp).then_inc(s["exped"], 1)
            for t in range(NLAT):
                act.wait_ge(s["k_turned"], t + 1)
                act.activation(kr[:, t].rearrange("p c e -> p (c e)"), pA[:, 0, 0:2 * P], ACT.Copy).then_inc(s["k_moved"], 1)
            for i in range(NLAT * GH):
                t, h = i // GH, i % GH
                rows = slice((h % 2) * 64, (h % 2) * 64 + 64)
                act.wait_ge(s["kv"], i + 1)
                for half in range(2):
                    c0 = t * BM + half * 4
                    last = act.activation(S[rows, h // 2, c0:c0 + 4, :].rearrange("p c e -> p (c e)"), pB[rows, 2 * (i % 2) + half, :], ACT.Copy)
                last.then_inc(s["kv_moved"], 1)
            for d in range(1, GCH):
                w = NCH * (GCH - d)
                act.wait_ge(s["rel_ready"], d)
                act.activation(rel[:, d % 2, :, 0:w], rel[:, d % 2, :, 0:w], ACT.Exp).then_inc(s["rel_exp"], 1)
            act.wait_ge(s["means"], 1)
            for h in range(GH):
                last = act.activation(S[:, 0].rearrange("p n e -> p (n e)")[:, h * 512:(h + 1) * 512], pA[:, h, :], ACT.Sqrt, scale=1.0 / P, bias=eps[:])
            last.then_inc(s["roots"], 1)
            act.activation(gT[:], gT[:], ACT.Silu).then_inc(s["silus"], 1)

        @block.vector
        def _(dve):
            step = Steps(dve, s["order"])
            step(dve.memset(eps[:], EPS2))
            dve.wait_ge(s["const_in"], 128)
            dve.wait_ge(s["raised"], 1)
            for c in range(2):
                step(dve.tensor_scalar(lc[:, c], pA[:, 1 + c, :], ba[:, c:c + 1], None, ALU.add))
            dve.scalar_tensor_tensor(out=u[:], in0=lc[:], scalar=-1.0, in1=lc[:], op0=ALU.mult, op1=ALU.max).then_inc(s["logs"], 1)
            step(dve.tensor_scalar(lc[:], lc[:], 0.0, None, ALU.min))
            dve.wait_ge(s["logs"], 2)
            step(dve.tensor_tensor(lc[:], lc[:], u[:], ALU.subtract))
            step(dve.tensor_scalar(u[:], lc[:], 1.0 / 16.0, None, ALU.mult))
            for c in range(2):
                step(dve.tensor_tensor_scan(lc[:, c], keep[:], u[:, c], 0.0, ALU.mult, ALU.add))
            for c in range(2):
                x = by_chunk(lc[:, c])
                last = dve.tensor_tensor(by_chunk(u[:, c]), x[:, :, GCH - 1:GCH].broadcast_to([P, NCH, GCH]), x, ALU.subtract)
            last.then_inc(s["cum"], 1)
            step(dve.tensor_scalar(qT[:], qT[:], 64.0 ** -0.5, None, ALU.mult))
            dve.wait_ge(s["exped"], 1)
            dve.tensor_tensor(qi[:], qi[:], qT[:], ALU.mult)
            dve.tensor_tensor(ki[:], ki[:], kT[:], ALU.mult).then_inc(s["inputs"], 1)
            dve.wait_ge(s["kv_moved"], NLAT * GH)
            dve.sem_inc(s["states"], 1)
            for n in range(1, NCH):
                for c in range(2):
                    last = dve.scalar_tensor_tensor(out=S[:, c, n, :], in0=S[:, c, n - 1, :], scalar=dn[:, c, n:n + 1], in1=S[:, c, n, :],
                                                    op0=ALU.mult, op1=ALU.add)
                last.then_inc(s["states"], 1)
                dve.wait_ge(s["states"], n + 1)

            def weights(d):
                n = GCH - d
                for c in range(2):
                    x = by_chunk(lc[:, c])
                    if d:
                        last = dve.tensor_tensor(rel[:, d % 2, c, 0:NCH * n].rearrange("p (c i) -> p c i", i=n), x[:, :, d:GCH], x[:, :, 0:n], ALU.subtract)
                if d:
                    last.then_inc(s["rel_ready"], 1)
                for c in range(2):
                    md = m[:, d % 2, c, 0:NCH * n].rearrange("p (c i) -> p c i", i=n)
                    last = dve.tensor_tensor(md, by_chunk(qT[:, c])[:, :, d:GCH], by_chunk(kT[:, c])[:, :, 0:n], ALU.mult)
                if not d:
                    last.then_inc(s["m_ready"], 1)
                    return
                step(last)
                dve.wait_ge(s["rel_exp"], d)
                md = m[:, d % 2, :, 0:NCH * n]
                dve.tensor_tensor(md, md, rel[:, d % 2, :, 0:NCH * n], ALU.mult).then_inc(s["m_ready"], 1)

            weights(0)
            dve.wait_ge(s["inter"], 1)
            step(dve.memset(o[:, :, 0:GCH], 0.0))
            for h in range(GH):
                last = dve.tensor_copy(o[:, h, GCH:LAT], pA[:, h, GCH:LAT])
            last.then_inc(s["inter_out"], 1)
            dve.wait_ge(s["inter_out"], 1)
            for d in range(GCH):
                if d < GCH - 1:
                    if d:
                        dve.wait_ge(s["s_done"], 4 * d)
                    weights(d + 1)
                n = GCH - d
                for h in range(GH):
                    dve.wait_ge(s["s_done"], 4 * d + h + 1)
                    pvh = pv[:, h % 2, 0:NCH * n].rearrange("p (c i) -> p c i", i=n)
                    dve.tensor_tensor(pvh, pB[:, h, 0:NCH * n].rearrange("p (c i) -> p c i", i=n), by_chunk(vT[:, h])[:, :, 0:n], ALU.mult).then_inc(s["s_used"], 1)
                    dve.wait_ge(s["s_used"], 4 * d + h + 1)
                    oh = by_chunk(o[:, h])[:, :, d:GCH]
                    step(dve.tensor_tensor(oh, oh, pvh, ALU.add))
            sq = S[:, 0].rearrange("p n e -> p (n e)")[:, 0:2048].rearrange("p (h t) -> p h t", h=GH)
            dve.tensor_tensor(sq, o[:], o[:], ALU.mult).then_inc(s["squares"], 1)
            dve.wait_ge(s["roots"], 1)
            step(dve.reciprocal(sq, sq))
            step(dve.scalar_tensor_tensor(out=o[:], in0=o[:], scalar=gn[:], in1=sq, op0=ALU.mult, op1=ALU.mult))
            dve.wait_ge(s["silus"], 1)
            step(dve.tensor_tensor(o[:], o[:], gT[:], ALU.mult))


def short_conv_phase(nc, g, Z, yT):
    with Phase(nc) as ph:
        w = ph.sb("w", [P, 3, 4])
        acc = ph.sb("acc", [P, 4, LAT])
        w_in, order = ph.sem("w_in"), ph.sem("order")
        block = ph.block()

        @block.sync
        def _(sp):
            ph.clear_other_pool(sp)
            for j in range(3):
                sp.dma_start(w[:, j, :], g["sc_conv_w_2"][0, j, :].rearrange("(k p) -> p k", p=P), allow_slow_non_contiguous=True).then_inc(w_in, 16)

        @block.vector
        def _(dve):
            step = Steps(dve, order)
            b, c, x = Z[:, 0:4], Z[:, 4:8], Z[:, 8:12]
            dve.wait_ge(w_in, 48)
            step(dve.tensor_tensor(x, c, x, ALU.mult))
            for k in range(4):
                step(dve.tensor_scalar(acc[:, k], x[:, k], w[:, 2, k:k + 1], None, ALU.mult))
                for j in (1, 2):
                    step(dve.scalar_tensor_tensor(out=acc[:, k, j:], in0=x[:, k, 0:LAT - j], scalar=w[:, 2 - j, k:k + 1],
                                                  in1=acc[:, k, j:], op0=ALU.mult, op1=ALU.add))
            step(dve.tensor_tensor(yT[:, 4:8], acc[:], b, ALU.mult))


def dilated_phase(nc, g, QK, vrow, yT):
    H, S3 = 4, 3
    DSC = 128.0 ** -0.5

    def keys(t):
        return [(s, k) for s in range(S3) for k in range(max(0, t - 1) if s == 0 else 0, t + 1)]

    KMAX = max(len(keys(t)) for t in range(NLAT))
    RND = sum((len(keys(t)) + 3) // 4 for t in range(NLAT))
    with Phase(nc) as ph:
        mask = ph.sb("mask", [P, S3, NLAT, LAT])
        q2 = ph.sb("q2", [P, S3, LAT])
        E = ph.sb("E", [P, 2, KMAX * P])
        PT = ph.sb("PT", [P, 2, 512])
        o = ph.sb("o", [P, NLAT, 512])
        st = ph.sb("st", [P, 2, 4])
        pS = [ph.ps(f"pS{i}", [P, 512]) for i in range(3)]
        pT = [ph.ps(f"pT{i}", [P, 512]) for i in range(2)]
        pO = [ph.ps(f"pO{i}", [P, P]) for i in range(2)]
        names = ("mask_in", "q_ready", "scored", "s_used", "shifted", "e_ready", "r_ready", "turned", "moved", "pv", "o_out", "last_turned", "last_moved", "order", "o_all")
        s = {k: ph.sem(k) for k in names}
        block = ph.block()

        def segments(t):
            out, at = [], 0
            for st_ in range(S3):
                k0 = max(0, t - 1) if st_ == 0 else 0
                out.append((st_, k0, t + 1 - k0, at))
                at += t + 1 - k0
            return out

        def rounds():
            return [(t, i, min(4, len(keys(t)) - i)) for t in range(NLAT) for i in range(0, len(keys(t)), 4)]

        @block.sync
        def _(sp):
            ph.clear_other_pool(sp)
            for i in range(S3):
                sp.dma_start(mask[:, i], g["dil_mask"][i].rearrange("(t p) n -> p t n", p=P)).then_inc(s["mask_in"], 16)

        @block.gpsimd
        def _(pool):
            with pool.Fori(0, H) as h:
                pool.wait_ge(s["o_all"], h + 1)
                for i in range(S3):
                    last = pool.tensor_copy(q2[:, i:i + 1], QK[:, ds(h + 4 * i, 1), :])
                last.then_inc(s["q_ready"], 1)

        @block.tensor
        def _(pe):
            def score(h, t):
                for i, (st_, k0, n, at) in enumerate(segments(t)):
                    pe.wait_ge(s["s_used"], 12 * h + 3 * t + i + 1)
                    pe.matmul(pS[i][:, 0:n * P], q2[:, st_, t * P:(t + 1) * P],
                              QK[:, ds(h + (12 + 4 * st_), 1), k0 * P:(k0 + n) * P].rearrange("p o n -> p (o n)"),
                              start=True, stop=True).then_inc(s["scored"], 1)

            with pe.Fori(0, H) as h:
                pe.wait_ge(s["q_ready"], h + 1)
                score(h, 0)
                for r, (t, i0, n) in enumerate(rounds()):
                    if i0 == 0:
                        pe.wait_ge(s["e_ready"], NLAT * h + t + 1)
                    pe.wait_ge(s["moved"], RND * h + r + 1)
                    for j in range(n):
                        last = pe.transpose(pT[r % 2][:, j * P:(j + 1) * P], E[:, t % 2, (i0 + j) * P:(i0 + j + 1) * P], g["ident"][:])
                    last.then_inc(s["turned"], 1)
                    if i0 == 0 and t < NLAT - 1:
                        score(h, t + 1)
                    pe.wait_ge(s["moved"], RND * h + r + 2)
                    if i0 == 0:
                        pe.wait_ge(s["o_out"], NLAT * h + t + 1)
                    nk = len(keys(t))
                    for j in range(n):
                        st_, k = keys(t)[i0 + j]
                        last = pe.matmul(pO[t % 2][:], PT[:, r % 2, j * P:(j + 1) * P],
                                         vrow[:, k, st_, ds(h * P, P)],
                                         start=(i0 + j == 0), stop=(i0 + j == nk - 1))
                    if i0 + n == nk:
                        last.then_inc(s["pv"], 1)
            pe.wait_ge(s["o_out"], NLAT * H + 1)
            for t in range(NLAT):
                if t >= 2:
                    pe.wait_ge(s["last_moved"], t - 1)
                for c in range(4):
                    last = pe.transpose(pT[t % 2][:, c * P:(c + 1) * P], o[:, t, c * P:(c + 1) * P], g["ident"][:])
                last.then_inc(s["last_turned"], 1)

        @block.scalar
        def _(act):
            act.sem_inc(s["moved"], 1)
            act.sem_inc(s["o_out"], 1)
            act.sem_inc(s["o_all"], 1)
            with act.Fori(0, H) as h:
                def exp(t):
                    n = len(keys(t)) * P
                    act.wait_ge(s["shifted"], NLAT * h + t + 1)
                    act.activation(E[:, t % 2, 0:n], E[:, t % 2, 0:n], ACT.Exp, bias=st[:, t % 2, 1:2],
                                   accum_out=st[:, t % 2, 2:3]).then_inc(s["e_ready"], 1)

                exp(0)
                for r, (t, i0, n) in enumerate(rounds()):
                    act.wait_ge(s["turned"], RND * h + r + 1)
                    act.activation(PT[:, r % 2, 0:n * P], pT[r % 2][:, 0:n * P], ACT.Copy).then_inc(s["moved"], 1)
                    if i0 + n == len(keys(t)):
                        if t < NLAT - 1:
                            exp(t + 1)
                        act.wait_ge(s["pv"], NLAT * h + t + 1)
                        act.wait_ge(s["r_ready"], NLAT * h + t + 1)
                        act.activation(o[:, t, ds(h * P, P)], pO[t % 2][:], ACT.Copy, scale=st[:, t % 2, 3:4]).then_inc(s["o_out"], 1)
                act.sem_inc(s["o_all"], 1)
            for t in range(NLAT):
                act.wait_ge(s["last_turned"], t + 1)
                act.activation(yT[:, 8:12, t * P:(t + 1) * P], pT[t % 2][:].rearrange("p (c n) -> p c n", c=4), ACT.Copy).then_inc(s["last_moved"], 1)

        @block.vector
        def _(dve):
            step = Steps(dve, s["order"])
            dve.sem_inc(s["s_used"], 3)
            dve.wait_ge(s["mask_in"], 48)
            with dve.Fori(0, H) as h:
                step.restart()

                def shift(t):
                    for i, (st_, k0, n, at) in enumerate(segments(t)):
                        dve.wait_ge(s["scored"], 12 * h + 3 * t + i + 1)
                        last = dve.scalar_tensor_tensor(out=E[:, t % 2, at * P:(at + n) * P], in0=pS[i][:, 0:n * P], scalar=DSC,
                                                        in1=mask[:, st_, t, k0 * P:(k0 + n) * P], op0=ALU.mult, op1=ALU.add)
                        last.then_inc(s["s_used"], 1)
                    dve.wait_ge(s["s_used"], 12 * h + 3 * t + 6)
                    step(dve.tensor_reduce(st[:, t % 2, 0:1], E[:, t % 2, 0:len(keys(t)) * P], AX.X, ALU.max))
                    dve.tensor_scalar(st[:, t % 2, 1:2], st[:, t % 2, 0:1], -1.0, None, ALU.mult).then_inc(s["shifted"], 1)

                shift(0)
                for t in range(NLAT):
                    dve.wait_ge(s["e_ready"], NLAT * h + t + 1)
                    dve.reciprocal(st[:, t % 2, 3:4], st[:, t % 2, 2:3]).then_inc(s["r_ready"], 1)
                    if t < NLAT - 1:
                        shift(t + 1)


D_FF = 2816
NF = D_FF // P


def merge_phase(nc, g, hT, yT, merged):
    wg_dram = g["w_gate_2"][0].rearrange("(p k) n -> p k n", p=P)
    with Phase(nc) as ph:
        wg = ph.sb("wg", [P, 2, C, 512])
        wb = ph.sb("wb", [P, 2, 4, 512])
        bias = ph.sb("bias", [P, 2, 512])
        z = ph.sb("z", [P, 2, 512])
        y = ph.sb("y", [P, 4, LAT])
        pG = [ph.ps(f"pG{i}", [P, 512]) for i in range(2)]
        pY = [ph.ps(f"pY{i}", [P, 512]) for i in range(2)]
        w_in, used, gate_done, branch_done, logit, gate, taken = (
            ph.sems(k) for k in ("w_in", "used", "gate_done", "branch_done", "logit", "gate", "taken"))
        y_ready, order = ph.sem("y_ready"), ph.sem("order")
        block = ph.block()

        @block.sync
        def _(sp):
            ph.clear_other_pool(sp)
            with sp.Fori(0, 3) as i:
                for b in range(2):
                    sp.wait_ge(used[b], i + 1)
                    sp.dma_start(wg[:, b], wg_dram[:, :, ds(i * D + b * 512, 512)]).then_inc(w_in[b], 16)
                    sp.dma_start(wb[:, b], g["w_branch_2"][0, ds(i, 1)].rearrange("o (k p) n -> p (o k) n", p=P)[:, :, b * 512:(b + 1) * 512]).then_inc(w_in[b], 16)
                    sp.dma_start(bias[:, b], g["b_gate_2"][:, ds(i * D + b * 512, 512)].broadcast_to([P, 512])).then_inc(w_in[b], 16)

        @block.gpsimd
        def _(pool):
            with pool.Fori(0, 3) as i:
                pool.wait_ge(used[1], i + 1)
                pool.tensor_copy(y[:], yT[:, ds(4 * i, 4), :]).then_inc(y_ready, 1)

        @block.tensor
        def _(pe):
            with pe.Fori(0, 3) as i:
                pe.wait_ge(y_ready, i + 1)
                for b in range(2):
                    pe.wait_ge(w_in[b], 48 * (i + 1))
                    for t in range(NLAT):
                        q, n = t % 2, 4 * i + 2 * b + t // 2
                        pe.wait_ge(taken[q], n + 1)
                        for k in range(C):
                            last = pe.matmul(pG[q][:], hT[:, k, t * P:(t + 1) * P], wg[:, b, k, :], start=(k == 0), stop=(k == C - 1))
                        last.then_inc(gate_done[q], 1)
                        for k in range(4):
                            last = pe.matmul(pY[q][:], y[:, k, t * P:(t + 1) * P], wb[:, b, k, :], start=(k == 0), stop=(k == 3))
                        last.then_inc(branch_done[q], 1)

        @block.scalar
        def _(act):
            with act.Fori(0, 3) as i:
                for b in range(2):
                    for t in range(NLAT):
                        q, n = t % 2, 4 * i + 2 * b + t // 2
                        act.wait_ge(logit[q], n + 1)
                        act.activation(z[:, q], z[:, q], ACT.Sigmoid).then_inc(gate[q], 1)

        @block.vector
        def _(dve):
            step = Steps(dve, order)
            for b in range(2):
                dve.sem_inc(used[b], 1)
                dve.sem_inc(taken[b], 1)
            step(dve.memset(merged[:], 0.0))
            with dve.Fori(0, 3) as i:
                step.restart()
                for b in range(2):
                    dve.wait_ge(w_in[b], 48 * (i + 1))
                    for t in range(NLAT):
                        q, n = t % 2, 4 * i + 2 * b + t // 2
                        dve.wait_ge(gate_done[q], n + 1)
                        dve.tensor_tensor(z[:, q], pG[q][:], bias[:, b], ALU.add).then_inc(logit[q], 1)
                        dve.wait_ge(gate[q], n + 1)
                        dve.wait_ge(branch_done[q], n + 1)
                        dve.tensor_tensor(z[:, q], z[:, q], pY[q][:], ALU.mult).then_inc(taken[q], 1)
                        dve.wait_ge(taken[q], n + 2)
                        mt = merged[:, t, b * 512:(b + 1) * 512]
                        step(dve.tensor_tensor(mt, mt, z[:, q], ALU.add))
                    dve.sem_inc(used[b], 1)


def mix_out_phase(nc, g, merged, hT):
    with Phase(nc) as ph:
        w = ph.sb("w", [P, C, D])
        mT = ph.sb("mT", [P, C, P])
        x = ph.sb("x", [P, 2, D])
        r = ph.sb("r", [P, D])
        grow = ph.sb("grow", [P, D])
        gcol = ph.sb("gcol", [P, C])
        ss = ph.sb("ss", [P, 4])
        eps = ph.sb("eps", [P, 1])
        pT = ph.ps("pT", [P, 1024])
        pM = ph.ps("pM", [P, 1024])
        names = ("const_in", "w_in", "turned", "movedA", "movedD", "mixed", "squared", "rooted", "x_ready", "scaled", "order", "order_a")
        s = {k: ph.sem(k) for k in names}
        x_in, stored = ph.sems("x_in"), ph.sems("stored")
        block = ph.block()

        @block.sync
        def _(sp):
            ph.clear_other_pool(sp)
            sp.dma_start(w[:], g["w_mix_out_2"][0].rearrange("(p k) n -> p k n", p=P)).then_inc(s["w_in"], 16)
            sp.dma_start(grow[:], g["post_mix_g_2"].broadcast_to([P, D])).then_inc(s["const_in"], 16)
            sp.dma_start(gcol[:], g["pre_ffn_g_2"][0].rearrange("(p k) -> p k", p=P)).then_inc(s["const_in"], 16)
            for t in range(NLAT):
                if t >= 2:
                    sp.wait_ge(s["turned"], 2 * (t - 1))
                    sp.wait_ge(stored[t % 2], 16)
                sp.dma_start(x[:, t % 2], g["h"][t * P:(t + 1) * P, :]).then_inc(x_in[t % 2], 16)
                sp.wait_ge(s["x_ready"], t + 1)
                sp.dma_start(g["x_mid"][t * P:(t + 1) * P, :], x[:, t % 2]).then_inc(stored[t % 2], 16)
            for b in range(2):
                sp.wait_ge(stored[b], 32)

        @block.tensor
        def _(pe):
            pe.wait_ge(s["w_in"], 16)
            for t in range(NLAT):
                if t:
                    pe.wait_ge(s["movedA"], 2 * t)
                    pe.wait_ge(s["movedD"], 2 * t)
                for k in range(C):
                    last = pe.transpose(pT[:, k * P:(k + 1) * P], merged[:, t, k::C], g["ident"][:])
                last.then_inc(s["turned"], 1)
                pe.wait_ge(s["movedA"], 2 * t + 1)
                pe.wait_ge(s["movedD"], 2 * t + 1)
                for b in range(2):
                    for k in range(C):
                        last = pe.matmul(pM[:, b * 512:(b + 1) * 512], mT[:, k, :], w[:, k, b * 512:(b + 1) * 512], start=(k == 0), stop=(k == C - 1))
                last.then_inc(s["mixed"], 1)
                pe.wait_ge(s["scaled"], t + 1)
                for k in range(C):
                    last = pe.transpose(pT[:, k * P:(k + 1) * P], r[:, k::C], g["ident"][:])
                last.then_inc(s["turned"], 1)

        @block.scalar
        def _(act):
            step = Steps(act, s["order_a"])
            for t in range(NLAT):
                act.wait_ge(s["turned"], 2 * t + 1)
                act.activation(mT[:, 0:4].rearrange("p k n -> p (k n)"), pT[:, 0:512], ACT.Copy).then_inc(s["movedA"], 1)
                act.wait_ge(s["mixed"], t + 1)
                act.wait_ge(s["movedD"], 2 * t + 1)
                for i in range(2):
                    if i:
                        act.wait_ge(s["x_ready"], t + 1)
                    step(act.activation(r[:], pM[:, :] if i == 0 else x[:, t % 2], ACT.Square, accum_out=ss[:, 0:1]))
                    act.activation(ss[:, 1:2], ss[:, 0:1], ACT.Sqrt, scale=1.0 / D, bias=eps[:]).then_inc(s["rooted"], 1)
                act.wait_ge(s["turned"], 2 * t + 2)
                for k in range(4):
                    last = act.activation(hT[:, k, t * P:(t + 1) * P], pT[:, k * P:(k + 1) * P], ACT.Copy, scale=gcol[:, k:k + 1])
                last.then_inc(s["movedA"], 1)

        @block.vector
        def _(dve):
            step = Steps(dve, s["order"])
            step(dve.memset(eps[:], EPS2))
            dve.wait_ge(s["const_in"], 32)
            for t in range(NLAT):
                dve.wait_ge(s["turned"], 2 * t + 1)
                dve.tensor_copy(mT[:, 4:8].rearrange("p k n -> p (k n)"), pT[:, 512:1024]).then_inc(s["movedD"], 1)
                dve.wait_ge(s["rooted"], 2 * t + 1)
                step(dve.reciprocal(ss[:, 2:3], ss[:, 1:2]))
                step(dve.scalar_tensor_tensor(out=r[:], in0=pM[:, :], scalar=ss[:, 2:3], in1=grow[:], op0=ALU.mult, op1=ALU.mult))
                dve.wait_ge(x_in[t % 2], 16 * (t // 2 + 1))
                dve.tensor_tensor(x[:, t % 2], x[:, t % 2], r[:], ALU.add).then_inc(s["x_ready"], 1)
                dve.wait_ge(s["rooted"], 2 * t + 2)
                step(dve.reciprocal(ss[:, 3:4], ss[:, 1:2]))
                dve.tensor_scalar(r[:], x[:, t % 2], ss[:, 3:4], None, ALU.mult).then_inc(s["scaled"], 1)
                dve.wait_ge(s["turned"], 2 * t + 2)
                for k in range(4, C):
                    last = dve.tensor_scalar(hT[:, k, t * P:(t + 1) * P], pT[:, k * P:(k + 1) * P], gcol[:, k:k + 1], None, ALU.mult)
                last.then_inc(s["movedD"], 1)


def feed_forward_up_phase(nc, g, hT, aT):
    with Phase(nc) as ph:
        wt = ph.sb("wt", [P, 2, 2, C, P])
        cw = ph.sb("cw", [P, 4, NF])
        x = ph.sb("x", [P, 2, LAT])
        pG = [ph.ps(f"pG{i}", [P, 512]) for i in range(2)]
        pU = [ph.ps(f"pU{i}", [P, 512]) for i in range(2)]
        conv_in, order = ph.sem("conv_in"), ph.sem("order")
        w_in, product, started, summed, gelu, done = (ph.sems(k) for k in ("w_in", "product", "started", "summed", "gelu", "done"))
        block = ph.block()

        @block.sync
        def _(sp):
            ph.clear_other_pool(sp)
            for j in range(3):
                sp.dma_start(cw[:, j], g["ff_conv_w_2"][0, j].rearrange("(k p) -> p k", p=P), allow_slow_non_contiguous=True).then_inc(conv_in, 16)
            sp.dma_start(cw[:, 3], g["ff_conv_b_2"][0].rearrange("(k p) -> p k", p=P), allow_slow_non_contiguous=True).then_inc(conv_in, 16)
            with sp.Fori(0, NF // 2) as i:
                for b in range(2):
                    sp.wait_ge(product[b], i + 1)
                    for j, name in enumerate(("w_ff_gate_2", "w_ff_up_2")):
                        sp.dma_start(wt[:, b, j], g[name][0].rearrange("(p k) n -> p k n", p=P)[:, :, ds(i * 2 * P + b * P, P)]).then_inc(w_in[b], 16)

        @block.tensor
        def _(pe):
            for b in range(2):
                pe.sem_inc(product[b], 1)
            with pe.Fori(0, NF // 2) as i:
                for b in range(2):
                    pe.wait_ge(w_in[b], 32 * (i + 1))
                    pe.wait_ge(done[b], i + 1)
                    for j, p in enumerate((pG, pU)):
                        for k in range(C):
                            last = pe.matmul(p[b][:], wt[:, b, j, k, :], hT[:, k, :], start=(k == 0), stop=(k == C - 1))
                    last.then_inc(product[b], 1)

        @block.scalar
        def _(act):
            act.wait_ge(conv_in, 64)
            with act.Fori(0, NF // 2) as i:
                for b in range(2):
                    act.wait_ge(product[b], i + 2)
                    act.wait_ge(done[b], i + 1)
                    act.activation(x[:, b], pG[b][:], ACT.Identity, scale=cw[:, 2, ds(2 * i + b, 1)], bias=cw[:, 3, ds(2 * i + b, 1)]).then_inc(started[b], 1)
                    act.wait_ge(summed[b], i + 1)
                    act.activation(x[:, b], x[:, b], ACT.Gelu_apprx_tanh).then_inc(gelu[b], 1)

        @block.vector
        def _(dve):
            step = Steps(dve, order)
            for b in range(2):
                dve.sem_inc(done[b], 1)
            dve.wait_ge(conv_in, 64)
            with dve.Fori(0, NF // 2) as i:
                step.restart()
                for b in range(2):
                    dve.wait_ge(started[b], i + 1)
                    step(dve.scalar_tensor_tensor(out=x[:, b, 1:], in0=pG[b][:, 0:LAT - 1], scalar=cw[:, 1, ds(2 * i + b, 1)], in1=x[:, b, 1:], op0=ALU.mult, op1=ALU.add))
                    dve.scalar_tensor_tensor(out=x[:, b, 2:], in0=pG[b][:, 0:LAT - 2], scalar=cw[:, 0, ds(2 * i + b, 1)], in1=x[:, b, 2:], op0=ALU.mult, op1=ALU.add).then_inc(summed[b], 1)
                    dve.wait_ge(gelu[b], i + 1)
                    dve.tensor_tensor(aT[:, ds(2 * i + b, 1), :], x[:, b:b + 1], pU[b][:].rearrange("p (o n) -> p o n", o=1), ALU.mult).then_inc(done[b], 1)


def feed_forward_down_phase(nc, g, aT):
    w_dram = g["w_ff_down_2"][0].rearrange("(k p) n -> p k n", p=P)
    with Phase(nc) as ph:
        w = ph.sb("w", [P, 2, D])
        a = ph.sb("a", [P, 2, LAT])
        x = ph.sb("x", [P, NLAT, D])
        r = ph.sb("r", [P, D])
        grow = ph.sb("grow", [P, D])
        ss = ph.sb("ss", [P, NLAT, 2])
        eps = ph.sb("eps", [P, 1])
        acc = [ph.ps(f"acc{t}", [P, D]) for t in range(NLAT)]
        w_in, a_ready, used = (ph.sems(k) for k in ("w_in", "a_ready", "used"))
        const_in, eps_set, squared, rooted, done, stored, order = (ph.sem(k) for k in ("const_in", "eps_set", "squared", "rooted", "done", "stored", "order"))
        block = ph.block()

        @block.sync
        def _(sp):
            ph.clear_other_pool(sp)
            with sp.Fori(0, NF // 2) as i:
                for b in range(2):
                    sp.wait_ge(used[b], i + 1)
                    sp.dma_start(w[:, b:b + 1], w_dram[:, ds(2 * i + b, 1), :]).then_inc(w_in[b], 16)
            sp.dma_start(grow[:], g["post_ffn_g_2"].broadcast_to([P, D])).then_inc(const_in, 16)
            sp.dma_start(x[:], g["x_mid"].rearrange("(t p) n -> p t n", p=P)).then_inc(const_in, 16)
            for t in range(NLAT):
                sp.wait_ge(done, t + 1)
                sp.dma_start(g["out"][0, t * P:(t + 1) * P, :], x[:, t]).then_inc(stored, 16)
            sp.wait_ge(stored, 16 * NLAT)

        @block.gpsimd
        def _(pool):
            with pool.Fori(0, NF // 2) as i:
                for b in range(2):
                    pool.wait_ge(used[b], i + 1)
                    pool.tensor_copy(a[:, b:b + 1], aT[:, ds(2 * i + b, 1), :]).then_inc(a_ready[b], 1)

        @block.tensor
        def _(pe):
            for b in range(2):
                pe.sem_inc(used[b], 1)

            def product(i, b, first, end):
                pe.wait_ge(w_in[b], 16 * (i + 1))
                pe.wait_ge(a_ready[b], i + 1)
                for t in range(NLAT):
                    for h in range(2):
                        last = pe.matmul(acc[t][:, h * 512:(h + 1) * 512], a[:, b, t * P:(t + 1) * P], w[:, b, h * 512:(h + 1) * 512],
                                         start=first, stop=end)
                last.then_inc(used[b], 1)

            product(0, 0, True, False)
            product(0, 1, False, False)
            with pe.Fori(1, NF // 2 - 1) as i:
                for b in range(2):
                    product(i, b, False, False)
            product(NF // 2 - 1, 0, False, False)
            product(NF // 2 - 1, 1, False, True)

        @block.scalar
        def _(act):
            act.wait_ge(eps_set, 1)
            act.wait_ge(used[1], NF // 2 + 1)
            for t in range(NLAT):
                if t:
                    act.wait_ge(done, t)
                act.activation(r[:], acc[t][:, :], ACT.Square, accum_out=ss[:, t, 0:1]).then_inc(squared, 1)
                act.wait_ge(squared, t + 1)
                act.activation(ss[:, t, 1:2], ss[:, t, 0:1], ACT.Sqrt, scale=1.0 / D, bias=eps[:]).then_inc(rooted, 1)

        @block.vector
        def _(dve):
            step = Steps(dve, order)
            dve.memset(eps[:], EPS2).then_inc(eps_set, 1)
            dve.wait_ge(const_in, 32)
            for t in range(NLAT):
                dve.wait_ge(rooted, t + 1)
                step(dve.reciprocal(ss[:, t, 1:2], ss[:, t, 1:2]))
                step(dve.scalar_tensor_tensor(out=r[:], in0=acc[t][:, :], scalar=ss[:, t, 1:2], in1=grow[:], op0=ALU.mult, op1=ALU.mult))
                dve.tensor_tensor(x[:, t], x[:, t], r[:], ALU.add).then_inc(done, 1)


def program(nc, g):
    Phase.count = 0

    def dram(name, shape, dt=F32):
        g[name] = nc.dram_tensor(name, shape, dt, kind="Internal").ap()

    dram("mods", [DEPTH, 2, 6 * D])
    dram("h_mid", [TOK, D])
    dram("f", [TOK, D])
    dram("y", [2 * TOK, D])
    dram("h", [TOK, D])
    dram("x_mid", [LAT, D])
    dram("rpb_pad", [8 * 15, P])
    with ExitStack() as whole:
        ident = whole.enter_context(nc.sbuf_tensor("ident", [P, P], F32))
        ident_in = whole.enter_context(nc.semaphore("ident_in"))
        with nc.Block() as block:
            @block.sync
            def _(sp):
                sp.dma_start(ident[:], g["ident"]).then_inc(ident_in, 16)
                sp.wait_ge(ident_in, 16)
        g["ident"] = ident
        modulation_phase(nc, g)
        srcs = (g["x"][0], g["ctx"][0])
        for l in range(DEPTH):
            nt = NTILE if l < DEPTH - 1 else NLAT
            with ExitStack() as layer:
                def keep(name, shape, dt=F32, stack=layer):
                    return stack.enter_context(nc.sbuf_tensor(f"{name}{l}", shape, dt))

                logits = keep("logits", [P, NTILE, 36])
                share = keep("share", [P, NTILE, 2])
                gather_at = keep("gather_at", [P, items(NTILE) + 2], I32)
                scatter_at = keep("scatter_at", [P, items(NTILE)], I32)
                expert_of = keep("expert_of", [P, items(NTILE)], I32)
                pairs_of = keep("pairs_of", [P, 1], I32)
                with ExitStack() as mixer:
                    qT, kT, V = (keep(n, s, stack=mixer) for n, s in (
                        ("qT", [P, 8, TOK]), ("kT", [P, 6, TOK]), ("V", [P, NTILE, 640])))
                    projection_phase(nc, g, l, srcs, qT, kT, V)
                    bias = None
                    if l == 1:
                        bias = keep("na_bias", [P, 8, 14, HD], stack=mixer)
                        neighbour_bias_phase(nc, g, bias)
                    attention_phase(nc, g, l, srcs, qT, kT, V, logits, bias)
                routing_phase(nc, g, nt, logits, share, gather_at, scatter_at, expert_of, pairs_of)
                expert_phase(nc, g, l, nt, gather_at, scatter_at, expert_of, pairs_of)
                combine_phase(nc, g, l, share, g["h"])
                srcs = (g["h"][0:LAT, :], g["h"][LAT:TOK, :])
        with ExitStack() as mix:
            def keep2(name, shape, stack=mix):
                return stack.enter_context(nc.sbuf_tensor(name, shape, F32))

            hT = keep2("hT", [P, C, LAT])
            yT = keep2("yT", [P, 12, LAT])
            norm_turn_phase(nc, g, g["h"], g["pre_mix_g_2"], hT)
            with ExitStack() as part:
                G, gv = keep2("G", [P, 12, LAT], part), keep2("gv", [P, NLAT, 1, 512], part)
                columns_phase(nc, g, hT, 0, 12, G)
                rows_phase(nc, g, hT, [2 * GLA_Q], gv)
                gla_phase(nc, g, hT, G, gv, yT)
            with ExitStack() as part:
                Z = keep2("Z", [P, 12, LAT], part)
                columns_phase(nc, g, hT, SC_AT, 12, Z)
                short_conv_phase(nc, g, Z, yT)
            with ExitStack() as part:
                QK, dv = keep2("QK", [P, 24, LAT], part), keep2("dv", [P, NLAT, 3, 512], part)
                columns_phase(nc, g, hT, DIL_AT, 24, QK, turn=True)
                rows_phase(nc, g, hT, [DIL_AT + 2 * DIL_W + 512 * i for i in range(3)], dv)
                dilated_phase(nc, g, QK, dv, yT)
            merged = keep2("merged", [P, NLAT, D])
            merge_phase(nc, g, hT, yT, merged)
            mix_out_phase(nc, g, merged, hT)
            aT = keep2("aT", [P, NF, LAT])
            feed_forward_up_phase(nc, g, hT, aT)
            feed_forward_down_phase(nc, g, aT)


def constants():
    f = np.float32
    k = {}
    k["ident"] = np.eye(P, dtype=f)
    k["ones"] = np.ones((P, P), f)
    k["earlier"] = np.triu(np.ones((P, P), f), 1)
    for n in (64, 128):
        r = np.zeros((P, P), f)
        for m in range(P):
            first = m % n < n // 2
            r[m + n // 2 if first else m - n // 2, m] = -1.0 if first else 1.0
        k[f"rot{n}"] = r
    k["blk64"] = (np.kron(np.eye(2), np.ones((64, 64))) / 64).astype(f)
    t = np.arange(LAT)
    inv = (f(10000.0) ** (-np.arange(16, dtype=f) / f(16))).astype(f)
    ang = np.concatenate([(t // GRID_W).astype(f)[:, None] * inv, (t % GRID_W).astype(f)[:, None] * inv], -1).astype(f)
    for name, fn in (("cos", np.cos), ("sin", np.sin)):
        k[name] = np.ascontiguousarray(np.tile(fn(ang).T, (4, 1)).astype(f))
    q, m = t[:, None], t[None, :]
    k["win_mask"] = np.where(np.abs(q - m) <= WINDOW, 0.0, NEG).astype(f)
    col = np.arange(GRID_W)
    start = np.clip(col - NA_COLS // 2, 0, GRID_W - NA_COLS)
    ok = (col[None, :] >= start[:, None]) & (col[None, :] < start[:, None] + NA_COLS)
    k["na_keep"] = np.tile(ok.astype(f), (2, 1))
    k["na_mask"] = np.tile(np.where(ok, 0.0, NEG).astype(f), (2, 1))
    k["dil_mask"] = np.stack([np.where((q >= m) & ((q - m) % s == 0) & (q - m <= 128 * s), 0.0, NEG) for s in (1, 4, 16)]).astype(f)
    k["chunk_keep"] = np.tile((t % GCH != 0).astype(f), (P, 1))
    k["member"] = (np.arange(P)[:, None] // GCH == np.arange(P // GCH)[None, :]).astype(f)
    k["flip64"] = np.kron(np.eye(2), np.eye(64)[::-1]).astype(f)
    k["count"] = np.tile(np.arange(P, dtype=f), (P, 1))
    k["token"] = (np.arange(NTILE)[None, :] * P + np.arange(P)[:, None]).astype(f)
    k["inv_freq"] = np.tile((f(10000.0) ** (-np.arange(0, 128, 2, dtype=f) / f(128))).astype(f), 2)[:, None].copy()
    return k


def kernel(**inputs):
    import concourse.bacc as _bacc
    from concourse.bass_utils import run_bass_kernel_spmd as _run

    nc = _bacc.Bacc("TRN2", target_bir_lowering=False, num_devices=1)
    arrays, g = {}, {}
    for name, a in list(inputs.items()) + list(constants().items()):
        a = np.ascontiguousarray(a)
        arrays[f"in_{name}"] = a
        g[name] = nc.dram_tensor(f"in_{name}", a.shape, mybir.dt.from_np(a.dtype), kind="ExternalInput").ap()
    g["out"] = nc.dram_tensor("out_dram", (1, LAT, D), F32, kind="ExternalOutput").ap()
    program(nc, g)
    r = _run(nc, [arrays], core_ids=[0])
    return r.results[0]["out_dram"]
```

```python
from contextlib import ExitStack
import math

import numpy as np

import concourse.bass as bass
from concourse import mybir

F32 = mybir.dt.float32
I32 = mybir.dt.int32
ALU = mybir.AluOpType
ACT = mybir.ActivationFunctionType
AX = mybir.AxisListType
ds = bass.ds

P = 128
D = 1024
C = D // P
LAT, CTX = 512, 256
TOK = LAT + CTX
NLAT, NCTX = LAT // P, CTX // P
NTILE = NLAT + NCTX
DEPTH = 2
HD = 64
GRID_W = 64
ROWS = LAT // GRID_W
NA_COLS = 16
WINDOW = 128
NG, EPG = 4, 8
NE = NG * EPG
DE = 512
ALPHA = (2.0 * DEPTH) ** 0.25
LN_EPS = 1e-5
RMS_EPS = 1e-6
SCALE = HD ** -0.5
NEG = -1e30
LAM_INIT = 0.8 - 0.6 * math.exp(0.0)


class Steps:

    def __init__(self, eng, sem):
        self.eng, self.sem, self.n = eng, sem, 0

    def __call__(self, ins):
        self.n += 1
        ins.then_inc(self.sem, 1)
        self.eng.wait_ge(self.sem, self.n)

    def settle(self):
        self.n += 1
        self.eng.sem_inc(self.sem, 1)
        self.eng.wait_ge(self.sem, self.n)

    def restart(self):
        self.eng.sem_clear(self.sem)
        self.n = 0


class Phase:

    POOL = 52
    FIRST = 150
    count = 0

    def __init__(self, nc):
        self.nc, self.stack = nc, ExitStack()
        self.base = Phase.FIRST + Phase.POOL * (Phase.count % 2)
        self.other = Phase.FIRST + Phase.POOL * ((Phase.count + 1) % 2)
        self.first = Phase.count == 0
        self.used = 0
        Phase.count += 1

    def __enter__(self):
        return self

    def __exit__(self, *a):
        return self.stack.__exit__(*a)

    def sb(self, name, shape, dt=F32):
        return self.stack.enter_context(self.nc.sbuf_tensor(f"{name}_{Phase.count}", shape, dt))

    def ps(self, name, shape, dt=F32):
        return self.stack.enter_context(self.nc.psum_tensor(f"{name}_{Phase.count}", shape, dt))

    def sem(self, name):
        s = self.stack.enter_context(self.nc.semaphore(f"{name}_{Phase.count}", num=self.base + self.used))
        self.used += 1
        assert self.used <= Phase.POOL
        return s

    def sems(self, name, n=2):
        return [self.sem(f"{name}{i}") for i in range(n)]

    def block(self):
        return self.stack.enter_context(self.nc.Block())

    def clear_other_pool(self, sp):
        if not self.first:
            sp.sem_clear(range(self.other, self.other + Phase.POOL))


def modulation_phase(nc, g):
    W = 1024
    H = W // 2
    with Phase(nc) as ph:
        vec = ph.sb("vec", [P, 2, C])
        act_vec = ph.sb("act_vec", [P, C, 2])
        w = ph.sb("w", [P, 2, C, W])
        bias = ph.sb("bias", [64, 2, H])
        row = ph.sb("row", [64, 2, H])
        acc = [ph.ps(f"acc{b}", [P, W]) for b in range(2)]
        vec_in, silu_done = ph.sem("vec_in"), ph.sem("silu_done")
        w_in, product, added, stored = (ph.sems(n) for n in ("w_in", "product", "added", "stored"))
        block = ph.block()

        def chunks(eng):
            for l in range(DEPTH):
                with eng.Fori(0, 3) as m:
                    yield l, m, m + 3 * l

        @block.sync
        def _(sp):
            ph.clear_other_pool(sp)
            sp.dma_start(vec[:, 0, :], g["c"].rearrange("a (p k) -> (a p) k", p=P)).then_inc(vec_in, 16)
            sp.dma_start(vec[:, 1, :], g["c_ctx"].rearrange("(p k) -> p k", p=P)).then_inc(vec_in, 16)
            for l, m, n in chunks(sp):
                wv = g["mod_w"][l].rearrange("(p k) n -> p k n", p=P)
                bv = g["mod_b"][l:l + 1, :].broadcast_to([2, 6 * D])
                for b in range(2):
                    sp.wait_ge(product[b], n + 1)
                    sp.wait_ge(added[b], n + 1)
                    sp.dma_start(w[:, b], wv[:, :, ds(m * 2 * W + b * W, W)]).then_inc(w_in[b], 16)
                    for h in range(2):
                        sp.dma_start(bias[32 * h:32 * h + 2, b], bv[:, ds(m * 2 * W + b * W + h * H, H)]).then_inc(w_in[b], 16)

        @block.scalar
        def _(act):
            act.wait_ge(vec_in, 32)
            act.activation(act_vec[:].rearrange("p k v -> p v k"), vec[:], ACT.Silu).then_inc(silu_done, 1)
            for b in range(2):
                act.sem_inc(stored[b], 32)
            for l, m, n in chunks(act):
                for b in range(2):
                    act.wait_ge(added[b], n + 2)
                    for h in range(2):
                        act.dma_start(g["mods"][l, :, ds(m * 2 * W + b * W + h * H, H)], row[32 * h:32 * h + 2, b]).then_inc(stored[b], 16)
            for b in range(2):
                act.wait_ge(stored[b], 32 * (3 * DEPTH + 1))

        @block.vector
        def _(dve):
            for b in range(2):
                dve.sem_inc(added[b], 1)
            for l, m, n in chunks(dve):
                for b in range(2):
                    dve.wait_ge(w_in[b], 48 * (n + 1))
                    dve.wait_ge(product[b], n + 2)
                    dve.wait_ge(stored[b], 32 * (n + 1))
                    for h in range(2):
                        strip = slice(32 * h, 32 * h + 2)
                        last = dve.tensor_tensor(row[strip, b], acc[b][strip, h * H:(h + 1) * H], bias[strip, b], ALU.add)
                    last.then_inc(added[b], 1)

        @block.tensor
        def _(pe):
            for b in range(2):
                pe.sem_inc(product[b], 1)
            pe.wait_ge(silu_done, 1)
            for l, m, n in chunks(pe):
                for b in range(2):
                    pe.wait_ge(w_in[b], 48 * (n + 1))
                    pe.wait_ge(added[b], n + 1)
                    for k in range(C):
                        for h in range(2):
                            last = pe.matmul(acc[b][32 * h:32 * h + 2, h * H:(h + 1) * H], act_vec[:, k, :],
                                             w[:, b, k, h * H:(h + 1) * H], start=(k == 0), stop=(k == C - 1))
                    last.then_inc(product[b], 1)


GROUPS = [
    [(0, 4, False, None, True, "q", 0), (512, 4, False, 0, True, "q", 4),
     (1024, 4, False, None, True, "k", 0), (2048, 2, True, 1, True, "k", 4)],
    [(0, 4, False, None, True, "q", 0), (512, 4, False, None, False, "q", 4),
     (1024, 2, True, None, True, "k", 0), (1280, 4, False, None, False, "k", 2)],
]
V_COLS = [(1536, 2176), (1792, 1152)]


def projection_phase(nc, g, l, srcs, qT, kT, V):
    w_in_dram = g["ab_w_in" if l == 0 else "cd_w_in"][0].rearrange("(p k) n -> p k n", p=P)
    with Phase(nc) as ph:
        rows = ph.sb("rows", [P, 2, D])
        aT = ph.sb("aT", [P, C, TOK])
        mcol = ph.sb("mcol", [P, 2, 2, C])
        w = ph.sb("w", [P, 2, C, P])
        wv = ph.sb("wv", [P, C, 640])
        xs = ph.sb("xs", [P, 2, TOK])
        sq = ph.sb("sq", [P, 2, TOK])
        t1 = ph.sb("t1", [P, 2, LAT])
        t2 = ph.sb("t2", [P, 2, LAT])
        cos, sin = ph.sb("cos", [P, LAT]), ph.sb("sin", [P, LAT])
        rot, blk = ph.sb("rot", [P, P]), ph.sb("blk", [P, P])
        gain = ph.sb("gain", [P, 2])
        eps = ph.sb("eps", [P, 1])
        pa = [ph.ps(f"pa{b}", [P, 1024]) for b in range(2)]
        pn = ph.ps("pn", [P, 1024])
        pr = [ph.ps(f"pr{b}", [P, 512]) for b in range(2)]
        const_in, wv_in, plus_one, eps_set = (ph.sem(n) for n in ("const_in", "wv_in", "plus_one", "eps_set"))
        row_in, turned, moved = ph.sems("row_in"), ph.sems("turned"), ph.sems("moved")
        w_in, projected, x_ready, squared, meaned, rooted, rotated, written = (
            ph.sems(n) for n in ("w_in", "projected", "x_ready", "squared", "meaned", "rooted", "rotated", "written"))
        v_done, v_out = ph.sems("v_done"), ph.sems("v_out")
        order = ph.sem("order")
        block = ph.block()
        ident = g["ident"]

        def pairs(eng):
            with eng.Fori(0, NLAT // 2) as m:
                yield srcs[0], m, 0, m
            yield srcs[1], 0, 1, NLAT // 2

        def groups(eng):
            n0 = 0
            for col, n, dup, norm, rope, dst, at in GROUPS[l]:
                with eng.Fori(0, n // 2) as i:
                    yield (col, dup, norm, rope, qT if dst == "q" else kT, at), i, i + n0
                n0 += n // 2

        @block.sync
        def _(sp):
            ph.clear_other_pool(sp)
            for v in range(2):
                for s in range(2):
                    sp.dma_start(mcol[:, v, s, :], g["mods"][l, v, s * D:(s + 1) * D].rearrange("(p k) -> p k", p=P)).then_inc(const_in, 16)
            for dst, src in ((cos, "cos"), (sin, "sin"), (rot, "rot64"), (blk, "blk64")):
                sp.dma_start(dst[:], g[src]).then_inc(const_in, 16)
            for s in range(2):
                for half in range(2):
                    sp.dma_start(gain[half * HD:(half + 1) * HD, s:s + 1],
                                 g["gqa_qk_g"][0, s, :].rearrange("(p o) -> p o", o=1)).then_inc(const_in, 16)
            for (src, m, v, n) in pairs(sp):
                for b in range(2):
                    sp.wait_ge(turned[1], 2 * n + b + 1)
                    sp.dma_start(rows[:, b], src[ds(m * 2 * P + b * P, P), :]).then_inc(row_in[b], 16)
            c5, c1 = V_COLS[l]
            sp.dma_start(wv[:, :, 0:512], w_in_dram[:, :, c5:c5 + 512]).then_inc(wv_in, 16)
            sp.dma_start(wv[:, :, 512:640], w_in_dram[:, :, c1:c1 + 128]).then_inc(wv_in, 16)
            for (col, dup, norm, rope, dst, at), i, n in groups(sp):
                for b in range(2):
                    sp.wait_ge(projected[b], n + 1)
                    if dup:
                        src = w_in_dram[:, :, col + b * HD:col + (b + 1) * HD]
                        src = src.rearrange("p k (o n) -> p k o n", o=1).broadcast_to([P, C, 2, HD])
                        dstw = w[:, b].rearrange("p k (o n) -> p k o n", o=2)
                        for o in range(2):
                            sp.dma_start(dstw[:, :, o, :], src[:, :, o, :]).then_inc(w_in[b], 16)
                    else:
                        for o in range(2):
                            sp.dma_start(w[o * 64:(o + 1) * 64, b], w_in_dram[o * 64:(o + 1) * 64, :, ds(i * 2 * P + col + b * P, P)]).then_inc(w_in[b], 16)

        @block.tensor
        def _(pe):
            pe.sem_inc(turned[1], 2)
            for b in range(2):
                pe.sem_inc(projected[b], 1)
            for (src, m, v, n) in pairs(pe):
                for b in range(2):
                    pe.wait_ge(row_in[b], 16 * (n + 1))
                    for h in range(2):
                        pe.wait_ge(moved[h], 2 * n + b + 1)
                        for k in range(4):
                            last = pe.transpose(pr[h][:, k * P:(k + 1) * P], rows[:, b, h * 4 + k::C], ident[:])
                        last.then_inc(turned[h], 1)
            pe.wait_ge(const_in, 16 * 12)
            pe.wait_ge(moved[0], NTILE + 1)
            pe.wait_ge(moved[1], NTILE + 1)
            for (col, dup, norm, rope, dst, at), i, n in groups(pe):
                for b in range(2):
                    pe.wait_ge(w_in[b], 32 * (n + 1))
                    pe.wait_ge(x_ready[b], n + 1)
                    pe.wait_ge(written[b], n + 1)
                    for k in range(C):
                        pe.matmul(pa[b][:, 0:512], w[:, b, k, :], aT[:, k, 0:512], start=(k == 0), stop=(k == C - 1))
                        last = pe.matmul(pa[b][:, 512:768], w[:, b, k, :], aT[:, k, 512:768], start=(k == 0), stop=(k == C - 1))
                    last.then_inc(projected[b], 1)
                if norm is not None:
                    for b in range(2):
                        pe.wait_ge(squared[b], i + 1 + (norm * 2))
                        pe.wait_ge(rooted[1 - b], i + norm * 2 + 1)
                        pe.matmul(pn[:, 0:512], blk[:], sq[:, b, 0:512], start=True, stop=True)
                        pe.matmul(pn[:, 512:768], blk[:], sq[:, b, 512:768], start=True, stop=True).then_inc(meaned[b], 1)
                if rope:
                    for b in range(2):
                        pe.wait_ge(x_ready[b], n + 2)
                        pe.matmul(pr[b][:, :], rot[:], xs[:, b, 0:512], start=True, stop=True).then_inc(rotated[b], 1)
            pe.wait_ge(wv_in, 32)
            npairs = sum(x[1] for x in GROUPS[l]) // 2
            for b in range(2):
                pe.wait_ge(x_ready[b], npairs + 1)
                pe.wait_ge(written[b], npairs + 1)
            for t in range(NTILE):
                b = t % 2
                if t >= 2:
                    pe.wait_ge(v_out[b], t // 2)
                for k in range(C):
                    pe.matmul(pa[b][:, 0:512], aT[:, k, t * P:(t + 1) * P], wv[:, k, 0:512], start=(k == 0), stop=(k == C - 1))
                    last = pe.matmul(pa[b][:, 512:640], aT[:, k, t * P:(t + 1) * P], wv[:, k, 512:640], start=(k == 0), stop=(k == C - 1))
                last.then_inc(v_done[b], 1)

        @block.scalar
        def _(act):
            act.sem_inc(moved[0], 1)
            for b in range(2):
                act.sem_inc(x_ready[b], 1)
            act.sem_inc(rooted[1], 1)
            act.wait_ge(plus_one, 1)
            for (src, m, v, n) in pairs(act):
                for b in range(2):
                    act.wait_ge(turned[0], 2 * n + b + 1)
                    for k in range(4):
                        last = act.activation(aT[:, k, ds(n * 2 * P + b * P, P)], pr[0][:, k * P:(k + 1) * P], ACT.Identity,
                                              scale=mcol[:, v, 1, k:k + 1], bias=mcol[:, v, 0, k:k + 1])
                    last.then_inc(moved[0], 1)
            for (col, dup, norm, rope, dst, at), i, n in groups(act):
                for b in range(2):
                    act.wait_ge(projected[b], n + 2)
                    act.wait_ge(written[b], n + 1)
                    if norm is not None:
                        act.activation(sq[:, b, :], pa[b][:, 0:768], ACT.Square).then_inc(squared[b], 1)
                    else:
                        last = act.activation(dst[:, ds(i * 2 + at + b, 1), 512:768], pa[b][:, 512:768], ACT.Copy)
                        if rope:
                            last = act.activation(xs[:, b, 0:512], pa[b][:, 0:512], ACT.Copy)
                        last.then_inc(x_ready[b], 1)
                if norm is not None:
                    for b in range(2):
                        act.wait_ge(meaned[b], i + 1 + norm * 2)
                        act.activation(sq[:, b, :], pn[:, 0:768], ACT.Sqrt, bias=eps[:]).then_inc(rooted[b], 1)
            for t in range(NTILE):
                act.wait_ge(v_done[t % 2], t // 2 + 1)
                act.activation(V[:, t, :], pa[t % 2][:, 0:640], ACT.Copy).then_inc(v_out[t % 2], 1)

        @block.vector
        def _(dve):
            step = Steps(dve, order)
            dve.sem_inc(moved[1], 1)
            for b in range(2):
                dve.sem_inc(written[b], 1)
            dve.wait_ge(const_in, 16 * 12)
            step(dve.memset(eps[:], RMS_EPS))
            dve.tensor_scalar(mcol[:, :, 1, :], mcol[:, :, 1, :], 1.0, None, ALU.add).then_inc(plus_one, 1)
            dve.wait_ge(plus_one, 1)
            for (src, m, v, n) in pairs(dve):
                for b in range(2):
                    dve.wait_ge(turned[1], 2 * n + b + 3)
                    for k in range(4):
                        last = dve.tensor_scalar(aT[:, 4 + k, ds(n * 2 * P + b * P, P)], pr[1][:, k * P:(k + 1) * P],
                                                 mcol[:, v, 1, 4 + k:5 + k], mcol[:, v, 0, 4 + k:5 + k], ALU.mult, ALU.add)
                    last.then_inc(moved[1], 1)
            for (col, dup, norm, rope, dst, at), i, n in groups(dve):
                step.restart()
                for b in range(2):
                    o = dst[:, ds(i * 2 + at + b, 1), :].rearrange("p o n -> p (o n)")
                    if norm is not None:
                        dve.wait_ge(rooted[b], i + 1 + norm * 2 + b)
                        step(dve.reciprocal(sq[:, b, :], sq[:, b, :]))
                        dve.scalar_tensor_tensor(out=xs[:, b, :], in0=pa[b][:, 0:768], scalar=gain[:, norm:norm + 1],
                                                 in1=sq[:, b, :], op0=ALU.mult, op1=ALU.mult).then_inc(x_ready[b], 1)
                for b in range(2):
                    o = dst[:, ds(i * 2 + at + b, 1), :]
                    if rope:
                        dve.wait_ge(x_ready[b], n + 2)
                        dve.tensor_tensor(t1[:, b, :], xs[:, b, 0:512], cos[:], ALU.mult)
                        dve.wait_ge(rotated[b], n + 1 - _unrotated(l, col))
                        step(dve.tensor_tensor(t2[:, b, :], pr[b][:, :], sin[:], ALU.mult))
                        if norm is not None:
                            dve.tensor_copy(o[:, :, 512:768], xs[:, b:b + 1, 512:768])
                        dve.tensor_tensor(o[:, :, 0:512], t1[:, b:b + 1, :], t2[:, b:b + 1, :], ALU.add).then_inc(written[b], 1)
                    else:
                        dve.wait_ge(projected[b], n + 2)
                        dve.tensor_copy(o[:, :, 0:512], pa[b][:, 0:512].rearrange("p (o n) -> p o n", o=1)).then_inc(written[b], 1)


def _unrotated(l, col):
    n = 0
    for c, k, dup, norm, rope, dst, at in GROUPS[l]:
        if c == col:
            return n
        n += 0 if rope else k // 2


def neighbour_bias_phase(nc, g, bias):
    NH, NR, NC = 8, 15, 31
    PAD = (P - NC) // 2
    W = 14 * HD // 2
    with Phase(nc) as ph:
        pad = ph.sb("pad", [NH * NR, P])
        keep, mask, flip = ph.sb("keep", [P, HD]), ph.sb("mask", [P, HD]), ph.sb("flip", [P, P])
        back = ph.sb("back", [P, NH, 14, HD])
        pF = [ph.ps(f"pF{b}", [P, 512]) for b in range(2)]
        zeroed, table_in, padded, bias_in, const_in, flipped, kept, order = (
            ph.sem(n) for n in ("zeroed", "table_in", "padded", "bias_in", "const_in", "flipped", "kept", "order"))
        block = ph.block()

        @block.sync
        def _(sp):
            ph.clear_other_pool(sp)
            for dst, src in ((keep, "na_keep"), (mask, "na_mask"), (flip, "flip64")):
                sp.dma_start(dst[:], g[src]).then_inc(const_in, 16)
            sp.wait_ge(zeroed, 1)
            sp.dma_start(pad[:, PAD:PAD + NC], g["na_rpb"][0].rearrange("h r k -> (h r) k")).then_inc(table_in, 16)
            sp.wait_ge(table_in, 16)
            sp.dma_start(g["rpb_pad"], pad[:]).then_inc(padded, 16)
            sp.wait_ge(padded, 16)
            for h in range(NH):
                for r in range(2):
                    src = bass.AP(g["rpb_pad"].tensor, (h * NR + 1 - r) * P, [[1, 64], [P, 14], [1, 64]])
                    sp.dma_start(back[r * 64:(r + 1) * 64, h], src).then_inc(bias_in, 16)

        @block.tensor
        def _(pe):
            pe.wait_ge(const_in, 48)
            pe.wait_ge(bias_in, 16 * 2 * NH)
            for i in range(2 * NH):
                if i >= 2:
                    pe.wait_ge(kept, i - 1)
                pe.matmul(pF[i % 2][:, 0:W], flip[:], back[:, i // 2].rearrange("p a n -> p (a n)")[:, (i % 2) * W:(i % 2 + 1) * W],
                          start=True, stop=True).then_inc(flipped, 1)

        @block.vector
        def _(dve):
            step = Steps(dve, order)
            dve.memset(pad[:], 0.0).then_inc(zeroed, 1)
            dve.wait_ge(const_in, 48)
            for i in range(2 * NH):
                def wide(x):
                    return x[:].rearrange("p (o n) -> p o n", o=1).broadcast_to([P, 7, HD])
                to = bias[:, i // 2, (i % 2) * 7:(i % 2 + 1) * 7, :]
                dve.wait_ge(flipped, i + 1)
                dve.tensor_tensor(to, pF[i % 2][:, 0:W].rearrange("p (a n) -> p a n", n=HD), wide(keep), ALU.mult).then_inc(kept, 1)
                dve.wait_ge(kept, i + 1)
                step(dve.tensor_tensor(to, to, wide(mask), ALU.add))


def attention_phase(nc, g, l, srcs, qT, kT, V, logits, na_bias):
    diff = 4 if l == 0 else 0
    R = diff + 2 * (8 - diff)
    last_l = l == DEPTH - 1
    groups = [(0, NLAT, 0, 6)] + ([] if last_l else [(NLAT, NCTX, 1, 2)])
    with Phase(nc) as ph:
        q2 = ph.sb("q2", [P, 8, 2, P])
        E = ph.sb("E", [P, 2, 2, TOK])
        a = ph.sb("a", [P, 2, TOK]) if diff else None
        PT = ph.sb("PT", [P, 6, P])
        o = ph.sb("o", [P, D])
        oT = ph.sb("oT", [P, C, P])
        wout = ph.sb("wout", [P, C, D])
        wr = ph.sb("wr", [P, C, 36])
        rb = ph.sb("rb", [P, 36])
        h = ph.sb("h", [P, D])
        r = ph.sb("r", [P, D])
        total = sum(x[1] for x in groups)
        f = ph.sb("f", [P, total, D])
        nv = len(groups)
        mrow = ph.sb("mrow", [P, nv, 3, D])
        lrow = ph.sb("lrow", [P, 2, D])
        st = ph.sb("st", [P, 3, 2, 6])
        bn = ph.sb("bn", [P, 2, 6])
        mv = ph.sb("mv", [P, 4])
        root = ph.sb("root", [P, 1])
        own = ph.sb("own", [P, 2])
        eps = ph.sb("eps", [P, 2])
        lv = ph.sb("lv", [P, 4, HD]) if diff else None
        lam = ph.sb("lam", [P, 8]) if diff else None
        sub_g = ph.sb("sub_g", [P, P]) if diff else None
        ss = ph.sb("ss", [P, 4]) if diff else None
        wmask = None if diff else ph.sb("wmask", [P, NLAT, LAT])
        sink = None if diff else ph.sb("sink", [P, 8])
        pS = [ph.ps(f"pS{b}", [P, 1024]) for b in range(2)]
        pT = ph.ps("pT", [P, 1024])
        pO = [ph.ps(f"pO{b}", [P, 512]) for b in range(2)]
        first_in, const_in, const_set, lam_sum, lam_exp = (ph.sem(n) for n in ("first_in", "const_in", "const_set", "lam_sum", "lam_exp"))
        zeroed, q_ready, q_used, h_in = (ph.sem(n) for n in ("zeroed", "q_ready", "q_used", "h_in"))
        scored, s_free, shifted, e_ready, summed, r_ready = (
            ph.sems(n) for n in ("scored", "s_free", "shifted", "e_ready", "summed", "r_ready"))
        a_ready, turned, moved, pv, o_out, merged, mixed = (
            ph.sem(n) for n in ("a_ready", "turned", "moved", "pv", "o_out", "merged", "mixed"))
        o_ready, var_ready, root_ready, h_ready, f_ready, ss_ready, ss_root = (
            ph.sem(n) for n in ("o_ready", "var_ready", "root_ready", "h_ready", "f_ready", "ss_ready", "ss_root"))
        bigT, bigA, bigD, f_free, routed, summed_up, h_stored, f_stored = (
            ph.sem(n) for n in ("bigT", "bigA", "bigD", "f_free", "routed", "summed_up", "h_stored", "f_stored"))
        order, order_a, order_p, rstd_ready = (ph.sem(n) for n in ("order", "order_a", "order_p", "rstd_ready"))
        block = ph.block()
        ident = g["ident"]
        n_const = 1 + 2 + 2 + 3 * nv + 2

        def tiles(eng):
            for base, n, v, nk in groups:
                with eng.Fori(0, n) as t:
                    yield t + base, t, v, 6 - nk, nk

        def rounds(i):
            return [i] if i < diff else [diff + 2 * (i - diff) + b for b in range(2)]

        def k_chunk(i):
            if l == 0:
                return i if i < 4 else 4 + (i - 4) // 2
            return i // 2 if i < 4 else 2 + i - 4

        def v_cols(i, b):
            if i < diff:
                return i * P, P
            grouped = i >= 4 if l == 0 else i < 4
            if grouped:
                return 512 + HD * ((i % 4) // 2), HD
            return (i % 4) * P + b * HD, HD

        @block.sync
        def _(sp):
            ph.clear_other_pool(sp)
            if diff:
                sp.dma_start(lv[:].rearrange("p a b -> p (a b)"),
                             g["diff_lambda"].rearrange("o a b -> o (a b)").broadcast_to([P, 4 * HD])).then_inc(first_in, 16)
                sp.dma_start(sub_g[:], g["diff_subln_g"].broadcast_to([P, P])).then_inc(first_in, 16)
            else:
                sp.dma_start(wmask[:], g["win_mask"].rearrange("(t p) n -> p t n", p=P)).then_inc(first_in, 16)
                sp.dma_start(sink[:], g["win_sink"].broadcast_to([P, 8])).then_inc(first_in, 16)
            w_out_dram = g["ab_w_out" if l == 0 else "cd_w_out"][0].rearrange("(p k) n -> p k n", p=P)
            sp.dma_start(wout[:], w_out_dram).then_inc(const_in, 16)
            sp.dma_start(wr[:, :, 0:NG], g["moe_w_group"][l].rearrange("(p k) n -> p k n", p=P)).then_inc(const_in, 16)
            sp.dma_start(wr[:, :, NG:36], g["moe_w_router"][l].rearrange("(p k) n -> p k n", p=P)).then_inc(const_in, 16)
            sp.dma_start(rb[:, 0:NG], g["moe_b_group"][l:l + 1, :].broadcast_to([P, NG])).then_inc(const_in, 16)
            sp.dma_start(rb[:, NG:36], g["moe_b_router"][l:l + 1, :].broadcast_to([P, NE])).then_inc(const_in, 16)
            for v in range(nv):
                for j, m in enumerate((2, 3, 4)):
                    sp.dma_start(mrow[:, v, j], g["mods"][l, v:v + 1, m * D:(m + 1) * D].broadcast_to([P, D])).then_inc(const_in, 16)
            sp.dma_start(lrow[:, 0], g["ln_g"][l, 0:1, :].broadcast_to([P, D])).then_inc(const_in, 16)
            sp.dma_start(lrow[:, 1], g["ln_b"][l, 0:1, :].broadcast_to([P, D])).then_inc(const_in, 16)
            for n, t, v, k0, nk in tiles(sp):
                sp.wait_ge(summed_up, n + 1)
                sp.dma_start(h[:], srcs[v][ds(t * P, P), :]).then_inc(h_in, 16)
                sp.wait_ge(h_ready, n + 1)
                sp.dma_start(g["h_mid"][ds(n * P, P), :], r[:]).then_inc(h_stored, 16)
                sp.wait_ge(f_ready, n + 1)
                sp.dma_start(g["f"][ds(n * P, P), :], f[:, ds(n, 1), :].rearrange("p o n -> p (o n)")).then_inc(f_stored, 16)
            sp.wait_ge(h_stored, 16 * (total + 1))
            sp.wait_ge(f_stored, 16 * total)

        @block.gpsimd
        def _(pool):
            for b in range(2):
                pool.memset(q2[(1 - b) * HD:(2 - b) * HD, :, b, :], 0.0).then_inc(zeroed, 1)
                pool.wait_ge(zeroed, b + 1)
            pool.memset(qT[:, :, TOK:TOK + P], 0.0).then_inc(zeroed, 1)
            step = Steps(pool, order_p)
            pool.sem_inc(f_free, 1)
            pool.wait_ge(const_in, 16 * n_const)
            for v in range(nv):
                step(pool.tensor_scalar(mrow[:, v, 2], mrow[:, v, 2], 1.0, None, ALU.add))
            for n, t, v, k0, nk in tiles(pool):
                step.restart()
                pool.wait_ge(rstd_ready, n + 1)
                step.settle()
                step(pool.tensor_copy(own[:], mv[:, 2:4]))
                step(pool.tensor_scalar(r[:], r[:], own[:, 0:1], own[:, 1:2], ALU.subtract, ALU.mult))
                step(pool.tensor_tensor(r[:], r[:], lrow[:, 0], ALU.mult))
                pool.tensor_tensor(r[:], r[:], lrow[:, 1], ALU.add).then_inc(h_ready, 1)
                pool.wait_ge(h_ready, n + 1)
                fn = f[:, ds(n, 1), :].rearrange("p o n -> p (o n)")
                step(pool.tensor_tensor(fn, r[:], mrow[:, v, 2], ALU.mult))
                pool.tensor_tensor(fn, fn, mrow[:, v, 1], ALU.add).then_inc(f_ready, 1)
                pool.wait_ge(f_ready, n + 1)
                pool.sem_inc(f_free, 1)

        @block.tensor
        def _(pe):
            pe.wait_ge(zeroed, 3)

            def turn_rows(block, count):
                for k in range(C):
                    last = pe.transpose(pT[:, k * P:(k + 1) * P], block(k), ident[:])
                last.then_inc(bigT, 1)
                pe.wait_ge(bigA, count)
                pe.wait_ge(bigD, count)

            for n, t, v, k0, nk in tiles(pe):
                def score(i, b):
                    pe.wait_ge(s_free[b], 8 * n + i + 1)
                    if nk == 6:
                        pe.matmul(pS[b][:, 0:512], q2[:, i, b, :], kT[:, k_chunk(i), 0:512], start=True, stop=True)
                    pe.matmul(pS[b][:, 512:768], q2[:, i, b, :], kT[:, k_chunk(i), 512:768],
                              start=True, stop=True).then_inc(scored[b], 1)
                    if i == 7 and b == 1:
                        pe.wait_ge(scored[b], 8 * n + 8)
                        pe.sem_inc(q_used, 1)

                def turn(i, j):
                    c = rounds(i)[j]
                    if i < diff:
                        pe.wait_ge(a_ready, diff * n + i + 1)
                        src = a[:, i % 2]
                    else:
                        pe.wait_ge(e_ready[j], 8 * n + i + 1)
                        src = E[:, i % 2, j]
                    pe.wait_ge(moved, R * n + c + 1)
                    for k in range(k0, 6):
                        last = pe.transpose(pT[:, k * P:(k + 1) * P], src[:, k * P:(k + 1) * P], ident[:])
                    last.then_inc(turned, 1)

                def weigh(i, j):
                    c = rounds(i)[j]
                    pe.wait_ge(moved, R * n + c + 2)
                    pe.wait_ge(o_out, R * n + c + 1)
                    c0, w = v_cols(i, j)
                    for k in range(k0, 6):
                        last = pe.matmul(pO[c % 2][:, 0:w], PT[:, k, :], V[:, k, c0:c0 + w], start=(k == k0), stop=(k == 5))
                    last.then_inc(pv, 1)

                pe.wait_ge(q_ready, 2 * n + 2)
                pe.wait_ge(merged, n + 1)
                for i in range(2):
                    for b in range(2):
                        score(i, b)
                for i in range(8):
                    for j in range(len(rounds(i))):
                        turn(i, j)
                        if i < 6:
                            for b in ([0, 1] if i < diff else [j]):
                                score(i + 2, b)
                        weigh(i, j)
                pe.wait_ge(const_in, 16 * n_const)
                pe.wait_ge(o_ready, n + 1)
                pe.wait_ge(q_used, n + 1)
                turn_rows(lambda k: o[:, k::C], n + 1)
                for b in range(2):
                    for k in range(C):
                        last = pe.matmul(pS[0][:, b * 512:(b + 1) * 512], oT[:, k, :], wout[:, k, b * 512:(b + 1) * 512],
                                         start=(k == 0), stop=(k == C - 1))
                last.then_inc(mixed, 1)
            pe.wait_ge(merged, total + 1)
            for t in range(total):
                pe.wait_ge(f_ready, t + 1)
                turn_rows(lambda k: f[:, t, k::C], total + t + 1)
                for k in range(C):
                    last = pe.matmul(pS[0][:, 36 * t:36 * t + 36], oT[:, k, :], wr[:, k, :], start=(k == 0), stop=(k == C - 1))
            last.then_inc(routed, 1)

        @block.scalar
        def _(act):
            step = Steps(act, order_a)
            for s in s_free + [moved]:
                act.sem_inc(s, 1)
            act.sem_inc(o_out, 2)
            if diff:
                act.wait_ge(lam_sum, 1)
                act.activation(lam[:, 2:4], lam[:, 0:2], ACT.Exp).then_inc(lam_exp, 1)
            act.wait_ge(const_set, 1)
            act.wait_ge(zeroed, 3)

            def copy_queries(n):
                for b in range(2):
                    rows = slice(b * HD, (b + 1) * HD)
                    act.activation(q2[rows, :, b, :], qT[rows, :, ds(n * P, P)], ACT.Copy).then_inc(q_ready, 1)

            copy_queries(0)
            for n, t, v, k0, nk in tiles(act):
                step.restart()
                keys = slice(k0 * P, TOK)

                def exp(i, b):
                    s = st[:, i % 3, b]
                    act.wait_ge(shifted[b], 8 * n + i + 1)
                    src, scale = (pS[b][:, keys], SCALE) if l == 0 else (E[:, i % 2, b, keys], 1.0)
                    last = act.activation(E[:, i % 2, b, keys], src, ACT.Exp, bias=s[:, 1:2], scale=scale, accum_out=s[:, 2:3])
                    if l == 1 and i < 4:
                        last = act.activation(s[:, 3:4], sink[:, 2 * i + b:2 * i + b + 1], ACT.Exp, bias=s[:, 1:2])
                    last.then_inc(e_ready[b], 1)
                    if l == 0:
                        act.wait_ge(e_ready[b], 8 * n + i + 1)
                        act.sem_inc(s_free[b], 1)

                for i in range(2):
                    for b in range(2):
                        exp(i, b)
                later = []
                for i in range(8):
                    for j, c in enumerate(rounds(i)):
                        act.wait_ge(turned, R * n + c + 1)
                        act.activation(PT[:, k0:6, :].rearrange("p k n -> p (k n)"), pT[:, keys], ACT.Copy).then_inc(moved, 1)
                        for unit in later:
                            exp(*unit)
                        later = []
                        if i < diff:
                            exp(i + 2, 0)
                            exp(i + 2, 1)
                        elif i < 6:
                            later = [(i + 2, j)]
                        act.wait_ge(pv, R * n + c + 1)
                        if i < diff:
                            act.activation(o[:, i * P:(i + 1) * P], pO[c % 2][:, 0:P], ACT.Copy).then_inc(o_out, 1)
                        else:
                            act.wait_ge(r_ready[j], (8 - diff) * n + i - diff + 1)
                            act.activation(o[:, i * P + j * HD:i * P + (j + 1) * HD], pO[c % 2][:, 0:HD], ACT.Copy,
                                           scale=st[:, i % 3, j, 4:5]).then_inc(o_out, 1)
                if diff:
                    act.wait_ge(ss_ready, n + 1)
                    act.activation(ss[:], ss[:], ACT.Sqrt, scale=1.0 / P, bias=eps[:, 1:2]).then_inc(ss_root, 1)
                act.wait_ge(bigT, n + 1)
                act.activation(oT[:, 0:4, :].rearrange("p k n -> p (k n)"), pT[:, 0:512], ACT.Copy).then_inc(bigA, 1)
                act.wait_ge(q_used, n + 1)
                copy_queries(n + 1)
                act.wait_ge(var_ready, n + 1)
                act.activation(root[:], mv[:, 1:2], ACT.Sqrt, bias=eps[:, 0:1]).then_inc(root_ready, 1)
            for t in range(total, 2 * total):
                act.wait_ge(bigT, t + 1)
                act.activation(oT[:, 0:4, :].rearrange("p k n -> p (k n)"), pT[:, 0:512], ACT.Copy).then_inc(bigA, 1)

        @block.vector
        def _(dve):
            step = Steps(dve, order)
            dve.sem_inc(merged, 1)
            dve.sem_inc(summed_up, 1)
            dve.sem_inc(h_stored, 16)
            dve.memset(eps[:, 0:1], LN_EPS)
            dve.memset(eps[:, 1:2], RMS_EPS).then_inc(const_set, 1)
            dve.wait_ge(first_in, 32)
            if diff:
                for j in range(2):
                    last = dve.tensor_tensor_reduce(lv[:, 2 * j], lv[:, 2 * j], lv[:, 2 * j + 1], 1.0, 0.0, ALU.mult, ALU.add, lam[:, j:j + 1])
                last.then_inc(lam_sum, 1)
                dve.wait_ge(lam_exp, 1)
                step(dve.tensor_tensor(lam[:, 4:5], lam[:, 3:4], lam[:, 2:3], ALU.subtract))
                step(dve.tensor_scalar(lam[:, 5:6], lam[:, 4:5], -LAM_INIT, None, ALU.add))
                step(dve.tensor_scalar(sub_g[:], sub_g[:], 1.0 - LAM_INIT, None, ALU.mult))
            for n, t, v, k0, nk in tiles(dve):
                step.restart()
                keys = slice(k0 * P, TOK)

                def shift(i, b):
                    s = st[:, i % 3, b]
                    dve.wait_ge(scored[b], 8 * n + i + 1)
                    if l == 0:
                        step(dve.tensor_reduce(s[:, 0:1], pS[b][:, keys], AX.X, ALU.max))
                        dve.tensor_scalar(s[:, 1:2], s[:, 0:1], -SCALE, None, ALU.mult).then_inc(shifted[b], 1)
                        return
                    e = E[:, i % 2, b]
                    if i < 4:
                        bias = wmask[:, ds(t, 1), :].rearrange("p o n -> p (o n)")
                    else:
                        bias = na_bias[:, 2 * (i - 4) + b, ds(6 - 2 * t, 8), :].rearrange("p a n -> p (a n)")
                    dve.scalar_tensor_tensor(out=e[:, 0:512], in0=pS[b][:, 0:512], scalar=SCALE, in1=bias, op0=ALU.mult, op1=ALU.add)
                    dve.tensor_scalar(e[:, 512:768], pS[b][:, 512:768], SCALE, None, ALU.mult).then_inc(s_free[b], 1)
                    dve.wait_ge(s_free[b], 8 * n + i + 2)
                    step(dve.tensor_reduce(s[:, 0:1], e[:, :], AX.X, ALU.max))
                    if i < 4:
                        step(dve.tensor_tensor(s[:, 0:1], s[:, 0:1], sink[:, 2 * i + b:2 * i + b + 1], ALU.max))
                    dve.tensor_scalar(s[:, 1:2], s[:, 0:1], -1.0, None, ALU.mult).then_inc(shifted[b], 1)

                for i in range(2):
                    for b in range(2):
                        shift(i, b)
                def shares(i):
                    s = st[:, i % 3]
                    for b in range(2):
                        dve.wait_ge(e_ready[b], 8 * n + i + 1)
                        if l == 1 and i < 4:
                            step(dve.tensor_tensor(s[:, b, 2:3], s[:, b, 2:3], s[:, b, 3:4], ALU.add))
                        if i < diff:
                            step(dve.reciprocal(s[:, b, 4:5], s[:, b, 2:3]))
                        else:
                            dve.reciprocal(s[:, b, 4:5], s[:, b, 2:3]).then_inc(r_ready[b], 1)
                    if i < diff:
                        step(dve.tensor_tensor(s[:, 1, 5:6], s[:, 1, 4:5], lam[:, 5:6], ALU.mult))
                        if i >= 2:
                            dve.wait_ge(turned, R * n + i - 1)
                        step(dve.tensor_scalar(a[:, i % 2, keys], E[:, i % 2, 0, keys], s[:, 0, 4:5], None, ALU.mult))
                        dve.scalar_tensor_tensor(out=a[:, i % 2, keys], in0=E[:, i % 2, 1, keys], scalar=s[:, 1, 5:6],
                                                 in1=a[:, i % 2, keys], op0=ALU.mult, op1=ALU.add).then_inc(a_ready, 1)

                shares(0)
                for i in range(8):
                    if i < 7:
                        shares(i + 1)
                    for j, c in enumerate(rounds(i)):
                        if l == 1:
                            dve.wait_ge(turned, R * n + c + 1)
                        if i < 6:
                            for b in ([0, 1] if i < diff else [j]):
                                shift(i + 2, b)
                dve.wait_ge(o_out, R * (n + 1) + 2)
                if diff:
                    for hd in range(4):
                        oh = o[:, hd * P:(hd + 1) * P]
                        last = dve.tensor_tensor_reduce(a[:, 0, hd * P:(hd + 1) * P], oh, oh, 1.0, 0.0, ALU.mult, ALU.add, ss[:, hd:hd + 1])
                    last.then_inc(ss_ready, 1)
                    dve.wait_ge(ss_root, n + 1)
                    step(dve.reciprocal(ss[:], ss[:]))
                    for hd in range(4):
                        oh = o[:, hd * P:(hd + 1) * P]
                        last = dve.scalar_tensor_tensor(out=oh, in0=oh, scalar=ss[:, hd:hd + 1], in1=sub_g[:], op0=ALU.mult, op1=ALU.mult)
                    last.then_inc(o_ready, 1)
                else:
                    dve.sem_inc(o_ready, 1)
                dve.wait_ge(bigT, n + 1)
                dve.tensor_copy(oT[:, 4:8, :].rearrange("p k n -> p (k n)"), pT[:, 512:1024]).then_inc(bigD, 1)
                dve.wait_ge(mixed, n + 1)
                dve.wait_ge(const_in, 16 * n_const)
                dve.wait_ge(h_in, 16 * (n + 1))
                dve.wait_ge(h_stored, 16 * (n + 1))
                dve.wait_ge(f_free, n + 1)
                step(dve.tensor_tensor(r[:], pS[0][:, :], mrow[:, v, 0], ALU.mult))
                dve.sem_inc(merged, 1)
                step(dve.scalar_tensor_tensor(out=r[:], in0=h[:], scalar=ALPHA, in1=r[:], op0=ALU.mult, op1=ALU.add))
                dve.sem_inc(summed_up, 1)
                dve.bn_stats(bn[:, 0, :], r[:, 0:512])
                step(dve.bn_stats(bn[:, 1, :], r[:, 512:1024]))
                dve.bn_aggr(mv[:, 0:2], bn[:]).then_inc(var_ready, 1)
                dve.wait_ge(root_ready, n + 1)
                dve.tensor_copy(mv[:, 2:3], mv[:, 0:1])
                dve.reciprocal(mv[:, 3:4], root[:]).then_inc(rstd_ready, 1)
            for t in range(total, 2 * total):
                dve.wait_ge(bigT, t + 1)
                dve.tensor_copy(oT[:, 4:8, :].rearrange("p k n -> p (k n)"), pT[:, 512:1024]).then_inc(bigD, 1)
            dve.wait_ge(routed, 1)
            dve.tensor_tensor(logits[:, 0:total, :], pS[0][:, 0:36 * total].rearrange("p (t n) -> p t n", n=36),
                              rb[:].rearrange("p (o n) -> p o n", o=1).broadcast_to([P, total, 36]), ALU.add)


def layer_norm_rows(dve, step, r, f, bn, mv, lrow, var_ready, root_ready, n):
    dve.bn_stats(bn[:, 0, :], r[:, 0:512])
    step(dve.bn_stats(bn[:, 1, :], r[:, 512:1024]))
    dve.bn_aggr(mv[:, 0:2], bn[:]).then_inc(var_ready, 1)
    dve.wait_ge(root_ready, n + 1)
    step(dve.reciprocal(mv[:, 3:4], mv[:, 2:3]))
    step(dve.tensor_scalar(f[:], r[:], mv[:, 0:1], mv[:, 3:4], ALU.subtract, ALU.mult))
    step(dve.tensor_tensor(f[:], f[:], lrow[:, 0], ALU.mult))


BIG = 1 << 20


def large_items(nt):
    n = 2 * nt * P // (HD + 1)
    return n + n % 2


def blocks(nt):
    return large_items(nt) + NE // 2


def routing_phase(nc, g, nt, logits, share, gather_at, scatter_at, expert_of, pairs_of):
    T = nt * P
    NL, NW = large_items(nt), blocks(nt)
    with Phase(nc) as ph:
        x = ph.sb("x", [P, nt, NE])
        ohg = ph.sb("ohg", [P, nt, NG])
        oh = ph.sb("oh", [P, 2, nt, NE])
        both = ph.sb("both", [P, nt, NE])
        tmp = ph.sb("tmp", [P, nt, NE])
        vals = ph.sb("vals", [P, 2, nt, 3, NW])
        m = ph.sb("m", [P, nt, 12])
        rank = ph.sb("rank", [P, 2, nt])
        place = ph.sb("place", [P, 2, nt])
        item = ph.sb("item", [P, 2, nt])
        own = ph.sb("own", [P, 3, 2, nt])
        whole = ph.sb("whole", [P, 2, nt])
        large = ph.sb("large", [P, 2, nt])
        half = ph.sb("half", [P, 2, nt])
        small = ph.sb("small", [P, 2, 2, nt])
        integer = ph.sb("integer", [P, 2, nt], I32)
        slot = ph.sb("slot", [P, 2, P])
        count, token = ph.sb("count", [P, P]), ph.sb("token", [P, NTILE])
        down = ph.sb("down", [P, P])
        ones, earlier = ph.sb("ones", [P, P]), ph.sb("earlier", [P, P])
        cut = ph.sb("cut", [P, 3, 2, NE])
        blocks_i = ph.sb("blocks_i", [P, 2, NE], I32)
        past = ph.sb("past", [P, NL + NE, NE])
        ids = ph.sb("ids", [P, NL + NE])
        total = ph.sb("total", [P, 2])
        number = ph.sb("number", [P, 2], I32)
        table = ph.sb("table", [P, 3, NW])
        pR = ph.ps("pR", [P, nt + 1, NE])
        pV = ph.ps("pV", [P, 3 * NW])
        const_in, exp_in, exp_out, used, ranked, slotted, slot_used = (
            ph.sem(n) for n in ("const_in", "exp_in", "exp_out", "used", "ranked", "slotted", "slot_used"))
        order = ph.sem("order")
        block = ph.block()

        @block.sync
        def _(sp):
            ph.clear_other_pool(sp)
            for dst, src in ((count, "count"), (token, "token"), (ones, "ones"), (earlier, "earlier")):
                sp.dma_start(dst[:], g[src]).then_inc(const_in, 16)

        @block.scalar
        def _(act):
            act.wait_ge(exp_in, 1)
            act.activation(m[:, :, 4:8], m[:, :, 4:8], ACT.Exp).then_inc(exp_out, 1)
            act.wait_ge(exp_in, 2)
            act.activation(m[:, :, 9:10], m[:, :, 9:10], ACT.Exp).then_inc(exp_out, 1)

        @block.tensor
        def _(pe):
            pe.wait_ge(const_in, 64)
            pe.wait_ge(used, 1)
            for t in range(nt + 1):
                for s in range(t):
                    last = pe.matmul(pR[:, t, :], ones[:], both[:, s, :], start=(s == 0), stop=(t == nt and s == nt - 1))
                if t < nt:
                    last = pe.matmul(pR[:, t, :], earlier[:], both[:, t, :], start=(t == 0), stop=True)
            last.then_inc(ranked, 1)
            for i in range(2 * nt):
                k, t = i % 2, i // 2
                pe.wait_ge(slotted, i + 1)
                pe.matmul(pV[:, :], slot[:, k, :], vals[:, k, t].rearrange("p a w -> p (a w)"),
                          start=(i == 0), stop=(i == 2 * nt - 1)).then_inc(slot_used, 1)

        @block.vector
        def _(dve):
            step = Steps(dve, order)
            dve.wait_ge(const_in, 64)
            gl = logits[:, 0:nt, 0:NG]
            el = logits[:, 0:nt, NG:36]

            def wide(ap, n):
                return ap.broadcast_to([P, nt, n])

            def row(ap, n):
                return ap.rearrange("p (o n) -> p o n", o=1).broadcast_to([P, nt, n])

            def first_max(src, n, m_at, out):
                step(dve.tensor_reduce(m[:, :, m_at:m_at + 1], src, AX.X, ALU.max))
                step(dve.tensor_tensor(tmp[:, :, 0:n], src, wide(m[:, :, m_at:m_at + 1], n), ALU.is_equal))
                step(dve.tensor_tensor(tmp[:, :, 0:n], tmp[:, :, 0:n], row(down[:, 0:n], n), ALU.mult))
                step(dve.tensor_reduce(m[:, :, 8:9], tmp[:, :, 0:n], AX.X, ALU.max))
                step(dve.tensor_tensor(out, tmp[:, :, 0:n], wide(m[:, :, 8:9], n), ALU.is_equal))

            step(dve.tensor_scalar(down[:], count[:], -1.0, float(P), ALU.mult, ALU.add))
            first_max(gl, NG, 0, ohg[:])
            dve.tensor_tensor(m[:, :, 4:8], gl, wide(m[:, :, 0:1], NG), ALU.subtract).then_inc(exp_in, 1)
            step(dve.tensor_scalar(ohg[:], ohg[:], -1.0, -NEG, ALU.add, ALU.mult))
            for e in range(NG):
                step(dve.tensor_tensor(x[:, :, e * EPG:(e + 1) * EPG], el[:, :, e * EPG:(e + 1) * EPG],
                                       wide(ohg[:, :, e:e + 1], EPG), ALU.add))
            first_max(x[:], NE, 1, oh[:, 0])
            step(dve.tensor_scalar(both[:], oh[:, 0], -1e38, None, ALU.mult))
            step(dve.tensor_tensor(x[:], x[:], both[:], ALU.add))
            first_max(x[:], NE, 2, oh[:, 1])
            dve.tensor_tensor(both[:], oh[:, 0], oh[:, 1], ALU.add).then_inc(used, 1)
            dve.tensor_tensor(m[:, :, 9:10], m[:, :, 2:3], m[:, :, 1:2], ALU.subtract).then_inc(exp_in, 1)
            dve.wait_ge(exp_out, 1)
            step(dve.tensor_reduce(m[:, :, 10:11], m[:, :, 4:8], AX.X, ALU.add))
            dve.wait_ge(exp_out, 2)
            step(dve.tensor_scalar(m[:, :, 11:12], m[:, :, 9:10], 1.0, None, ALU.add))
            step(dve.tensor_tensor(m[:, :, 10:11], m[:, :, 10:11], m[:, :, 11:12], ALU.mult))
            step(dve.reciprocal(share[:, 0:nt, 0:1], m[:, :, 10:11]))
            step(dve.tensor_tensor(share[:, 0:nt, 1:2], share[:, 0:nt, 0:1], m[:, :, 9:10], ALU.mult))
            dve.wait_ge(ranked, 1)
            for j in range(2):
                step(dve.tensor_scalar(cut[:, 1, j], pR[:, nt, :], float(HD - 1 + j * HD), None, ALU.add))
            step(dve.tensor_copy(blocks_i[:], cut[:, 1]))
            step(dve.tensor_scalar(blocks_i[:], blocks_i[:], 7, None, ALU.arith_shift_right))
            step(dve.tensor_copy(cut[:, 0], blocks_i[:]))
            step(dve.tensor_tensor(cut[:, 0, 1], cut[:, 0, 1], cut[:, 0, 0], ALU.subtract))
            for j in range(2):
                step(dve.tensor_tensor_scan(cut[:, 1, j], ones[:, 0:NE], cut[:, 0, j], 0.0, ALU.mult, ALU.add))
            step(dve.tensor_tensor(cut[:, 2], cut[:, 1], cut[:, 0], ALU.subtract))
            for k in range(2):
                step(dve.tensor_tensor(tmp[:], oh[:, k], pR[:, 0:nt, :], ALU.mult))
                step(dve.tensor_reduce(rank[:, k].rearrange("p (t o) -> p t o", o=1), tmp[:], AX.X, ALU.add))
                for j, of in enumerate((cut[:, 0, 0], cut[:, 2, 0], cut[:, 2, 1])):
                    step(dve.tensor_tensor(tmp[:], oh[:, k], row(of, NE), ALU.mult))
                    step(dve.tensor_reduce(own[:, j, k].rearrange("p (t o) -> p t o", o=1), tmp[:], AX.X, ALU.add))

            def shifted(out, src, bits):
                step(dve.tensor_copy(integer[:], src))
                step(dve.tensor_scalar(integer[:], integer[:], bits, None, ALU.arith_shift_right))
                step(dve.tensor_copy(out, integer[:]))

            shifted(whole[:], rank[:], 7)
            shifted(half[:], own[:, 2], 1)
            step(dve.tensor_tensor(large[:], whole[:], own[:, 0], ALU.is_lt))
            step(dve.scalar_tensor_tensor(out=small[:, 0], in0=own[:, 0], scalar=-float(P), in1=rank[:], op0=ALU.mult, op1=ALU.add))
            step(dve.scalar_tensor_tensor(out=small[:, 0], in0=own[:, 2], scalar=float(HD), in1=small[:, 0], op0=ALU.mult, op1=ALU.add))
            step(dve.scalar_tensor_tensor(out=small[:, 0], in0=half[:], scalar=-float(P), in1=small[:, 0], op0=ALU.mult, op1=ALU.add))
            step(dve.tensor_scalar(small[:, 1], half[:], float(NL), None, ALU.add))
            step(dve.scalar_tensor_tensor(out=place[:], in0=whole[:], scalar=-float(P), in1=rank[:], op0=ALU.mult, op1=ALU.add))
            step(dve.tensor_tensor(item[:], own[:, 1], whole[:], ALU.add))
            for to, j in ((place, 0), (item, 1)):
                step(dve.tensor_tensor(to[:], to[:], small[:, j], ALU.subtract))
                step(dve.tensor_tensor(to[:], to[:], large[:], ALU.mult))
                step(dve.tensor_tensor(to[:], to[:], small[:, j], ALU.add))
            for i in range(2 * nt):
                k, t = i % 2, i // 2
                v = vals[:, k, t]
                step(dve.tensor_scalar(v[:, 1, :], count[:, 0:NW], item[:, k, t:t + 1], None, ALU.is_equal))
                dve.tensor_scalar(v[:, 0, :], v[:, 1, :], token[:, t:t + 1], None, ALU.mult)
                dve.tensor_scalar(v[:, 2, :], v[:, 1, :], float(k * T), None, ALU.mult)
                if i >= 2:
                    dve.wait_ge(slot_used, i - 1)
                dve.tensor_scalar(slot[:, k, :], count[:], place[:, k, t:t + 1], None, ALU.is_equal).then_inc(slotted, 1)
            for j, (at, n) in enumerate(((0, NL), (NL, NE))):
                step(dve.tensor_tensor(past[:, at:at + n], count[:, 0:n].rearrange("p (w o) -> p w o", o=1).broadcast_to([P, n, NE]),
                                       cut[:, 1, j].rearrange("p (o e) -> p o e", o=1).broadcast_to([P, n, NE]), ALU.is_ge))
            step(dve.tensor_reduce(ids[:].rearrange("p (w o) -> p w o", o=1), past[:], AX.X, ALU.add))
            step(dve.tensor_scalar(ids[:], ids[:], float(NE - 1), None, ALU.min))
            step(dve.tensor_copy(expert_of[:, 0:NL + NE], ids[:]))
            step(dve.tensor_scalar(total[:], cut[:, 1, :, NE - 1:NE].rearrange("p j o -> p (j o)"), 1.0, 2.0, ALU.add, ALU.max))
            step(dve.tensor_copy(number[:], total[:]))
            step(dve.tensor_scalar(pairs_of[:], number[:], 1, None, ALU.arith_shift_right))
            step(dve.memset(gather_at[:, NW:NW + 2], 0))
            dve.wait_ge(slot_used, 2 * nt)
            step(dve.tensor_copy(table[:].rearrange("p a w -> p (a w)"), pV[:, :]))
            step(dve.tensor_copy(gather_at[:, 0:NW], table[:, 0]))
            step(dve.tensor_tensor(table[:, 0], table[:, 0], table[:, 2], ALU.add))
            step(dve.tensor_scalar(table[:, 1], table[:, 1], -float(BIG), float(BIG), ALU.mult, ALU.add))
            step(dve.tensor_tensor(table[:, 0], table[:, 0], table[:, 1], ALU.add))
            step(dve.tensor_copy(scatter_at[:, 0:NW], table[:, 0]))


def large_item_phase(nc, g, l, nt, gather_at, scatter_at, expert_of, pairs_of):
    T = nt * P
    HC = DE // P
    NW = large_items(nt)
    with Phase(nc) as ph:
        w1, w3 = ph.sb("w1", [P, 2, C, DE]), ph.sb("w3", [P, 2, C, DE])
        w2 = ph.sb("w2", [P, 2, HC, D])
        at = ph.sb("at", [P, 2, 2], I32)
        x = ph.sb("x", [P, 2, D])
        xT = ph.sb("xT", [P, 2, C, P])
        hs = ph.sb("hs", [P, 2, DE])
        hh = ph.sb("hh", [P, 2, DE])
        hT = ph.sb("hT", [P, 2, HC, P])
        y = ph.sb("y", [P, 2, D])
        pT = [ph.ps(f"pT{i}", [P, 512]) for i in range(2)]
        pH = [[ph.ps(f"pH{b}{k}", [P, DE]) for k in range(2)] for b in range(2)]
        pY = ph.ps("pY", [P, 1024])
        w13_in, w2_in, y_free, hidden, gated, silu, multiplied = (
            ph.sems(n) for n in ("w13_in", "w2_in", "y_free", "hidden", "gated", "silu", "multiplied"))
        x_in, y_out = ([ph.stack.enter_context(nc.semaphore(f"{n}{b}_{l}", num=Phase.FIRST - 12 + 4 * l + 2 * i + b)) for b in range(2)]
                       for i, n in enumerate(("x_in", "y_out")))
        turned, moved = ph.sems("turned"), ph.sems("moved")
        yA, yD, order = (ph.sem(n) for n in ("yA", "yD", "order"))
        block = ph.block()
        ident = g["ident"]
        QUADS = [(0, "h", 0, 0), (1, "x", 0, 0), (0, "x", 0, 4), (1, "h", 1, 0), (0, "x", 1, 0), (1, "x", 1, 4)]
        HEAD = [(0, "x", 0, 0), (1, "x", 0, 4), (0, "x", 1, 0), (1, "x", 1, 4)]

        def pair_loop(eng):
            n = eng.value_load(pairs_of[0:1, 0:1], min_val=1, max_val=NW // 2)
            with eng.Fori(0, n) as p:
                yield p

        def empty(eng, bank, quads, at0):
            for r, (_, what, b, k0) in enumerate([q for q in quads if q[0] == bank]):
                yield at0 + r, what, b, (xT[:, b, k0:k0 + 4] if what == "x" else hT[:, b]).rearrange("p k n -> p (k n)")

        @block.sync
        def _(sp):
            ph.clear_other_pool(sp)
            for p in pair_loop(sp):
                for b in range(2):
                    e = sp.value_load(expert_of[0:1, ds(2 * p + b, 1)], min_val=0, max_val=NE - 1)
                    sp.wait_ge(hidden[b], p + 1)
                    for dst, src in ((w1, "moe_w1"), (w3, "moe_w3")):
                        sp.dma_start(dst[:, b], g[src][l, ds(e, 1)].rearrange("o (p k) n -> p (o k) n", p=P)).then_inc(w13_in[b], 16)
                    sp.wait_ge(multiplied[b], p + 1)
                    sp.dma_start(w2[:, b], g["moe_w2"][l, ds(e, 1)].rearrange("o (p k) n -> p (o k) n", p=P)).then_inc(w2_in[b], 16)

        @block.gpsimd
        def _(pool):
            last_row, last_out = pool.to_reg(T - 1), pool.to_reg(2 * T - 1)
            step = Steps(pool, order)

            def gather(p, b):
                step(pool.tensor_copy(at[:, b, 0:1], gather_at[:, ds(2 * p + b, 1)]))
                pool.indirect_dma_start(out=x[:, b], out_offset=None, in_=g["f"][0:T, :],
                                        in_offset=bass.IndirectOffsetOnAxis(ap=at[:, b, 0:1], axis=0),
                                        bounds_check=last_row, oob_is_err=False).then_inc(x_in[b], 16)

            for b in range(2):
                pool.sem_inc(y_free[b], 1)
                gather(0, b)
            for b in range(2):
                for bank in range(2):
                    pool.wait_ge(turned[bank], 1 + b)
                gather(1, b)
            for p in pair_loop(pool):
                step.restart()
                for b in range(2):
                    pool.wait_ge(yA, 2 * p + b + 2)
                    pool.wait_ge(yD, 2 * p + b + 2)
                    step(pool.tensor_copy(at[:, b, 1:2], scatter_at[:, ds(2 * p + b, 1)]))
                    pool.indirect_dma_start(out=g["y"][0:2 * T, :], out_offset=bass.IndirectOffsetOnAxis(ap=at[:, b, 1:2], axis=0),
                                            in_=y[:, b], in_offset=None, bounds_check=last_out, oob_is_err=False).then_inc(y_out[b], 16)
                    pool.wait_ge(turned[0], 3 * p + 4 + b)
                    pool.wait_ge(turned[1], 3 * p + 3 + 2 * b)
                    gather(p + 2, b)
                for b in range(2):
                    pool.wait_ge(y_out[b], 16 * (p + 1))
                    pool.sem_inc(y_free[b], 1)
                    pool.wait_ge(x_in[b], 16 * (p + 3))

        @block.tensor
        def _(pe):
            def turn(bank, what, b, k0, r):
                src = (lambda k: x[:, b, k::C]) if what == "x" else (lambda k: hh[:, b, k::HC])
                if r is not None:
                    pe.wait_ge(moved[bank], r)
                for k in range(4):
                    last = pe.transpose(pT[bank][:, k * P:(k + 1) * P], src(k0 + k), ident[:])
                last.then_inc(turned[bank], 1)

            for b in range(2):
                pe.sem_inc(hidden[b], 1)
                pe.sem_inc(multiplied[b], 1)
            for i, (bank, what, b, k0) in enumerate(HEAD):
                pe.wait_ge(x_in[b], 16)
                turn(bank, what, b, k0, i // 2 if i >= 2 else None)
            for p in pair_loop(pe):
                for b in range(2):
                    pe.wait_ge(w13_in[b], 32 * (p + 1))
                    pe.wait_ge(gated[b], p + 1)
                    pe.wait_ge(moved[0], 3 * p + 1 + b)
                    pe.wait_ge(moved[1], 3 * p + 1 + b)
                    for i, w in enumerate((w1, w3)):
                        for k in range(C):
                            last = pe.matmul(pH[b][i][:], xT[:, b, k, :], w[:, b, k, :], start=(k == 0), stop=(k == C - 1))
                    last.then_inc(hidden[b], 1)
                for b in range(2):
                    pe.wait_ge(gated[b], p + 2)
                    pe.wait_ge(x_in[b], 16 * (p + 2))
                    for j in range(3):
                        i = 3 * b + j
                        turn(*QUADS[i], 3 * p + 2 + i // 2)
                    pe.wait_ge(moved[b], 3 * p + 3 + b)
                    pe.wait_ge(w2_in[b], 16 * (p + 1))
                    pe.wait_ge(yA, 2 * p + b + 1)
                    pe.wait_ge(yD, 2 * p + b + 1)
                    for i in range(2):
                        for k in range(HC):
                            last = pe.matmul(pY[:, i * 512:(i + 1) * 512], hT[:, b, k, :], w2[:, b, k, i * 512:(i + 1) * 512],
                                             start=(k == 0), stop=(k == HC - 1))
                    last.then_inc(multiplied[b], 1)

        @block.scalar
        def _(act):
            act.sem_inc(yA, 1)
            for r, what, b, to in empty(act, 0, HEAD, 1):
                act.wait_ge(turned[0], r)
                act.activation(to, pT[0][:], ACT.Copy).then_inc(moved[0], 1)
            for p in pair_loop(act):
                for b in range(2):
                    act.wait_ge(hidden[b], p + 2)
                    act.activation(hs[:, b], pH[b][0][:], ACT.Silu).then_inc(silu[b], 1)
                quads = list(empty(act, 0, QUADS, 3))
                for b in range(2):
                    for r, what, _, to in (quads[:2] if b == 0 else quads[2:]):
                        act.wait_ge(turned[0], 3 * p + r)
                        act.activation(to, pT[0][:], ACT.Copy).then_inc(moved[0], 1)
                    act.wait_ge(multiplied[b], p + 2)
                    act.wait_ge(y_free[b], p + 1)
                    act.activation(y[:, b, 0:512], pY[:, 0:512], ACT.Copy).then_inc(yA, 1)

        @block.vector
        def _(dve):
            dve.sem_inc(yD, 1)
            for b in range(2):
                dve.sem_inc(gated[b], 1)
            for r, what, b, to in empty(dve, 1, HEAD, 1):
                dve.wait_ge(turned[1], r)
                dve.tensor_copy(to, pT[1][:]).then_inc(moved[1], 1)
            for p in pair_loop(dve):
                for b in range(2):
                    dve.wait_ge(silu[b], p + 1)
                    dve.tensor_tensor(hh[:, b], hs[:, b], pH[b][1][:], ALU.mult).then_inc(gated[b], 1)
                quads = list(empty(dve, 1, QUADS, 3))
                for b in range(2):
                    for r, what, _, to in (quads[:1] if b == 0 else quads[1:]):
                        dve.wait_ge(turned[1], 3 * p + r)
                        dve.tensor_copy(to, pT[1][:]).then_inc(moved[1], 1)
                    dve.wait_ge(multiplied[b], p + 2)
                    dve.wait_ge(y_free[b], p + 1)
                    dve.tensor_copy(y[:, b, 512:1024], pY[:, 512:1024]).then_inc(yD, 1)


def small_item_phase(nc, g, l, nt, gather_at, scatter_at, expert_of, pairs_of):
    T = nt * P
    HC = DE // P
    NL = large_items(nt)
    with Phase(nc) as ph:
        w1, w3 = ph.sb("w1", [P, 2, C, DE]), ph.sb("w3", [P, 2, C, DE])
        w2 = ph.sb("w2", [P, 2, HC, D])
        at = ph.sb("at", [P, 2], I32)
        x = ph.sb("x", [P, D])
        xT = ph.sb("xT", [P, C, P])
        hs, hh = ph.sb("hs", [P, DE]), ph.sb("hh", [P, DE])
        hT = ph.sb("hT", [P, HC, P])
        y = ph.sb("y", [P, D])
        pX = [ph.ps(f"pX{i}", [P, 512]) for i in range(2)]
        pT = ph.ps("pT", [P, 512])
        pH = [ph.ps(f"pH{i}", [P, DE]) for i in range(2)]
        pY = [ph.ps(f"pY{i}", [P, 512]) for i in range(2)]
        w_in, used = ([ph.sem(f"{n}{i}") for i in range(3)] for n in ("w_in", "used"))
        x_turned, x_moved, y_moved = ph.sems("x_turned"), ph.sems("x_moved"), ph.sems("y_moved")
        silu, gated, h_turned, h_moved, y_free, order = (
            ph.sem(n) for n in ("silu", "gated", "h_turned", "h_moved", "y_free", "order"))
        x_in, y_out = (ph.stack.enter_context(nc.semaphore(f"small_{n}_{l}", num=Phase.FIRST - 4 + 2 * l + i))
                       for i, n in enumerate(("x_in", "y_out")))
        block = ph.block()
        ident = g["ident"]

        def pair_loop(eng):
            n = eng.value_load(pairs_of[0:1, 1:2], min_val=1, max_val=NE // 2)
            with eng.Fori(0, n) as p:
                yield p

        def strip(b):
            return slice(b * HD, (b + 1) * HD)

        @block.sync
        def _(sp):
            ph.clear_other_pool(sp)
            for p in pair_loop(sp):
                e = [sp.value_load(expert_of[0:1, ds(2 * p + NL + b, 1)], min_val=0, max_val=NE - 1) for b in range(2)]
                for i, (dst, src) in enumerate(((w1, "moe_w1"), (w3, "moe_w3"), (w2, "moe_w2"))):
                    sp.wait_ge(used[i], p + 1)
                    for b in range(2):
                        sp.dma_start(dst[:, b], g[src][l, ds(e[b], 1)].rearrange("o (p k) n -> p (o k) n", p=P)).then_inc(w_in[i], 16)

        @block.gpsimd
        def _(pool):
            last_row, last_out = pool.to_reg(T - 1), pool.to_reg(2 * T - 1)
            step = Steps(pool, order)

            def gather(p):
                step(pool.tensor_copy(at[:, 0:1], gather_at[:, ds(p + NL, 1)]))
                pool.indirect_dma_start(out=x[:], out_offset=None, in_=g["f"][0:T, :],
                                        in_offset=bass.IndirectOffsetOnAxis(ap=at[:, 0:1], axis=0),
                                        bounds_check=last_row, oob_is_err=False).then_inc(x_in, 16)

            pool.sem_inc(y_free, 1)
            gather(0)
            for i in range(2):
                pool.wait_ge(x_turned[i], 1)
            gather(1)
            for p in pair_loop(pool):
                step.restart()
                for i in range(2):
                    pool.wait_ge(y_moved[i], p + 2)
                step(pool.tensor_copy(at[:, 1:2], scatter_at[:, ds(p + NL, 1)]))
                pool.indirect_dma_start(out=g["y"][0:2 * T, :], out_offset=bass.IndirectOffsetOnAxis(ap=at[:, 1:2], axis=0),
                                        in_=y[:], in_offset=None, bounds_check=last_out, oob_is_err=False).then_inc(y_out, 16)
                for i in range(2):
                    pool.wait_ge(x_turned[i], p + 2)
                gather(p + 2)
                pool.wait_ge(y_out, 16 * (p + 1))
                pool.sem_inc(y_free, 1)
                pool.wait_ge(x_in, 16 * (p + 3))

        @block.tensor
        def _(pe):
            def turn_x():
                for i in range(2):
                    for k in range(4):
                        last = pe.transpose(pX[i][:, k * P:(k + 1) * P], x[:, i * 4 + k::C], ident[:])
                    last.then_inc(x_turned[i], 1)

            for s in used + y_moved + [gated]:
                pe.sem_inc(s, 1)
            pe.wait_ge(x_in, 16)
            turn_x()
            for p in pair_loop(pe):
                for i in range(2):
                    pe.wait_ge(x_moved[i], p + 1)
                pe.wait_ge(gated, p + 1)
                for i, w in enumerate((w1, w3)):
                    pe.wait_ge(w_in[i], 32 * (p + 1))
                    for k in range(C):
                        for b in range(2):
                            last = pe.matmul(pH[i][strip(b), :], xT[:, k, strip(b)], w[:, b, k, :], start=(k == 0), stop=(k == C - 1))
                    last.then_inc(used[i], 1)
                pe.wait_ge(x_in, 16 * (p + 2))
                turn_x()
                pe.wait_ge(gated, p + 2)
                for k in range(HC):
                    last = pe.transpose(pT[:, k * P:(k + 1) * P], hh[:, k::HC], ident[:])
                last.then_inc(h_turned, 1)
                pe.wait_ge(h_moved, p + 1)
                pe.wait_ge(w_in[2], 32 * (p + 1))
                for i in range(2):
                    pe.wait_ge(y_moved[i], p + 1)
                    for k in range(HC):
                        for b in range(2):
                            last = pe.matmul(pY[i][strip(b), :], hT[:, k, strip(b)], w2[:, b, k, i * 512:(i + 1) * 512],
                                             start=(k == 0), stop=(k == HC - 1))
                last.then_inc(used[2], 1)

        @block.scalar
        def _(act):
            act.wait_ge(x_turned[0], 1)
            act.activation(xT[:, 0:4].rearrange("p k n -> p (k n)"), pX[0][:], ACT.Copy).then_inc(x_moved[0], 1)
            for p in pair_loop(act):
                act.wait_ge(used[0], p + 2)
                act.activation(hs[:], pH[0][:], ACT.Silu).then_inc(silu, 1)
                act.wait_ge(x_turned[0], p + 2)
                act.activation(xT[:, 0:4].rearrange("p k n -> p (k n)"), pX[0][:], ACT.Copy).then_inc(x_moved[0], 1)
                act.wait_ge(used[2], p + 2)
                act.wait_ge(y_free, p + 1)
                act.activation(y[:, 0:512], pY[0][:], ACT.Copy).then_inc(y_moved[0], 1)

        @block.vector
        def _(dve):
            dve.wait_ge(x_turned[1], 1)
            dve.tensor_copy(xT[:, 4:8].rearrange("p k n -> p (k n)"), pX[1][:]).then_inc(x_moved[1], 1)
            for p in pair_loop(dve):
                dve.wait_ge(silu, p + 1)
                dve.wait_ge(used[1], p + 2)
                dve.tensor_tensor(hh[:], hs[:], pH[1][:], ALU.mult).then_inc(gated, 1)
                dve.wait_ge(x_turned[1], p + 2)
                dve.tensor_copy(xT[:, 4:8].rearrange("p k n -> p (k n)"), pX[1][:]).then_inc(x_moved[1], 1)
                dve.wait_ge(h_turned, p + 1)
                dve.tensor_copy(hT[:].rearrange("p k n -> p (k n)"), pT[:]).then_inc(h_moved, 1)
                dve.wait_ge(used[2], p + 2)
                dve.wait_ge(y_free, p + 1)
                dve.tensor_copy(y[:, 512:1024], pY[1][:]).then_inc(y_moved[1], 1)


def combine_phase(nc, g, l, share, out):
    last_l = l == DEPTH - 1
    groups = [(0, NLAT, 0)] + ([] if last_l else [(NLAT, NCTX, 1)])
    T = sum(x[1] for x in groups) * P
    with Phase(nc) as ph:
        yh = ph.sb("yh", [P, 2, 3, D])
        r = ph.sb("r", [P, D])
        f = ph.sb("f", [P, 2, D])
        gate = ph.sb("gate", [P, len(groups), D])
        lrow = ph.sb("lrow", [P, 2, D])
        bn = ph.sb("bn", [P, 2, 6])
        mv = ph.sb("mv", [P, 4])
        eps = ph.sb("eps", [P, 1])
        const_in, eps_set, var_ready, root_ready, order = (ph.sem(n) for n in ("const_in", "eps_set", "var_ready", "root_ready", "order"))
        rows_in, summed, normed, stored = (ph.sems(n) for n in ("rows_in", "summed", "normed", "stored"))
        block = ph.block()

        def pairs(eng):
            for base, n, v in groups:
                with eng.Fori(0, n // 2) as m:
                    yield m + base // 2, v

        @block.sync
        def _(sp):
            ph.clear_other_pool(sp)
            sp.dma_start(lrow[:, 0], g["ln_g"][l, 1:2, :].broadcast_to([P, D])).then_inc(const_in, 16)
            sp.dma_start(lrow[:, 1], g["ln_b"][l, 1:2, :].broadcast_to([P, D])).then_inc(const_in, 16)
            for _, _, v in groups:
                sp.dma_start(gate[:, v], g["mods"][l, v:v + 1, 5 * D:6 * D].broadcast_to([P, D])).then_inc(const_in, 16)
            for n, v in pairs(sp):
                for b in range(2):
                    sp.wait_ge(summed[b], n + 1)
                    rows = n * 2 * P + b * P
                    sp.dma_start(yh[:, b, 0], g["y"][ds(rows, P), :]).then_inc(rows_in[b], 16)
                    sp.dma_start(yh[:, b, 1], g["y"][ds(rows + T, P), :]).then_inc(rows_in[b], 16)
                    sp.dma_start(yh[:, b, 2], g["h_mid"][ds(rows, P), :]).then_inc(rows_in[b], 16)

        @block.scalar
        def _(act):
            for b in range(2):
                act.sem_inc(stored[b], 16)
            act.wait_ge(eps_set, 1)
            for n, v in pairs(act):
                for b in range(2):
                    act.wait_ge(var_ready, 2 * n + b + 1)
                    act.activation(mv[:, 2:3], mv[:, 1:2], ACT.Sqrt, bias=eps[:]).then_inc(root_ready, 1)
                    act.wait_ge(normed[b], n + 1)
                    act.dma_start(out[ds(n * 2 * P + b * P, P), :], f[:, b]).then_inc(stored[b], 16)
            for b in range(2):
                act.wait_ge(stored[b], 16 * (T // P // 2 + 1))

        @block.vector
        def _(dve):
            step = Steps(dve, order)
            for b in range(2):
                dve.sem_inc(summed[b], 1)
            dve.memset(eps[:], LN_EPS).then_inc(eps_set, 1)
            dve.wait_ge(const_in, 16 * (2 + len(groups)))
            for n, v in pairs(dve):
                step.restart()
                for b in range(2):
                    w = share[:, ds(2 * n + b, 1), :].rearrange("p o k -> p (o k)")
                    dve.wait_ge(rows_in[b], 48 * (n + 1))
                    step(dve.tensor_scalar(r[:], yh[:, b, 0], w[:, 0:1], None, ALU.mult))
                    step(dve.scalar_tensor_tensor(out=r[:], in0=yh[:, b, 1], scalar=w[:, 1:2], in1=r[:], op0=ALU.mult, op1=ALU.add))
                    step(dve.tensor_tensor(r[:], r[:], gate[:, v], ALU.mult))
                    dve.scalar_tensor_tensor(out=r[:], in0=yh[:, b, 2], scalar=ALPHA, in1=r[:], op0=ALU.mult, op1=ALU.add).then_inc(summed[b], 1)
                    dve.wait_ge(summed[b], n + 2)
                    dve.wait_ge(stored[b], 16 * (n + 1))
                    layer_norm_rows(dve, step, r, f[:, b], bn, mv, lrow, var_ready, root_ready, n * 2 + b)
                    dve.tensor_tensor(f[:, b], f[:, b], lrow[:, 1], ALU.add).then_inc(normed[b], 1)


EPS2 = 1e-6
GH, GCH = 4, 16
NCH = LAT // GCH
GLA_Q, GLA_V, GLA_A = 256, 512, 16
SC_AT = 2 * GLA_Q + 2 * GLA_V + GLA_A
DIL_AT = SC_AT + 3 * 512
DIL_W = 1536


def norm_turn_phase(nc, g, src, gain, hT):
    with Phase(nc) as ph:
        x = ph.sb("x", [P, 2, D])
        sq = ph.sb("sq", [P, D])
        gcol = ph.sb("gcol", [P, C])
        ss = ph.sb("ss", [P, 2, 2])
        eps = ph.sb("eps", [P, 1])
        pT = [ph.ps(f"pT{i}", [P, 512]) for i in range(2)]
        const_in, eps_set, order, squared = (ph.sem(n) for n in ("const_in", "eps_set", "order", "squared"))
        x_in, rooted, scaled, turned, moved = (ph.sems(n) for n in ("x_in", "rooted", "scaled", "turned", "moved"))
        block = ph.block()

        def pairs(eng):
            with eng.Fori(0, NLAT // 2) as m:
                yield m

        @block.sync
        def _(sp):
            ph.clear_other_pool(sp)
            sp.dma_start(gcol[:], gain[0].rearrange("(p k) -> p k", p=P)).then_inc(const_in, 16)
            for m in pairs(sp):
                for b in range(2):
                    sp.wait_ge(turned[1], 2 * m + b + 1)
                    sp.dma_start(x[:, b], src[ds(m * 2 * P + b * P, P), :]).then_inc(x_in[b], 16)

        @block.scalar
        def _(act):
            act.wait_ge(eps_set, 1)
            act.wait_ge(const_in, 16)
            act.sem_inc(moved[0], 1)
            for m in pairs(act):
                for b in range(2):
                    act.wait_ge(x_in[b], 16 * (m + 1))
                    act.activation(sq[:], x[:, b], ACT.Square, accum_out=ss[:, b, 0:1]).then_inc(squared, 1)
                    act.wait_ge(squared, 2 * m + b + 1)
                    act.activation(ss[:, b, 1:2], ss[:, b, 0:1], ACT.Sqrt, scale=1.0 / D, bias=eps[:]).then_inc(rooted[b], 1)
                    act.wait_ge(turned[0], 2 * m + b + 1)
                    for k in range(4):
                        last = act.activation(hT[:, k, ds(m * 2 * P + b * P, P)], pT[0][:, k * P:(k + 1) * P], ACT.Copy, scale=gcol[:, k:k + 1])
                    last.then_inc(moved[0], 1)

        @block.vector
        def _(dve):
            step = Steps(dve, order)
            dve.memset(eps[:], EPS2).then_inc(eps_set, 1)
            dve.wait_ge(const_in, 16)
            dve.sem_inc(moved[1], 1)
            for m in pairs(dve):
                step.restart()
                for b in range(2):
                    dve.wait_ge(rooted[b], m + 1)
                    step(dve.reciprocal(ss[:, b, 1:2], ss[:, b, 1:2]))
                    dve.tensor_scalar(x[:, b], x[:, b], ss[:, b, 1:2], None, ALU.mult).then_inc(scaled[b], 1)
                    dve.wait_ge(turned[1], 2 * m + b + 3)
                    for k in range(4):
                        last = dve.tensor_scalar(hT[:, 4 + k, ds(m * 2 * P + b * P, P)], pT[1][:, k * P:(k + 1) * P], gcol[:, 4 + k:5 + k], None, ALU.mult)
                    last.then_inc(moved[1], 1)

        @block.tensor
        def _(pe):
            pe.sem_inc(turned[1], 2)
            for m in pairs(pe):
                for b in range(2):
                    pe.wait_ge(scaled[b], m + 1)
                    for h in range(2):
                        pe.wait_ge(moved[h], 2 * m + b + 1)
                        for k in range(4):
                            last = pe.transpose(pT[h][:, k * P:(k + 1) * P], x[:, b, h * 4 + k::C], g["ident"][:])
                        last.then_inc(turned[h], 1)


def angle_tables(act, dve, step, pos, ang, cos, sin, inv, pos_in, angle, tables):
    TURN = 2 * math.pi
    C1 = 6.28125
    C2 = float(np.float32(1.93500518798828125e-3))
    C3 = TURN - C1 - C2
    MAGIC = 1.5 * 2 ** 23
    if dve is not None:
        dve.wait_ge(pos_in, 48)
        step(dve.tensor_copy(ang[:], pos[:]))
        step(dve.tensor_scalar(ang[:], ang[:], inv[:], None, ALU.mult))
        step(dve.tensor_scalar(cos[:], ang[:], 1.0 / TURN, None, ALU.mult))
        step(dve.tensor_scalar(cos[:], cos[:], MAGIC, None, ALU.add))
        step(dve.tensor_scalar(cos[:], cos[:], MAGIC, None, ALU.subtract))
        for c in (C1, C2, C3):
            step(dve.scalar_tensor_tensor(out=ang[:], in0=cos[:], scalar=-c, in1=ang[:], op0=ALU.mult, op1=ALU.add))
        step(dve.tensor_scalar(ang[:], ang[:], 3.1415925, -3.1415925, ALU.min, ALU.max))
        dve.scalar_tensor_tensor(out=cos[:], in0=ang[:], scalar=-1.0, in1=ang[:], op0=ALU.mult, op1=ALU.max).then_inc(angle, 1)
        dve.wait_ge(angle, 1)
        dve.tensor_scalar(cos[:], cos[:], -1.0, math.pi / 2, ALU.mult, ALU.add).then_inc(angle, 1)
    if act is not None:
        act.wait_ge(angle, 2)
        act.activation(sin[:], ang[:], ACT.Sin).then_inc(tables, 1)
        act.activation(cos[:], cos[:], ACT.Sin).then_inc(tables, 1)


def columns_phase(nc, g, hT, col, n, dst, turn=False):
    w_dram = g["w_in_2"][0].rearrange("(p k) n -> p k n", p=P)
    with Phase(nc) as ph:
        w = ph.sb("w", [P, 2, C, P])
        xs = ph.sb("xs", [P, 2, LAT]) if turn else None
        tmp = ph.sb("tmp", [P, 2, 2, LAT]) if turn else None
        rot = ph.sb("rot", [P, P]) if turn else None
        inv = ph.sb("inv", [P, 1]) if turn else None
        pos = ph.sb("pos", [P, LAT], I32) if turn else None
        ang, cos, sin = ([ph.sb(k, [P, LAT]) for k in ("ang", "cos", "sin")]) if turn else (None,) * 3
        pa = [ph.ps(f"pa{b}", [P, 512]) for b in range(2)]
        pr = [ph.ps(f"pr{b}", [P, 512]) for b in range(2)]
        w_in, product, moved, x_ready, rotated = (ph.sems(k) for k in ("w_in", "product", "moved", "x_ready", "rotated"))
        pos_in, angle, tables, order = (ph.sem(k) for k in ("pos_in", "angle", "tables", "order"))
        block = ph.block()

        @block.sync
        def _(sp):
            ph.clear_other_pool(sp)
            if turn:
                sp.dma_start(rot[:], g["rot128"]).then_inc(pos_in, 16)
                sp.dma_start(pos[:], g["positions_2"].broadcast_to([P, LAT])).then_inc(pos_in, 16)
                sp.dma_start(inv[:], g["inv_freq"]).then_inc(pos_in, 16)
            with sp.Fori(0, n // 2) as i:
                for b in range(2):
                    sp.wait_ge(product[b], i + 1)
                    sp.dma_start(w[:, b], w_dram[:, :, ds(i * 2 * P + (col + b * P), P)]).then_inc(w_in[b], 16)

        @block.tensor
        def _(pe):
            for b in range(2):
                pe.sem_inc(product[b], 1)
            if turn:
                pe.wait_ge(pos_in, 48)
            with pe.Fori(0, n // 2) as i:
                for b in range(2):
                    pe.wait_ge(w_in[b], 16 * (i + 1))
                    pe.wait_ge(x_ready[b] if turn else moved[b], i + 1)
                    for k in range(C):
                        last = pe.matmul(pa[b][:], w[:, b, k, :], hT[:, k, :], start=(k == 0), stop=(k == C - 1))
                    last.then_inc(product[b], 1)
                if turn:
                    for b in range(2):
                        pe.wait_ge(x_ready[b], i + 2)
                        pe.wait_ge(moved[b], i + 1)
                        pe.matmul(pr[b][:], rot[:], xs[:, b], start=True, stop=True).then_inc(rotated[b], 1)

        @block.scalar
        def _(act):
            if turn:
                act.sem_inc(x_ready[0], 1)
                act.sem_inc(x_ready[1], 1)
                angle_tables(act, None, None, pos, ang, cos, sin, inv, pos_in, angle, tables)
            else:
                act.sem_inc(moved[0], 1)
            with act.Fori(0, n // 2) as i:
                for b in (0, 1) if turn else (0,):
                    act.wait_ge(product[b], i + 2)
                    if turn:
                        act.wait_ge(moved[b], i + 1)
                        act.activation(xs[:, b], pa[b][:], ACT.Copy).then_inc(x_ready[b], 1)
                    else:
                        act.activation(dst[:, ds(2 * i, 1), :], pa[0][:].rearrange("p (o n) -> p o n", o=1), ACT.Copy).then_inc(moved[0], 1)

        @block.vector
        def _(dve):
            step = Steps(dve, order)
            if turn:
                dve.wait_ge(pos_in, 48)
                angle_tables(None, dve, step, pos, ang, cos, sin, inv, pos_in, angle, tables)
                dve.wait_ge(tables, 2)
                dve.sem_inc(moved[0], 1)
            dve.sem_inc(moved[1], 1)
            with dve.Fori(0, n // 2) as i:
                step.restart()
                if turn:
                    for b in range(2):
                        dve.wait_ge(x_ready[b], i + 2)
                        dve.tensor_tensor(tmp[:, b, 0], xs[:, b], cos[:], ALU.mult)
                        dve.wait_ge(rotated[b], i + 1)
                        step(dve.tensor_tensor(tmp[:, b, 1], pr[b][:], sin[:], ALU.mult))
                        dve.tensor_tensor(dst[:, ds(2 * i + b, 1), :], tmp[:, b, 0:1], tmp[:, b, 1:2], ALU.add).then_inc(moved[b], 1)
                else:
                    dve.wait_ge(product[1], i + 2)
                    dve.tensor_copy(dst[:, ds(2 * i + 1, 1), :], pa[1][:].rearrange("p (o n) -> p o n", o=1)).then_inc(moved[1], 1)


def rows_phase(nc, g, hT, cols, dst):
    w_dram = g["w_in_2"][0].rearrange("(p k) n -> p k n", p=P)
    with Phase(nc) as ph:
        w = ph.sb("w", [P, 2, C, 512])
        pa = [ph.ps(f"pa{b}", [P, 512]) for b in range(2)]
        w_in, product, moved = (ph.sems(k) for k in ("w_in", "product", "moved"))
        block = ph.block()

        @block.sync
        def _(sp):
            ph.clear_other_pool(sp)
            for i, col in enumerate(cols):
                if i >= 2:
                    sp.wait_ge(product[1], 2 * (i - 1))
                sp.dma_start(w[:, i % 2], w_dram[:, :, col:col + 512]).then_inc(w_in[i % 2], 16)

        @block.tensor
        def _(pe):
            for i in range(len(cols)):
                pe.wait_ge(w_in[i % 2], 16 * (i // 2 + 1))
                for t in range(NLAT):
                    if 4 * i + t >= 2:
                        pe.wait_ge(moved[t % 2], (4 * i + t) // 2)
                    for k in range(C):
                        last = pe.matmul(pa[t % 2][:], hT[:, k, t * P:(t + 1) * P], w[:, i % 2, k, :], start=(k == 0), stop=(k == C - 1))
                    last.then_inc(product[t % 2], 1)

        @block.scalar
        def _(act):
            for n in range(2 * len(cols)):
                act.wait_ge(product[0], n + 1)
                act.activation(dst[:, 2 * n % 4, n // 2, :], pa[0][:], ACT.Copy).then_inc(moved[0], 1)

        @block.vector
        def _(dve):
            for n in range(2 * len(cols)):
                dve.wait_ge(product[1], n + 1)
                dve.tensor_copy(dst[:, (2 * n + 1) % 4, n // 2, :], pa[1][:]).then_inc(moved[1], 1)


def gla_phase(nc, g, hT, G, vrow, yT):
    BM = P // GCH
    assert NLAT * GH == GCH
    with Phase(nc) as ph:
        wa = ph.sb("wa", [P, C, GLA_A])
        wu = ph.sb("wu", [GLA_A, 2, P])
        ba = ph.sb("ba", [P, 2])
        al = ph.sb("al", [GLA_A, LAT])
        keep, member = ph.sb("keep", [P, LAT]), ph.sb("member", [P, BM])
        ones = ph.sb("ones", [P, P])
        half_ones = ph.sb("half_ones", [P, 2, P])
        gn = ph.sb("gn", [P, 1])
        eps = ph.sb("eps", [P, 1])
        lc = ph.sb("lc", [P, 2, LAT])
        u = ph.sb("u", [P, 2, LAT])
        rel = ph.sb("rel", [P, 2, 2, LAT])
        m = ph.sb("m", [P, 2, 2, LAT])
        qi = ph.sb("qi", [P, 2, LAT])
        ki = ph.sb("ki", [P, 2, LAT])
        kr = ph.sb("kr", [P, NLAT, 2, P])
        dn = ph.sb("dn", [P, 2, NCH])
        vm = ph.sb("vm", [P, 2, BM, P])
        S = ph.sb("S", [P, 2, NCH, P])
        pv = ph.sb("pv", [P, 2, LAT])
        pA = ph.ps("pA", [P, 4, 512])
        pB = ph.ps("pB", [P, 4, 512])
        names = ("const_in", "a_low", "a_moved", "raised", "logs", "cum", "exped", "inputs", "k_turned", "k_moved", "vm_ready",
                 "kv", "kv_moved", "states", "inter", "rel_ready", "rel_exp", "m_ready", "s_done", "s_used",
                 "squares", "means", "roots", "silus", "order", "order_a", "halves")
        s = {k: ph.sem(k) for k in names}
        block = ph.block()
        qT, kT, vT, gT = G[:, 0:2], G[:, 2:4], G[:, 4:8], G[:, 8:12]
        o = yT[:, 0:4]

        def by_chunk(ap):
            return ap.rearrange("p (c i) -> p c i", i=GCH)

        @block.sync
        def _(sp):
            ph.clear_other_pool(sp)
            a0 = 2 * GLA_Q + 2 * GLA_V
            sp.dma_start(wa[:], g["w_in_2"][0].rearrange("(p k) n -> p k n", p=P)[:, :, a0:a0 + GLA_A]).then_inc(s["const_in"], 16)
            sp.dma_start(wu[:].rearrange("a c n -> a (c n)"), g["w_alpha_up_2"][0]).then_inc(s["const_in"], 16)
            for c in range(2):
                sp.dma_start(ba[:, c:c + 1], g["b_alpha_2"][0, c * P:(c + 1) * P].rearrange("(p o) -> p o", o=1)).then_inc(s["const_in"], 16)
            sp.dma_start(keep[:], g["chunk_keep"]).then_inc(s["const_in"], 16)
            sp.dma_start(member[:], g["member"]).then_inc(s["const_in"], 16)
            sp.dma_start(ones[:], g["ones"]).then_inc(s["const_in"], 16)
            sp.dma_start(gn[:], g["gla_norm_g_2"].rearrange("o p -> p o")).then_inc(s["const_in"], 16)
            sp.wait_ge(s["const_in"], 128)

        @block.gpsimd
        def _(pool):
            pool.wait_ge(s["const_in"], 128)
            for i in range(NLAT * GH):
                t, h = i // GH, i % GH
                if i >= 2:
                    pool.wait_ge(s["kv"], i - 1)
                pool.tensor_tensor(vm[:, i % 2], vrow[:, t, 0, h * P:(h + 1) * P].rearrange("p (o e) -> p o e", o=1).broadcast_to([P, BM, P]),
                                   member[:].rearrange("p (c o) -> p c o", o=1).broadcast_to([P, BM, P]), ALU.mult).then_inc(s["vm_ready"], 1)

        @block.tensor
        def _(pe):
            pe.wait_ge(s["const_in"], 128)
            for k in range(C):
                last = pe.matmul(pA[0:GLA_A, 0, :], wa[:, k, :], hT[:, k, :], start=(k == 0), stop=(k == C - 1))
            last.then_inc(s["a_low"], 1)
            pe.wait_ge(s["a_moved"], 1)
            for c in range(2):
                last = pe.matmul(pA[:, 1 + c, :], wu[:, c, :], al[:], start=True, stop=True)
            last.then_inc(s["raised"], 1)
            pe.wait_ge(s["inputs"], 1)
            for t in range(NLAT):
                if t:
                    pe.wait_ge(s["k_moved"], t)
                for c in range(2):
                    last = pe.transpose(pA[:, 0, c * P:(c + 1) * P], ki[:, c, t * P:(t + 1) * P], g["ident"][:])
                last.then_inc(s["k_turned"], 1)
            pe.wait_ge(s["k_moved"], NLAT)
            pe.wait_ge(s["halves"], 1)
            for i in range(GCH):
                t, h = i // GH, i % GH
                pe.wait_ge(s["vm_ready"], i + 1)
                if i >= 2:
                    pe.wait_ge(s["kv_moved"], i - 1)
                for half in range(2):
                    last = pe.matmul(pA[:, 2 * (i % 2) + half, :], kr[:, t, h // 2, :], vm[:, i % 2, half * 4:half * 4 + 4].rearrange("p c e -> p (c e)"),
                                     start=True, stop=True)
                last.then_inc(s["kv"], 1)
                w = NCH * (GCH - i)
                pe.wait_ge(s["m_ready"], i + 1)
                for h in range(GH):
                    if i:
                        pe.wait_ge(s["s_used"], 4 * (i - 1) + h + 1)
                    pe.matmul(pB[:, h, 0:w], half_ones[:, h % 2, :], m[:, i % 2, h // 2, 0:w], start=True, stop=True).then_inc(s["s_done"], 1)
            pe.wait_ge(s["kv_moved"], NLAT * GH)
            for n in range(1, NCH):
                pe.wait_ge(s["states"], n)
                for h in range(GH):
                    rows = slice((h % 2) * 64, (h % 2) * 64 + 64)
                    last = pe.matmul(pA[:, h, n * GCH:(n + 1) * GCH], S[rows, h // 2, n - 1, :], qi[rows, h // 2, n * GCH:(n + 1) * GCH],
                                     start=True, stop=True)
            last.then_inc(s["inter"], 1)
            pe.wait_ge(s["squares"], 1)
            for h in range(GH):
                last = pe.matmul(pA[:, h, :], ones[:], S[:, 0].rearrange("p n e -> p (n e)")[:, h * 512:(h + 1) * 512], start=True, stop=True)
            last.then_inc(s["means"], 1)

        @block.scalar
        def _(act):
            step = Steps(act, s["order_a"])
            act.wait_ge(s["a_low"], 1)
            act.activation(al[:], pA[0:GLA_A, 0, :], ACT.Copy).then_inc(s["a_moved"], 1)
            act.wait_ge(s["logs"], 1)
            step(act.activation(u[:], u[:], ACT.Exp, scale=-1.0))
            act.activation(u[:], u[:], ACT.Ln, bias=1.0).then_inc(s["logs"], 1)
            act.wait_ge(s["cum"], 1)
            act.activation(qi[:], lc[:], ACT.Exp)
            act.activation(ki[:], u[:], ACT.Exp)
            act.activation(dn[:], lc[:].rearrange("p a (c i) -> p a c i", i=GCH)[:, :, :, GCH - 1], ACT.Exp).then_inc(s["exped"], 1)
            for t in range(NLAT):
                act.wait_ge(s["k_turned"], t + 1)
                act.activation(kr[:, t].rearrange("p c e -> p (c e)"), pA[:, 0, 0:2 * P], ACT.Copy).then_inc(s["k_moved"], 1)
            for i in range(GCH):
                t, h = i // GH, i % GH
                rows = slice((h % 2) * 64, (h % 2) * 64 + 64)
                if i:
                    w = NCH * (GCH - i)
                    act.wait_ge(s["rel_ready"], i)
                    act.activation(rel[:, i % 2, :, 0:w], rel[:, i % 2, :, 0:w], ACT.Exp).then_inc(s["rel_exp"], 1)
                act.wait_ge(s["kv"], i + 1)
                for half in range(2):
                    c0 = t * BM + half * 4
                    last = act.activation(S[rows, h // 2, c0:c0 + 4, :].rearrange("p c e -> p (c e)"), pA[rows, 2 * (i % 2) + half, :], ACT.Copy)
                last.then_inc(s["kv_moved"], 1)
            act.wait_ge(s["means"], 1)
            for h in range(GH):
                last = act.activation(S[:, 0].rearrange("p n e -> p (n e)")[:, h * 512:(h + 1) * 512], pA[:, h, :], ACT.Sqrt, scale=1.0 / P, bias=eps[:])
            last.then_inc(s["roots"], 1)
            act.activation(gT[:], gT[:], ACT.Silu).then_inc(s["silus"], 1)

        @block.vector
        def _(dve):
            step = Steps(dve, s["order"])
            step(dve.memset(eps[:], EPS2))
            for half in range(2):
                dve.memset(half_ones[half * 64:(half + 1) * 64, half, :], 1.0)
                last = dve.memset(half_ones[(1 - half) * 64:(2 - half) * 64, half, :], 0.0)
            last.then_inc(s["halves"], 1)
            dve.wait_ge(s["const_in"], 128)
            dve.wait_ge(s["raised"], 1)
            for c in range(2):
                step(dve.tensor_scalar(lc[:, c], pA[:, 1 + c, :], ba[:, c:c + 1], None, ALU.add))
            dve.scalar_tensor_tensor(out=u[:], in0=lc[:], scalar=-1.0, in1=lc[:], op0=ALU.mult, op1=ALU.max).then_inc(s["logs"], 1)
            step(dve.tensor_scalar(lc[:], lc[:], 0.0, None, ALU.min))
            dve.wait_ge(s["logs"], 2)
            step(dve.tensor_tensor(lc[:], lc[:], u[:], ALU.subtract))
            step(dve.tensor_scalar(u[:], lc[:], 1.0 / 16.0, None, ALU.mult))
            for c in range(2):
                step(dve.tensor_tensor_scan(lc[:, c], keep[:], u[:, c], 0.0, ALU.mult, ALU.add))
            for c in range(2):
                x = by_chunk(lc[:, c])
                last = dve.tensor_tensor(by_chunk(u[:, c]), x[:, :, GCH - 1:GCH].broadcast_to([P, NCH, GCH]), x, ALU.subtract)
            last.then_inc(s["cum"], 1)
            step(dve.tensor_scalar(qT[:], qT[:], 64.0 ** -0.5, None, ALU.mult))
            dve.wait_ge(s["exped"], 1)
            dve.tensor_tensor(qi[:], qi[:], qT[:], ALU.mult)
            dve.tensor_tensor(ki[:], ki[:], kT[:], ALU.mult).then_inc(s["inputs"], 1)
            def weights(d):
                n = GCH - d
                for c in range(2):
                    x = by_chunk(lc[:, c])
                    if d:
                        last = dve.tensor_tensor(rel[:, d % 2, c, 0:NCH * n].rearrange("p (c i) -> p c i", i=n), x[:, :, d:GCH], x[:, :, 0:n], ALU.subtract)
                if d:
                    last.then_inc(s["rel_ready"], 1)
                for c in range(2):
                    md = m[:, d % 2, c, 0:NCH * n].rearrange("p (c i) -> p c i", i=n)
                    last = dve.tensor_tensor(md, by_chunk(qT[:, c])[:, :, d:GCH], by_chunk(kT[:, c])[:, :, 0:n], ALU.mult)
                if not d:
                    last.then_inc(s["m_ready"], 1)
                    return
                step(last)
                dve.wait_ge(s["rel_exp"], d)
                md = m[:, d % 2, :, 0:NCH * n]
                dve.tensor_tensor(md, md, rel[:, d % 2, :, 0:NCH * n], ALU.mult).then_inc(s["m_ready"], 1)

            weights(0)
            for d in range(GCH):
                if d < GCH - 1:
                    if d:
                        dve.wait_ge(s["s_done"], 4 * d)
                    weights(d + 1)
                n = GCH - d
                for h in range(GH):
                    dve.wait_ge(s["s_done"], 4 * d + h + 1)
                    if d == 0:
                        dve.tensor_tensor(o[:, h], pB[:, h, :], vT[:, h], ALU.mult).then_inc(s["s_used"], 1)
                        dve.wait_ge(s["s_used"], h + 1)
                        continue
                    pvh = pv[:, h % 2, 0:NCH * n].rearrange("p (c i) -> p c i", i=n)
                    dve.tensor_tensor(pvh, pB[:, h, 0:NCH * n].rearrange("p (c i) -> p c i", i=n), by_chunk(vT[:, h])[:, :, 0:n], ALU.mult).then_inc(s["s_used"], 1)
                    dve.wait_ge(s["s_used"], 4 * d + h + 1)
                    oh = by_chunk(o[:, h])[:, :, d:GCH]
                    step(dve.tensor_tensor(oh, oh, pvh, ALU.add))
            dve.wait_ge(s["kv_moved"], NLAT * GH)
            dve.sem_inc(s["states"], 1)
            for n in range(1, NCH):
                for c in range(2):
                    last = dve.scalar_tensor_tensor(out=S[:, c, n, :], in0=S[:, c, n - 1, :], scalar=dn[:, c, n:n + 1], in1=S[:, c, n, :],
                                                    op0=ALU.mult, op1=ALU.add)
                last.then_inc(s["states"], 1)
                dve.wait_ge(s["states"], n + 1)
            dve.wait_ge(s["inter"], 1)
            for h in range(GH):
                step(dve.tensor_tensor(o[:, h, GCH:LAT], o[:, h, GCH:LAT], pA[:, h, GCH:LAT], ALU.add))
            sq = S[:, 0].rearrange("p n e -> p (n e)")[:, 0:2048].rearrange("p (h t) -> p h t", h=GH)
            dve.tensor_tensor(sq, o[:], o[:], ALU.mult).then_inc(s["squares"], 1)
            dve.wait_ge(s["roots"], 1)
            step(dve.reciprocal(sq, sq))
            step(dve.scalar_tensor_tensor(out=o[:], in0=o[:], scalar=gn[:], in1=sq, op0=ALU.mult, op1=ALU.mult))
            dve.wait_ge(s["silus"], 1)
            step(dve.tensor_tensor(o[:], o[:], gT[:], ALU.mult))


def short_conv_phase(nc, g, Z, yT):
    with Phase(nc) as ph:
        w = ph.sb("w", [P, 3, 4])
        acc = ph.sb("acc", [P, 4, LAT])
        w_in, order = ph.sem("w_in"), ph.sem("order")
        block = ph.block()

        @block.sync
        def _(sp):
            ph.clear_other_pool(sp)
            for j in range(3):
                sp.dma_start(w[:, j, :], g["sc_conv_w_2"][0, j, :].rearrange("(k p) -> p k", p=P), allow_slow_non_contiguous=True).then_inc(w_in, 16)

        @block.vector
        def _(dve):
            step = Steps(dve, order)
            b, c, x = Z[:, 0:4], Z[:, 4:8], Z[:, 8:12]
            dve.wait_ge(w_in, 48)
            step(dve.tensor_tensor(x, c, x, ALU.mult))
            for k in range(4):
                step(dve.tensor_scalar(acc[:, k], x[:, k], w[:, 2, k:k + 1], None, ALU.mult))
                for j in (1, 2):
                    step(dve.scalar_tensor_tensor(out=acc[:, k, j:], in0=x[:, k, 0:LAT - j], scalar=w[:, 2 - j, k:k + 1],
                                                  in1=acc[:, k, j:], op0=ALU.mult, op1=ALU.add))
            step(dve.tensor_tensor(yT[:, 4:8], acc[:], b, ALU.mult))


def dilated_phase(nc, g, QK, vrow, yT):
    H, S3 = 4, 3
    DSC = 128.0 ** -0.5

    def keys(t):
        return [(s, k) for s in range(S3) for k in range(max(0, t - 1) if s == 0 else 0, t + 1)]

    KMAX = max(len(keys(t)) for t in range(NLAT))
    RND = sum((len(keys(t)) + 3) // 4 for t in range(NLAT))
    with Phase(nc) as ph:
        mask = ph.sb("mask", [P, S3, NLAT, LAT])
        q2 = ph.sb("q2", [P, S3, LAT])
        E = ph.sb("E", [P, 2, KMAX * P])
        PT = ph.sb("PT", [P, 2, 512])
        o = ph.sb("o", [P, NLAT, 512])
        st = ph.sb("st", [P, 2, 4])
        pS = [ph.ps(f"pS{i}", [P, 512]) for i in range(3)]
        pT = [ph.ps(f"pT{i}", [P, 512]) for i in range(2)]
        pO = [ph.ps(f"pO{i}", [P, P]) for i in range(2)]
        names = ("mask_in", "q_ready", "scored", "s_used", "shifted", "e_ready", "r_ready", "turned", "moved", "pv", "o_out", "last_turned", "last_moved", "order", "o_all")
        s = {k: ph.sem(k) for k in names}
        block = ph.block()

        def segments(t):
            out, at = [], 0
            for st_ in range(S3):
                k0 = max(0, t - 1) if st_ == 0 else 0
                out.append((st_, k0, t + 1 - k0, at))
                at += t + 1 - k0
            return out

        def rounds():
            return [(t, i, min(4, len(keys(t)) - i)) for t in range(NLAT) for i in range(0, len(keys(t)), 4)]

        @block.sync
        def _(sp):
            ph.clear_other_pool(sp)
            for i in range(S3):
                sp.dma_start(mask[:, i], g["dil_mask"][i].rearrange("(t p) n -> p t n", p=P)).then_inc(s["mask_in"], 16)

        @block.gpsimd
        def _(pool):
            with pool.Fori(0, H) as h:
                pool.wait_ge(s["o_all"], h + 1)
                for i in range(S3):
                    last = pool.tensor_copy(q2[:, i:i + 1], QK[:, ds(h + 4 * i, 1), :])
                last.then_inc(s["q_ready"], 1)

        @block.tensor
        def _(pe):
            def score(h, t):
                for i, (st_, k0, n, at) in enumerate(segments(t)):
                    pe.wait_ge(s["s_used"], 12 * h + 3 * t + i + 1)
                    pe.matmul(pS[i][:, 0:n * P], q2[:, st_, t * P:(t + 1) * P],
                              QK[:, ds(h + (12 + 4 * st_), 1), k0 * P:(k0 + n) * P].rearrange("p o n -> p (o n)"),
                              start=True, stop=True).then_inc(s["scored"], 1)

            with pe.Fori(0, H) as h:
                pe.wait_ge(s["q_ready"], h + 1)
                score(h, 0)
                for r, (t, i0, n) in enumerate(rounds()):
                    if i0 == 0:
                        pe.wait_ge(s["e_ready"], NLAT * h + t + 1)
                    pe.wait_ge(s["moved"], RND * h + r + 1)
                    for j in range(n):
                        last = pe.transpose(pT[r % 2][:, j * P:(j + 1) * P], E[:, t % 2, (i0 + j) * P:(i0 + j + 1) * P], g["ident"][:])
                    last.then_inc(s["turned"], 1)
                    if i0 == 0 and t < NLAT - 1:
                        score(h, t + 1)
                    pe.wait_ge(s["moved"], RND * h + r + 2)
                    if i0 == 0:
                        pe.wait_ge(s["o_out"], NLAT * h + t + 1)
                    nk = len(keys(t))
                    for j in range(n):
                        st_, k = keys(t)[i0 + j]
                        last = pe.matmul(pO[t % 2][:], PT[:, r % 2, j * P:(j + 1) * P],
                                         vrow[:, k, st_, ds(h * P, P)],
                                         start=(i0 + j == 0), stop=(i0 + j == nk - 1))
                    if i0 + n == nk:
                        last.then_inc(s["pv"], 1)
            pe.wait_ge(s["o_out"], NLAT * H + 1)
            for t in range(NLAT):
                if t >= 2:
                    pe.wait_ge(s["last_moved"], t - 1)
                for c in range(4):
                    last = pe.transpose(pT[t % 2][:, c * P:(c + 1) * P], o[:, t, c * P:(c + 1) * P], g["ident"][:])
                last.then_inc(s["last_turned"], 1)

        @block.scalar
        def _(act):
            act.sem_inc(s["moved"], 1)
            act.sem_inc(s["o_out"], 1)
            act.sem_inc(s["o_all"], 1)
            with act.Fori(0, H) as h:
                def exp(t):
                    n = len(keys(t)) * P
                    act.wait_ge(s["shifted"], NLAT * h + t + 1)
                    act.activation(E[:, t % 2, 0:n], E[:, t % 2, 0:n], ACT.Exp, bias=st[:, t % 2, 1:2],
                                   accum_out=st[:, t % 2, 2:3]).then_inc(s["e_ready"], 1)

                exp(0)
                for r, (t, i0, n) in enumerate(rounds()):
                    act.wait_ge(s["turned"], RND * h + r + 1)
                    act.activation(PT[:, r % 2, 0:n * P], pT[r % 2][:, 0:n * P], ACT.Copy).then_inc(s["moved"], 1)
                    if i0 + n == len(keys(t)):
                        if t < NLAT - 1:
                            exp(t + 1)
                        act.wait_ge(s["pv"], NLAT * h + t + 1)
                        act.wait_ge(s["r_ready"], NLAT * h + t + 1)
                        act.activation(o[:, t, ds(h * P, P)], pO[t % 2][:], ACT.Copy, scale=st[:, t % 2, 3:4]).then_inc(s["o_out"], 1)
                act.sem_inc(s["o_all"], 1)
            for t in range(NLAT):
                act.wait_ge(s["last_turned"], t + 1)
                act.activation(yT[:, 8:12, t * P:(t + 1) * P], pT[t % 2][:].rearrange("p (c n) -> p c n", c=4), ACT.Copy).then_inc(s["last_moved"], 1)

        @block.vector
        def _(dve):
            step = Steps(dve, s["order"])
            dve.sem_inc(s["s_used"], 3)
            dve.wait_ge(s["mask_in"], 48)
            with dve.Fori(0, H) as h:
                step.restart()

                def shift(t):
                    for i, (st_, k0, n, at) in enumerate(segments(t)):
                        dve.wait_ge(s["scored"], 12 * h + 3 * t + i + 1)
                        last = dve.scalar_tensor_tensor(out=E[:, t % 2, at * P:(at + n) * P], in0=pS[i][:, 0:n * P], scalar=DSC,
                                                        in1=mask[:, st_, t, k0 * P:(k0 + n) * P], op0=ALU.mult, op1=ALU.add)
                        last.then_inc(s["s_used"], 1)
                    dve.wait_ge(s["s_used"], 12 * h + 3 * t + 6)
                    step(dve.tensor_reduce(st[:, t % 2, 0:1], E[:, t % 2, 0:len(keys(t)) * P], AX.X, ALU.max))
                    dve.tensor_scalar(st[:, t % 2, 1:2], st[:, t % 2, 0:1], -1.0, None, ALU.mult).then_inc(s["shifted"], 1)

                shift(0)
                for t in range(NLAT):
                    dve.wait_ge(s["e_ready"], NLAT * h + t + 1)
                    dve.reciprocal(st[:, t % 2, 3:4], st[:, t % 2, 2:3]).then_inc(s["r_ready"], 1)
                    if t < NLAT - 1:
                        shift(t + 1)


D_FF = 2816
NF = D_FF // P


def merge_phase(nc, g, hT, yT, merged):
    wg_dram = g["w_gate_2"][0].rearrange("(p k) n -> p k n", p=P)
    with Phase(nc) as ph:
        wg = ph.sb("wg", [P, 2, C, 512])
        wb = ph.sb("wb", [P, 2, 4, 512])
        bias = ph.sb("bias", [P, 2, 512])
        z = ph.sb("z", [P, 2, 512])
        y = ph.sb("y", [P, 4, LAT])
        pG = [ph.ps(f"pG{i}", [P, 512]) for i in range(2)]
        pY = [ph.ps(f"pY{i}", [P, 512]) for i in range(2)]
        w_in, used, gate_done, branch_done, logit, gate, taken = (
            ph.sems(k) for k in ("w_in", "used", "gate_done", "branch_done", "logit", "gate", "taken"))
        y_ready, order = ph.sem("y_ready"), ph.sem("order")
        block = ph.block()

        @block.sync
        def _(sp):
            ph.clear_other_pool(sp)
            with sp.Fori(0, 3) as i:
                for b in range(2):
                    sp.wait_ge(used[b], i + 1)
                    sp.dma_start(wg[:, b], wg_dram[:, :, ds(i * D + b * 512, 512)]).then_inc(w_in[b], 16)
                    sp.dma_start(wb[:, b], g["w_branch_2"][0, ds(i, 1)].rearrange("o (k p) n -> p (o k) n", p=P)[:, :, b * 512:(b + 1) * 512]).then_inc(w_in[b], 16)
                    sp.dma_start(bias[:, b], g["b_gate_2"][:, ds(i * D + b * 512, 512)].broadcast_to([P, 512])).then_inc(w_in[b], 16)

        @block.gpsimd
        def _(pool):
            with pool.Fori(0, 3) as i:
                pool.wait_ge(used[1], i + 1)
                pool.tensor_copy(y[:], yT[:, ds(4 * i, 4), :]).then_inc(y_ready, 1)

        @block.tensor
        def _(pe):
            with pe.Fori(0, 3) as i:
                pe.wait_ge(y_ready, i + 1)
                for b in range(2):
                    pe.wait_ge(w_in[b], 48 * (i + 1))
                    for t in range(NLAT):
                        q, n = t % 2, 4 * i + 2 * b + t // 2
                        pe.wait_ge(taken[q], n + 1)
                        for k in range(C):
                            last = pe.matmul(pG[q][:], hT[:, k, t * P:(t + 1) * P], wg[:, b, k, :], start=(k == 0), stop=(k == C - 1))
                        last.then_inc(gate_done[q], 1)
                        for k in range(4):
                            last = pe.matmul(pY[q][:], y[:, k, t * P:(t + 1) * P], wb[:, b, k, :], start=(k == 0), stop=(k == 3))
                        last.then_inc(branch_done[q], 1)

        @block.scalar
        def _(act):
            with act.Fori(0, 3) as i:
                for b in range(2):
                    for t in range(NLAT):
                        q, n = t % 2, 4 * i + 2 * b + t // 2
                        act.wait_ge(logit[q], n + 1)
                        act.activation(z[:, q], z[:, q], ACT.Sigmoid).then_inc(gate[q], 1)

        @block.vector
        def _(dve):
            step = Steps(dve, order)
            for b in range(2):
                dve.sem_inc(used[b], 1)
                dve.sem_inc(taken[b], 1)
            step(dve.memset(merged[:], 0.0))
            with dve.Fori(0, 3) as i:
                step.restart()
                for b in range(2):
                    dve.wait_ge(w_in[b], 48 * (i + 1))
                    for t in range(NLAT):
                        q, n = t % 2, 4 * i + 2 * b + t // 2
                        dve.wait_ge(gate_done[q], n + 1)
                        dve.tensor_tensor(z[:, q], pG[q][:], bias[:, b], ALU.add).then_inc(logit[q], 1)
                        dve.wait_ge(gate[q], n + 1)
                        dve.wait_ge(branch_done[q], n + 1)
                        dve.tensor_tensor(z[:, q], z[:, q], pY[q][:], ALU.mult).then_inc(taken[q], 1)
                        dve.wait_ge(taken[q], n + 2)
                        mt = merged[:, t, b * 512:(b + 1) * 512]
                        step(dve.tensor_tensor(mt, mt, z[:, q], ALU.add))
                    dve.sem_inc(used[b], 1)


def mix_out_phase(nc, g, merged, hT):
    with Phase(nc) as ph:
        w = ph.sb("w", [P, C, D])
        mT = ph.sb("mT", [P, C, P])
        x = ph.sb("x", [P, 2, D])
        r = ph.sb("r", [P, D])
        grow = ph.sb("grow", [P, D])
        gcol = ph.sb("gcol", [P, C])
        ss = ph.sb("ss", [P, 4])
        eps = ph.sb("eps", [P, 1])
        pT = ph.ps("pT", [P, 1024])
        pM = ph.ps("pM", [P, 1024])
        names = ("const_in", "w_in", "turned", "movedA", "movedD", "mixed", "squared", "rooted", "x_ready", "scaled", "order", "order_a")
        s = {k: ph.sem(k) for k in names}
        x_in, stored = ph.sems("x_in"), ph.sems("stored")
        block = ph.block()

        @block.sync
        def _(sp):
            ph.clear_other_pool(sp)
            sp.dma_start(w[:], g["w_mix_out_2"][0].rearrange("(p k) n -> p k n", p=P)).then_inc(s["w_in"], 16)
            sp.dma_start(grow[:], g["post_mix_g_2"].broadcast_to([P, D])).then_inc(s["const_in"], 16)
            sp.dma_start(gcol[:], g["pre_ffn_g_2"][0].rearrange("(p k) -> p k", p=P)).then_inc(s["const_in"], 16)
            for t in range(NLAT):
                if t >= 2:
                    sp.wait_ge(s["turned"], 2 * (t - 1))
                    sp.wait_ge(stored[t % 2], 16)
                sp.dma_start(x[:, t % 2], g["h"][t * P:(t + 1) * P, :]).then_inc(x_in[t % 2], 16)
                sp.wait_ge(s["x_ready"], t + 1)
                sp.dma_start(g["x_mid"][t * P:(t + 1) * P, :], x[:, t % 2]).then_inc(stored[t % 2], 16)
            for b in range(2):
                sp.wait_ge(stored[b], 32)

        @block.tensor
        def _(pe):
            pe.wait_ge(s["w_in"], 16)
            for t in range(NLAT):
                if t:
                    pe.wait_ge(s["movedA"], 2 * t)
                    pe.wait_ge(s["movedD"], 2 * t)
                for k in range(C):
                    last = pe.transpose(pT[:, k * P:(k + 1) * P], merged[:, t, k::C], g["ident"][:])
                last.then_inc(s["turned"], 1)
                pe.wait_ge(s["movedA"], 2 * t + 1)
                pe.wait_ge(s["movedD"], 2 * t + 1)
                for b in range(2):
                    for k in range(C):
                        last = pe.matmul(pM[:, b * 512:(b + 1) * 512], mT[:, k, :], w[:, k, b * 512:(b + 1) * 512], start=(k == 0), stop=(k == C - 1))
                last.then_inc(s["mixed"], 1)
                pe.wait_ge(s["scaled"], t + 1)
                for k in range(C):
                    last = pe.transpose(pT[:, k * P:(k + 1) * P], r[:, k::C], g["ident"][:])
                last.then_inc(s["turned"], 1)

        @block.scalar
        def _(act):
            step = Steps(act, s["order_a"])
            for t in range(NLAT):
                act.wait_ge(s["turned"], 2 * t + 1)
                act.activation(mT[:, 0:4].rearrange("p k n -> p (k n)"), pT[:, 0:512], ACT.Copy).then_inc(s["movedA"], 1)
                act.wait_ge(s["mixed"], t + 1)
                act.wait_ge(s["movedD"], 2 * t + 1)
                for i in range(2):
                    if i:
                        act.wait_ge(s["x_ready"], t + 1)
                    step(act.activation(r[:], pM[:, :] if i == 0 else x[:, t % 2], ACT.Square, accum_out=ss[:, 0:1]))
                    act.activation(ss[:, 1:2], ss[:, 0:1], ACT.Sqrt, scale=1.0 / D, bias=eps[:]).then_inc(s["rooted"], 1)
                act.wait_ge(s["turned"], 2 * t + 2)
                for k in range(4):
                    last = act.activation(hT[:, k, t * P:(t + 1) * P], pT[:, k * P:(k + 1) * P], ACT.Copy, scale=gcol[:, k:k + 1])
                last.then_inc(s["movedA"], 1)

        @block.vector
        def _(dve):
            step = Steps(dve, s["order"])
            step(dve.memset(eps[:], EPS2))
            dve.wait_ge(s["const_in"], 32)
            for t in range(NLAT):
                dve.wait_ge(s["turned"], 2 * t + 1)
                dve.tensor_copy(mT[:, 4:8].rearrange("p k n -> p (k n)"), pT[:, 512:1024]).then_inc(s["movedD"], 1)
                dve.wait_ge(s["rooted"], 2 * t + 1)
                step(dve.reciprocal(ss[:, 2:3], ss[:, 1:2]))
                step(dve.scalar_tensor_tensor(out=r[:], in0=pM[:, :], scalar=ss[:, 2:3], in1=grow[:], op0=ALU.mult, op1=ALU.mult))
                dve.wait_ge(x_in[t % 2], 16 * (t // 2 + 1))
                dve.tensor_tensor(x[:, t % 2], x[:, t % 2], r[:], ALU.add).then_inc(s["x_ready"], 1)
                dve.wait_ge(s["rooted"], 2 * t + 2)
                step(dve.reciprocal(ss[:, 3:4], ss[:, 1:2]))
                dve.tensor_scalar(r[:], x[:, t % 2], ss[:, 3:4], None, ALU.mult).then_inc(s["scaled"], 1)
                dve.wait_ge(s["turned"], 2 * t + 2)
                for k in range(4, C):
                    last = dve.tensor_scalar(hT[:, k, t * P:(t + 1) * P], pT[:, k * P:(k + 1) * P], gcol[:, k:k + 1], None, ALU.mult)
                last.then_inc(s["movedD"], 1)


def feed_forward_up_phase(nc, g, hT, aT):
    with Phase(nc) as ph:
        wt = ph.sb("wt", [P, 2, 2, C, P])
        cw = ph.sb("cw", [P, 4, NF])
        x = ph.sb("x", [P, 2, LAT])
        pG = [ph.ps(f"pG{i}", [P, 512]) for i in range(2)]
        pU = [ph.ps(f"pU{i}", [P, 512]) for i in range(2)]
        conv_in, order = ph.sem("conv_in"), ph.sem("order")
        w_in, product, started, summed, gelu, done = (ph.sems(k) for k in ("w_in", "product", "started", "summed", "gelu", "done"))
        block = ph.block()

        @block.sync
        def _(sp):
            ph.clear_other_pool(sp)
            for j in range(3):
                sp.dma_start(cw[:, j], g["ff_conv_w_2"][0, j].rearrange("(k p) -> p k", p=P), allow_slow_non_contiguous=True).then_inc(conv_in, 16)
            sp.dma_start(cw[:, 3], g["ff_conv_b_2"][0].rearrange("(k p) -> p k", p=P), allow_slow_non_contiguous=True).then_inc(conv_in, 16)
            with sp.Fori(0, NF // 2) as i:
                for b in range(2):
                    sp.wait_ge(product[b], i + 1)
                    for j, name in enumerate(("w_ff_gate_2", "w_ff_up_2")):
                        sp.dma_start(wt[:, b, j], g[name][0].rearrange("(p k) n -> p k n", p=P)[:, :, ds(i * 2 * P + b * P, P)]).then_inc(w_in[b], 16)

        @block.tensor
        def _(pe):
            for b in range(2):
                pe.sem_inc(product[b], 1)
            with pe.Fori(0, NF // 2) as i:
                for b in range(2):
                    pe.wait_ge(w_in[b], 32 * (i + 1))
                    pe.wait_ge(done[b], i + 1)
                    for j, p in enumerate((pG, pU)):
                        for k in range(C):
                            last = pe.matmul(p[b][:], wt[:, b, j, k, :], hT[:, k, :], start=(k == 0), stop=(k == C - 1))
                    last.then_inc(product[b], 1)

        @block.scalar
        def _(act):
            act.wait_ge(conv_in, 64)
            with act.Fori(0, NF // 2) as i:
                for b in range(2):
                    act.wait_ge(product[b], i + 2)
                    act.wait_ge(done[b], i + 1)
                    act.activation(x[:, b], pG[b][:], ACT.Identity, scale=cw[:, 2, ds(2 * i + b, 1)], bias=cw[:, 3, ds(2 * i + b, 1)]).then_inc(started[b], 1)
                    act.wait_ge(summed[b], i + 1)
                    act.activation(x[:, b], x[:, b], ACT.Gelu_apprx_tanh).then_inc(gelu[b], 1)

        @block.vector
        def _(dve):
            step = Steps(dve, order)
            for b in range(2):
                dve.sem_inc(done[b], 1)
            dve.wait_ge(conv_in, 64)
            with dve.Fori(0, NF // 2) as i:
                step.restart()
                for b in range(2):
                    dve.wait_ge(started[b], i + 1)
                    step(dve.scalar_tensor_tensor(out=x[:, b, 1:], in0=pG[b][:, 0:LAT - 1], scalar=cw[:, 1, ds(2 * i + b, 1)], in1=x[:, b, 1:], op0=ALU.mult, op1=ALU.add))
                    dve.scalar_tensor_tensor(out=x[:, b, 2:], in0=pG[b][:, 0:LAT - 2], scalar=cw[:, 0, ds(2 * i + b, 1)], in1=x[:, b, 2:], op0=ALU.mult, op1=ALU.add).then_inc(summed[b], 1)
                    dve.wait_ge(gelu[b], i + 1)
                    dve.tensor_tensor(aT[:, ds(2 * i + b, 1), :], x[:, b:b + 1], pU[b][:].rearrange("p (o n) -> p o n", o=1), ALU.mult).then_inc(done[b], 1)


def feed_forward_down_phase(nc, g, aT):
    w_dram = g["w_ff_down_2"][0].rearrange("(k p) n -> p k n", p=P)
    with Phase(nc) as ph:
        w = ph.sb("w", [P, 2, D])
        a = ph.sb("a", [P, 2, LAT])
        x = ph.sb("x", [P, NLAT, D])
        r = ph.sb("r", [P, D])
        grow = ph.sb("grow", [P, D])
        ss = ph.sb("ss", [P, NLAT, 2])
        eps = ph.sb("eps", [P, 1])
        acc = [ph.ps(f"acc{t}", [P, D]) for t in range(NLAT)]
        w_in, a_ready, used = (ph.sems(k) for k in ("w_in", "a_ready", "used"))
        const_in, eps_set, squared, rooted, done, stored, order = (ph.sem(k) for k in ("const_in", "eps_set", "squared", "rooted", "done", "stored", "order"))
        block = ph.block()

        @block.sync
        def _(sp):
            ph.clear_other_pool(sp)
            with sp.Fori(0, NF // 2) as i:
                for b in range(2):
                    sp.wait_ge(used[b], i + 1)
                    sp.dma_start(w[:, b:b + 1], w_dram[:, ds(2 * i + b, 1), :]).then_inc(w_in[b], 16)
            sp.dma_start(grow[:], g["post_ffn_g_2"].broadcast_to([P, D])).then_inc(const_in, 16)
            sp.dma_start(x[:], g["x_mid"].rearrange("(t p) n -> p t n", p=P)).then_inc(const_in, 16)
            for t in range(NLAT):
                sp.wait_ge(done, t + 1)
                sp.dma_start(g["out"][0, t * P:(t + 1) * P, :], x[:, t]).then_inc(stored, 16)
            sp.wait_ge(stored, 16 * NLAT)

        @block.gpsimd
        def _(pool):
            with pool.Fori(0, NF // 2) as i:
                for b in range(2):
                    pool.wait_ge(used[b], i + 1)
                    pool.tensor_copy(a[:, b:b + 1], aT[:, ds(2 * i + b, 1), :]).then_inc(a_ready[b], 1)

        @block.tensor
        def _(pe):
            for b in range(2):
                pe.sem_inc(used[b], 1)

            def product(i, b, first, end):
                pe.wait_ge(w_in[b], 16 * (i + 1))
                pe.wait_ge(a_ready[b], i + 1)
                for t in range(NLAT):
                    for h in range(2):
                        last = pe.matmul(acc[t][:, h * 512:(h + 1) * 512], a[:, b, t * P:(t + 1) * P], w[:, b, h * 512:(h + 1) * 512],
                                         start=first, stop=end)
                last.then_inc(used[b], 1)

            product(0, 0, True, False)
            product(0, 1, False, False)
            with pe.Fori(1, NF // 2 - 1) as i:
                for b in range(2):
                    product(i, b, False, False)
            product(NF // 2 - 1, 0, False, False)
            product(NF // 2 - 1, 1, False, True)

        @block.scalar
        def _(act):
            act.wait_ge(eps_set, 1)
            act.wait_ge(used[1], NF // 2 + 1)
            for t in range(NLAT):
                if t:
                    act.wait_ge(done, t)
                act.activation(r[:], acc[t][:, :], ACT.Square, accum_out=ss[:, t, 0:1]).then_inc(squared, 1)
                act.wait_ge(squared, t + 1)
                act.activation(ss[:, t, 1:2], ss[:, t, 0:1], ACT.Sqrt, scale=1.0 / D, bias=eps[:]).then_inc(rooted, 1)

        @block.vector
        def _(dve):
            step = Steps(dve, order)
            dve.memset(eps[:], EPS2).then_inc(eps_set, 1)
            dve.wait_ge(const_in, 32)
            for t in range(NLAT):
                dve.wait_ge(rooted, t + 1)
                step(dve.reciprocal(ss[:, t, 1:2], ss[:, t, 1:2]))
                step(dve.scalar_tensor_tensor(out=r[:], in0=acc[t][:, :], scalar=ss[:, t, 1:2], in1=grow[:], op0=ALU.mult, op1=ALU.mult))
                dve.tensor_tensor(x[:, t], x[:, t], r[:], ALU.add).then_inc(done, 1)


def program(nc, g):
    Phase.count = 0

    def dram(name, shape, dt=F32):
        g[name] = nc.dram_tensor(name, shape, dt, kind="Internal").ap()

    dram("mods", [DEPTH, 2, 6 * D])
    dram("h_mid", [TOK, D])
    dram("f", [TOK, D])
    dram("y", [2 * TOK, D])
    dram("h", [TOK, D])
    dram("x_mid", [LAT, D])
    dram("rpb_pad", [8 * 15, P])
    with ExitStack() as whole:
        ident = whole.enter_context(nc.sbuf_tensor("ident", [P, P], F32))
        ident_in = whole.enter_context(nc.semaphore("ident_in"))
        with nc.Block() as block:
            @block.sync
            def _(sp):
                sp.dma_start(ident[:], g["ident"]).then_inc(ident_in, 16)
                sp.wait_ge(ident_in, 16)
        g["ident"] = ident
        modulation_phase(nc, g)
        srcs = (g["x"][0], g["ctx"][0])
        for l in range(DEPTH):
            nt = NTILE if l < DEPTH - 1 else NLAT
            with ExitStack() as layer:
                def keep(name, shape, dt=F32, stack=layer):
                    return stack.enter_context(nc.sbuf_tensor(f"{name}{l}", shape, dt))

                logits = keep("logits", [P, NTILE, 36])
                share = keep("share", [P, NTILE, 2])
                gather_at = keep("gather_at", [P, blocks(NTILE) + 2], I32)
                scatter_at = keep("scatter_at", [P, blocks(NTILE)], I32)
                expert_of = keep("expert_of", [P, large_items(NTILE) + NE], I32)
                pairs_of = keep("pairs_of", [P, 2], I32)
                with ExitStack() as mixer:
                    qT, kT, V = (keep(n, s, stack=mixer) for n, s in (
                        ("qT", [P, 8, TOK + P]), ("kT", [P, 6, TOK]), ("V", [P, NTILE, 640])))
                    projection_phase(nc, g, l, srcs, qT, kT, V)
                    bias = None
                    if l == 1:
                        bias = keep("na_bias", [P, 8, 14, HD], stack=mixer)
                        neighbour_bias_phase(nc, g, bias)
                    attention_phase(nc, g, l, srcs, qT, kT, V, logits, bias)
                routing_phase(nc, g, nt, logits, share, gather_at, scatter_at, expert_of, pairs_of)
                large_item_phase(nc, g, l, nt, gather_at, scatter_at, expert_of, pairs_of)
                small_item_phase(nc, g, l, nt, gather_at, scatter_at, expert_of, pairs_of)
                combine_phase(nc, g, l, share, g["h"])
                srcs = (g["h"][0:LAT, :], g["h"][LAT:TOK, :])
        with ExitStack() as mix:
            def keep2(name, shape, stack=mix):
                return stack.enter_context(nc.sbuf_tensor(name, shape, F32))

            hT = keep2("hT", [P, C, LAT])
            yT = keep2("yT", [P, 12, LAT])
            norm_turn_phase(nc, g, g["h"], g["pre_mix_g_2"], hT)
            with ExitStack() as part:
                G, gv = keep2("G", [P, 12, LAT], part), keep2("gv", [P, NLAT, 1, 512], part)
                columns_phase(nc, g, hT, 0, 12, G)
                rows_phase(nc, g, hT, [2 * GLA_Q], gv)
                gla_phase(nc, g, hT, G, gv, yT)
            with ExitStack() as part:
                Z = keep2("Z", [P, 12, LAT], part)
                columns_phase(nc, g, hT, SC_AT, 12, Z)
                short_conv_phase(nc, g, Z, yT)
            with ExitStack() as part:
                QK, dv = keep2("QK", [P, 24, LAT], part), keep2("dv", [P, NLAT, 3, 512], part)
                columns_phase(nc, g, hT, DIL_AT, 24, QK, turn=True)
                rows_phase(nc, g, hT, [DIL_AT + 2 * DIL_W + 512 * i for i in range(3)], dv)
                dilated_phase(nc, g, QK, dv, yT)
            merged = keep2("merged", [P, NLAT, D])
            merge_phase(nc, g, hT, yT, merged)
            mix_out_phase(nc, g, merged, hT)
            aT = keep2("aT", [P, NF, LAT])
            feed_forward_up_phase(nc, g, hT, aT)
            feed_forward_down_phase(nc, g, aT)


def constants():
    f = np.float32
    k = {}
    k["ident"] = np.eye(P, dtype=f)
    k["ones"] = np.ones((P, P), f)
    k["earlier"] = np.triu(np.ones((P, P), f), 1)
    for n in (64, 128):
        r = np.zeros((P, P), f)
        for m in range(P):
            first = m % n < n // 2
            r[m + n // 2 if first else m - n // 2, m] = -1.0 if first else 1.0
        k[f"rot{n}"] = r
    k["blk64"] = (np.kron(np.eye(2), np.ones((64, 64))) / 64).astype(f)
    t = np.arange(LAT)
    inv = (f(10000.0) ** (-np.arange(16, dtype=f) / f(16))).astype(f)
    ang = np.concatenate([(t // GRID_W).astype(f)[:, None] * inv, (t % GRID_W).astype(f)[:, None] * inv], -1).astype(f)
    for name, fn in (("cos", np.cos), ("sin", np.sin)):
        k[name] = np.ascontiguousarray(np.tile(fn(ang).T, (4, 1)).astype(f))
    q, m = t[:, None], t[None, :]
    k["win_mask"] = np.where(np.abs(q - m) <= WINDOW, 0.0, NEG).astype(f)
    col = np.arange(GRID_W)
    start = np.clip(col - NA_COLS // 2, 0, GRID_W - NA_COLS)
    ok = (col[None, :] >= start[:, None]) & (col[None, :] < start[:, None] + NA_COLS)
    k["na_keep"] = np.tile(ok.astype(f), (2, 1))
    k["na_mask"] = np.tile(np.where(ok, 0.0, NEG).astype(f), (2, 1))
    k["dil_mask"] = np.stack([np.where((q >= m) & ((q - m) % s == 0) & (q - m <= 128 * s), 0.0, NEG) for s in (1, 4, 16)]).astype(f)
    k["chunk_keep"] = np.tile((t % GCH != 0).astype(f), (P, 1))
    k["member"] = (np.arange(P)[:, None] // GCH == np.arange(P // GCH)[None, :]).astype(f)
    k["flip64"] = np.kron(np.eye(2), np.eye(64)[::-1]).astype(f)
    k["count"] = np.tile(np.arange(P, dtype=f), (P, 1))
    k["token"] = (np.arange(NTILE)[None, :] * P + np.arange(P)[:, None]).astype(f)
    k["inv_freq"] = np.tile((f(10000.0) ** (-np.arange(0, 128, 2, dtype=f) / f(128))).astype(f), 2)[:, None].copy()
    return k


def kernel(**inputs):
    import concourse.bacc as _bacc
    from concourse.bass_utils import run_bass_kernel_spmd as _run

    nc = _bacc.Bacc("TRN2", target_bir_lowering=False, num_devices=1)
    arrays, g = {}, {}
    for name, a in list(inputs.items()) + list(constants().items()):
        a = np.ascontiguousarray(a)
        arrays[f"in_{name}"] = a
        g[name] = nc.dram_tensor(f"in_{name}", a.shape, mybir.dt.from_np(a.dtype), kind="ExternalInput").ap()
    g["out"] = nc.dram_tensor("out_dram", (1, LAT, D), F32, kind="ExternalOutput").ap()
    program(nc, g)
    r = _run(nc, [arrays], core_ids=[0])
    return r.results[0]["out_dram"]
```
